# Optimizing a Trainium2 kernel written in Bass

```python
import math
import jax, jax.numpy as jnp
from jax import lax
import numpy as np

D_MODEL = 2048
BATCH = 1
SEQ = 256
DEPTH = 2

CHUNK = 64
N_MIXERS = 2
Q_BLOCK = 128

MLA_HEADS = 16
QK_NOPE = 128
QK_ROPE = 64
V_HEAD = 128
Q_LORA = 512
KV_LORA = 512
ROPE_THETA = 10000.0
MLA_QK = QK_NOPE + QK_ROPE
MLA_WIDTH = MLA_HEADS * V_HEAD
MLA_IN = Q_LORA + KV_LORA + QK_ROPE + MLA_WIDTH

ML_HEADS = 8
ML_QK = 128
ML_V = 256
ML_QK_WIDTH = ML_HEADS * ML_QK
ML_WIDTH = ML_HEADS * ML_V
CONV_W = 4
ML_IN = 2 * ML_QK_WIDTH + 2 * ML_WIDTH + 2 * ML_HEADS + ML_WIDTH

ALPHA = (2 * DEPTH) ** 0.25
BETA = (8 * DEPTH) ** -0.25
EPS = 1e-6


def _rmsnorm(x, w):
    xf = x.astype(jnp.float32)
    y = xf * lax.rsqrt(jnp.mean(xf * xf, axis=-1, keepdims=True) + EPS)
    return y.astype(x.dtype) * w

def _layernorm(x, w, b):
    xf = x.astype(jnp.float32)
    mu = jnp.mean(xf, axis=-1, keepdims=True)
    var = jnp.mean(jnp.square(xf - mu), axis=-1, keepdims=True)
    return ((xf - mu) * lax.rsqrt(var + EPS)).astype(x.dtype) * w + b

def _rope_tables(positions, dtype):
    inv_freq = ROPE_THETA ** (-jnp.arange(0, QK_ROPE, 2, dtype=jnp.float32) / QK_ROPE)
    ang = positions.astype(jnp.float32)[..., None] * inv_freq
    return jnp.cos(ang).astype(dtype), jnp.sin(ang).astype(dtype)

def _rope(x, cos, sin):
    half = x.shape[-1] // 2
    x1, x2 = x[..., :half], x[..., half:]
    return jnp.concatenate([x1 * cos - x2 * sin, x1 * sin + x2 * cos], axis=-1)

def _chunk_causal_attention(q, k, v):
    b, s, h, dk = q.shape
    nb = s // Q_BLOCK
    scale = dk ** -0.5
    q_blocks = q.reshape(b, nb, Q_BLOCK, h, dk).transpose(1, 0, 2, 3, 4)
    key_chunk = jnp.arange(s) // CHUNK

    def one_block(args):
        qb, bi = args
        q_chunk = (bi * Q_BLOCK + jnp.arange(Q_BLOCK)) // CHUNK
        mask = key_chunk[None, :] <= q_chunk[:, None]
        sc = jnp.einsum('bqhd,bkhd->bhqk', qb, k).astype(jnp.float32) * scale
        sc = jnp.where(mask, sc, -jnp.inf)
        p = jax.nn.softmax(sc, axis=-1).astype(v.dtype)
        return jnp.einsum('bhqk,bkhd->bqhd', p, v)

    out = lax.map(one_block, (q_blocks, jnp.arange(nb)))
    return out.transpose(1, 0, 2, 3, 4).reshape(b, s, h, v.shape[-1])

def _mla_mixer(x, cos, sin, w_in, q_norm, w_qb, kv_norm, w_kvb, w_out):
    b, s, _ = x.shape
    proj = x @ w_in
    c_q, c_kv, k_rope, z = jnp.split(
        proj, [Q_LORA, Q_LORA + KV_LORA, Q_LORA + KV_LORA + QK_ROPE], axis=-1)
    q = (_rmsnorm(c_q, q_norm) @ w_qb).reshape(b, s, MLA_HEADS, MLA_QK)
    q_nope, q_rope = q[..., :QK_NOPE], q[..., QK_NOPE:]
    kv = (_rmsnorm(c_kv, kv_norm) @ w_kvb).reshape(b, s, MLA_HEADS, QK_NOPE + V_HEAD)
    k_nope, v = kv[..., :QK_NOPE], kv[..., QK_NOPE:]
    q_rope = _rope(q_rope, cos[:, :, None, :], sin[:, :, None, :])
    k_rope = _rope(k_rope, cos, sin)
    q = jnp.concatenate([q_nope, q_rope], axis=-1)
    k = jnp.concatenate(
        [k_nope, jnp.broadcast_to(k_rope[:, :, None, :], (b, s, MLA_HEADS, QK_ROPE))], axis=-1)
    attn = _chunk_causal_attention(q, k, v).reshape(b, s, MLA_WIDTH)
    return (attn * jax.nn.silu(z)) @ w_out

def _causal_depthwise_conv(x, w, bias):
    c = x.shape[-1]
    y = lax.conv_general_dilated(
        x, w[:, None, :], window_strides=(1,), padding=[(CONV_W - 1, 0)],
        dimension_numbers=('NWC', 'WIO', 'NWC'), feature_group_count=c)
    return y + bias

def _mlstm_chunkwise(q, k, v, i_pre, f_pre):
    b, s, h, dk = q.shape
    dv = v.shape[-1]
    nc = s // CHUNK
    f32 = jnp.float32

    def chunks(t):
        return t.astype(f32).reshape(b, nc, CHUNK, h, -1).transpose(1, 0, 3, 2, 4)

    def gate_chunks(t):
        return t.astype(f32).reshape(b, nc, CHUNK, h).transpose(1, 0, 3, 2)

    qc = chunks(q)
    kc = chunks(k) * (dk ** -0.5)
    vc = chunks(v)
    log_i = gate_chunks(i_pre)
    log_f = jax.nn.log_sigmoid(gate_chunks(f_pre))
    tril = jnp.tril(jnp.ones((CHUNK, CHUNK), dtype=bool))

    def step(carry, xs):
        c_st, n_st, m_st = carry
        qx, kx, vx, li, lf = xs
        bcum = jnp.cumsum(lf, axis=-1)
        dmat = bcum[..., :, None] - bcum[..., None, :] + li[..., None, :]
        dmat = jnp.where(tril, dmat, -jnp.inf)
        m_inter = bcum + m_st[..., None]
        m_t = jnp.maximum(m_inter, jnp.max(dmat, axis=-1))
        w_inter = jnp.exp(m_inter - m_t)
        s_qk = jnp.einsum('bhtd,bhsd->bhts', qx, kx) * jnp.exp(dmat - m_t[..., None])
        num = (w_inter[..., None] * jnp.einsum('bhtd,bhdv->bhtv', qx, c_st)
               + jnp.einsum('bhts,bhsv->bhtv', s_qk, vx))
        den = w_inter * jnp.einsum('bhtd,bhd->bht', qx, n_st) + jnp.sum(s_qk, axis=-1)
        h_out = num / jnp.maximum(jnp.abs(den), jnp.exp(-m_t))[..., None]
        b_last = bcum[..., -1]
        g = b_last[..., None] - bcum + li
        m_new = jnp.maximum(b_last + m_st, jnp.max(g, axis=-1))
        decay = jnp.exp(b_last + m_st - m_new)
        wk = jnp.exp(g - m_new[..., None])
        c_new = decay[..., None, None] * c_st + jnp.einsum('bhs,bhsd,bhsv->bhdv', wk, kx, vx)
        n_new = decay[..., None] * n_st + jnp.einsum('bhs,bhsd->bhd', wk, kx)
        return (c_new, n_new, m_new), h_out

    init = (jnp.zeros((b, h, dk, dv), f32), jnp.zeros((b, h, dk), f32), jnp.zeros((b, h), f32))
    _, hs = lax.scan(step, init, (qc, kc, vc, log_i, log_f))
    return hs.transpose(1, 0, 3, 2, 4).reshape(b, s, h, dv)

def _mlstm_mixer(x, w_in, conv_w, conv_b, gate_b, head_norm, w_out):
    b, s, _ = x.shape
    proj = x @ w_in
    o1 = 2 * ML_QK_WIDTH
    o2 = o1 + ML_WIDTH
    o3 = o2 + ML_WIDTH
    o4 = o3 + 2 * ML_HEADS
    qk, v, o, gates, z = jnp.split(proj, [o1, o2, o3, o4], axis=-1)
    qk = jax.nn.silu(_causal_depthwise_conv(qk, conv_w, conv_b))
    q, k = jnp.split(qk, 2, axis=-1)
    gates = gates + gate_b
    i_pre, f_pre = gates[..., :ML_HEADS], gates[..., ML_HEADS:]
    cell = _mlstm_chunkwise(q.reshape(b, s, ML_HEADS, ML_QK), k.reshape(b, s, ML_HEADS, ML_QK),
                            v.reshape(b, s, ML_HEADS, ML_V), i_pre, f_pre)
    cell = _rmsnorm(cell.astype(x.dtype), head_norm.reshape(ML_HEADS, ML_V)).reshape(b, s, ML_WIDTH)
    hcell = jax.nn.sigmoid(o) * cell
    return (hcell * jax.nn.silu(z)) @ w_out

def first_inputs(seed: int = 0) -> dict:
    key = jax.random.key(seed)
    ks = jax.random.split(key, 20)
    n_a = (DEPTH + N_MIXERS - 1) // N_MIXERS
    n_b = DEPTH // N_MIXERS

    def nrm(k, shape, scale):
        return jax.random.normal(k, shape, jnp.float32) * scale

    x = nrm(ks[0], (BATCH, SEQ, D_MODEL), 1.0)
    offsets = jax.random.randint(ks[1], (BATCH, 1), 0, 4096, dtype=jnp.int32)
    positions = offsets + jnp.arange(SEQ, dtype=jnp.int32)[None, :]

    mla_w_in = nrm(ks[2], (n_a, D_MODEL, MLA_IN), D_MODEL ** -0.5)
    mla_q_norm = 1.0 + nrm(ks[3], (n_a, Q_LORA), 0.02)
    mla_w_qb = nrm(ks[4], (n_a, Q_LORA, MLA_HEADS * MLA_QK), Q_LORA ** -0.5)
    mla_kv_norm = 1.0 + nrm(ks[5], (n_a, KV_LORA), 0.02)
    mla_w_kvb = nrm(ks[6], (n_a, KV_LORA, MLA_HEADS * (QK_NOPE + V_HEAD)), KV_LORA ** -0.5)
    mla_w_out = nrm(ks[7], (n_a, MLA_WIDTH, D_MODEL), BETA * MLA_WIDTH ** -0.5)

    ml_w_in = nrm(ks[8], (n_b, D_MODEL, ML_IN), D_MODEL ** -0.5)
    ml_conv_w = nrm(ks[9], (n_b, CONV_W, 2 * ML_QK_WIDTH), CONV_W ** -0.5)
    ml_conv_b = nrm(ks[10], (n_b, 2 * ML_QK_WIDTH), 0.02)
    i_bias = nrm(ks[11], (n_b, ML_HEADS), 0.1)
    f_bias = jnp.linspace(3.0, 6.0, ML_HEADS, dtype=jnp.float32)[None, :] + nrm(ks[12], (n_b, ML_HEADS), 0.1)
    ml_gate_b = jnp.concatenate([i_bias, f_bias], axis=-1)
    ml_head_norm = 1.0 + nrm(ks[13], (n_b, ML_WIDTH), 0.02)
    ml_w_out = nrm(ks[14], (n_b, ML_WIDTH, D_MODEL), BETA * ML_WIDTH ** -0.5)

    ln_w = 1.0 + nrm(ks[15], (DEPTH, D_MODEL), 0.02)
    ln_b = nrm(ks[16], (DEPTH, D_MODEL), 0.02)
    return {'x': x, 'positions': positions,
            'mla_w_in': mla_w_in, 'mla_q_norm': mla_q_norm, 'mla_w_qb': mla_w_qb,
            'mla_kv_norm': mla_kv_norm, 'mla_w_kvb': mla_w_kvb, 'mla_w_out': mla_w_out,
            'ml_w_in': ml_w_in, 'ml_conv_w': ml_conv_w, 'ml_conv_b': ml_conv_b,
            'ml_gate_b': ml_gate_b, 'ml_head_norm': ml_head_norm, 'ml_w_out': ml_w_out,
            'ln_w': ln_w, 'ln_b': ln_b}

def first_block(x, positions, mla_w_in, mla_q_norm, mla_w_qb, mla_kv_norm, mla_w_kvb, mla_w_out,
              ml_w_in, ml_conv_w, ml_conv_b, ml_gate_b, ml_head_norm, ml_w_out, ln_w, ln_b):
    cos, sin = _rope_tables(positions, x.dtype)
    for layer in range(DEPTH):
        j = layer // N_MIXERS
        if layer % N_MIXERS == 0:
            y = _mla_mixer(x, cos, sin, mla_w_in[j], mla_q_norm[j], mla_w_qb[j],
                           mla_kv_norm[j], mla_w_kvb[j], mla_w_out[j])
        else:
            y = _mlstm_mixer(x, ml_w_in[j], ml_conv_w[j], ml_conv_b[j], ml_gate_b[j],
                             ml_head_norm[j], ml_w_out[j])
        x = _layernorm(ALPHA * x + y, ln_w[layer], ln_b[layer])
    return x


N_A_LAYERS = DEPTH // 2
N_B_LAYERS = DEPTH - N_A_LAYERS
HG_KDIM = 128
HG_HEADS = D_MODEL // HG_KDIM
HG_VDIM = D_MODEL // HG_HEADS
HG_FDIM = HG_HEADS * HG_KDIM
HG_BLOCK = CHUNK // 4
FOX_HDIM = 128
FOX_HEADS = D_MODEL // FOX_HDIM
FORGET_BIAS_INIT = 2.0


def rmsnorm(x, w):
    xf = x.astype(jnp.float32)
    y = xf * lax.rsqrt(jnp.mean(xf * xf, axis=-1, keepdims=True) + EPS)
    return (y * w.astype(jnp.float32)).astype(x.dtype)

def head_rmsnorm(x, w):
    xf = x.astype(jnp.float32)
    return xf * lax.rsqrt(jnp.mean(xf * xf, axis=-1, keepdims=True) + EPS) * w.astype(jnp.float32)

def hgrn2_chunkwise(q, k, v, g):
    B, H, T, dk = q.shape
    dv = v.shape[-1]
    n = T // HG_BLOCK

    def to_blocks(a):
        return jnp.moveaxis(a.reshape(B, H, n, HG_BLOCK, a.shape[-1]), 2, 0)

    mask = jnp.tril(jnp.ones((HG_BLOCK, HG_BLOCK), dtype=bool))[:, :, None]

    def step(S, blk):
        qc, kc, vc, gc = blk
        b = jnp.cumsum(gc, axis=-2)
        diff = b[..., :, None, :] - b[..., None, :, :]
        decay = jnp.exp(jnp.where(mask, diff, -jnp.inf))
        A = jnp.einsum('bhtd,bhsd,bhtsd->bhts', qc, kc, decay)
        o = (jnp.einsum('bhts,bhse->bhte', A, vc)
             + jnp.einsum('bhtd,bhde->bhte', qc * jnp.exp(b), S))
        b_last = b[..., -1:, :]
        S = (jnp.exp(b_last[..., 0, :])[..., None] * S
             + jnp.einsum('bhsd,bhse->bhde', kc * jnp.exp(b_last - b), vc))
        return S, o

    S0 = jnp.zeros((B, H, dk, dv), jnp.float32)
    _, o = lax.scan(step, S0, (to_blocks(q), to_blocks(k), to_blocks(v), to_blocks(g)))
    return jnp.moveaxis(o, 0, 2).reshape(B, H, T, dv)

def hgrn2_layer(x, norm_w, w_in, lb, out_norm_w, w_out):
    B, T, _ = x.shape
    h = rmsnorm(x, norm_w)
    proj = h @ w_in
    q = proj[..., :HG_FDIM]
    fz = proj[..., HG_FDIM:2 * HG_FDIM]
    i = proj[..., 2 * HG_FDIM:2 * HG_FDIM + D_MODEL]
    gate = proj[..., 2 * HG_FDIM + D_MODEL:]
    heads_k = lambda a: a.reshape(B, T, HG_HEADS, HG_KDIM).astype(jnp.float32).transpose(0, 2, 1, 3)
    q, fz = heads_k(q), heads_k(fz)
    i = i.reshape(B, T, HG_HEADS, HG_VDIM).astype(jnp.float32).transpose(0, 2, 1, 3)
    lb = lb.reshape(HG_HEADS, 1, HG_KDIM)
    log_f = jnp.logaddexp(jnp.log(lb), jnp.log1p(-lb) + jax.nn.log_sigmoid(fz))
    k = (1.0 - lb) * jax.nn.sigmoid(-fz)
    o = hgrn2_chunkwise(q, k, i, log_f)
    o = head_rmsnorm(o.transpose(0, 2, 1, 3), out_norm_w.reshape(HG_HEADS, HG_VDIM))
    o = o.reshape(B, T, D_MODEL) * jax.nn.silu(gate.astype(jnp.float32))
    return x + (o.astype(x.dtype) @ w_out)

def shared_kv(x, norm_w, w_kvf, f_bias, k_norm_w):
    B, T, _ = x.shape
    h = rmsnorm(x, norm_w)
    kvf = h @ w_kvf
    k = kvf[..., :D_MODEL].reshape(B, T, FOX_HEADS, FOX_HDIM)
    v = kvf[..., D_MODEL:2 * D_MODEL].reshape(B, T, FOX_HEADS, FOX_HDIM)
    fz = kvf[..., 2 * D_MODEL:].astype(jnp.float32) + f_bias.astype(jnp.float32)
    k = head_rmsnorm(k, k_norm_w).transpose(0, 2, 1, 3)
    v = v.astype(jnp.float32).transpose(0, 2, 1, 3)
    F = jnp.cumsum(jax.nn.log_sigmoid(fz), axis=1).transpose(0, 2, 1)
    return k, v, F

def forgetting_attention(q, k, v, F):
    T = q.shape[2]
    scale = FOX_HDIM ** -0.5
    local = jnp.arange(Q_BLOCK)
    outs = []
    for blk in range(T // Q_BLOCK):
        q0 = blk * Q_BLOCK
        kend = q0 + Q_BLOCK
        s = (jnp.einsum('bhqd,bhkd->bhqk', q[:, :, q0:kend], k[:, :, :kend]) * scale
             + F[:, :, q0:kend, None] - F[:, :, None, :kend])
        causal = (q0 + local)[:, None] >= jnp.arange(kend)[None, :]
        p = jax.nn.softmax(jnp.where(causal, s, -jnp.inf), axis=-1)
        outs.append(jnp.einsum('bhqk,bhkd->bhqd', p, v[:, :, :kend]))
    return jnp.concatenate(outs, axis=2)

def fox_layer(x, norm_w, w_in, q_norm_w, out_norm_w, w_out, k, v, F):
    B, T, _ = x.shape
    h = rmsnorm(x, norm_w)
    proj = h @ w_in
    q = proj[..., :D_MODEL].reshape(B, T, FOX_HEADS, FOX_HDIM)
    gate = proj[..., D_MODEL:]
    q = head_rmsnorm(q, q_norm_w).transpose(0, 2, 1, 3)
    o = forgetting_attention(q, k, v, F)
    o = head_rmsnorm(o.transpose(0, 2, 1, 3), out_norm_w.reshape(FOX_HEADS, FOX_HDIM))
    o = o.reshape(B, T, D_MODEL) * jax.nn.silu(gate.astype(jnp.float32))
    return x + (o.astype(x.dtype) @ w_out)

def second_inputs(seed: int = 0) -> dict:
    key = jax.random.key(seed)
    ks = jax.random.split(key, 16)
    D = D_MODEL
    s = D ** -0.5
    nrm = jax.random.normal
    return {
        "x": nrm(ks[0], (BATCH, SEQ, D), jnp.float32),
        "a_norm_w": 1.0 + 0.02 * nrm(ks[1], (N_A_LAYERS, D), jnp.float32),
        "a_w_in": s * nrm(ks[2], (N_A_LAYERS, D, 2 * HG_FDIM + 2 * D), jnp.float32),
        "a_lb_logits": 0.1 * nrm(ks[3], (N_A_LAYERS, HG_FDIM), jnp.float32),
        "a_out_norm_w": 1.0 + 0.02 * nrm(ks[4], (N_A_LAYERS, D), jnp.float32),
        "a_w_out": s * nrm(ks[5], (N_A_LAYERS, D, D), jnp.float32),
        "kv_norm_w": 1.0 + 0.02 * nrm(ks[6], (D,), jnp.float32),
        "kv_w": s * nrm(ks[7], (D, 2 * D + FOX_HEADS), jnp.float32),
        "kv_f_bias": FORGET_BIAS_INIT + 0.1 * nrm(ks[8], (FOX_HEADS,), jnp.float32),
        "k_norm_w": 1.0 + 0.02 * nrm(ks[9], (FOX_HDIM,), jnp.float32),
        "b_norm_w": 1.0 + 0.02 * nrm(ks[10], (N_B_LAYERS, D), jnp.float32),
        "b_w_in": s * nrm(ks[11], (N_B_LAYERS, D, 2 * D), jnp.float32),
        "b_q_norm_w": 1.0 + 0.02 * nrm(ks[12], (N_B_LAYERS, FOX_HDIM), jnp.float32),
        "b_out_norm_w": 1.0 + 0.02 * nrm(ks[13], (N_B_LAYERS, D), jnp.float32),
        "b_w_out": s * nrm(ks[14], (N_B_LAYERS, D, D), jnp.float32),
    }

def second_block(x, a_norm_w, a_w_in, a_lb_logits, a_out_norm_w, a_w_out,
              kv_norm_w, kv_w, kv_f_bias, k_norm_w,
              b_norm_w, b_w_in, b_q_norm_w, b_out_norm_w, b_w_out):
    lb_all = jnp.cumsum(jax.nn.softmax(a_lb_logits.astype(jnp.float32), axis=0), axis=0)
    lb_all = lb_all - lb_all[0:1]
    k = v = F = None
    for layer in range(DEPTH):
        if layer < N_A_LAYERS:
            x = hgrn2_layer(x, a_norm_w[layer], a_w_in[layer], lb_all[layer],
                            a_out_norm_w[layer], a_w_out[layer])
        else:
            if layer == N_A_LAYERS:
                k, v, F = shared_kv(x, kv_norm_w, kv_w, kv_f_bias, k_norm_w)
            j = layer - N_A_LAYERS
            x = fox_layer(x, b_norm_w[j], b_w_in[j], b_q_norm_w[j], b_out_norm_w[j],
                          b_w_out[j], k, v, F)
    return x


def setup_inputs(seed=0):
    out = dict(first_inputs(seed))
    for name, value in second_inputs(seed + 1).items():
        if name != "x":
            out[name + "_2"] = value
    return out


def reference(
    x, positions, mla_w_in, mla_q_norm, mla_w_qb, mla_kv_norm, mla_w_kvb, mla_w_out, ml_w_in,
    ml_conv_w, ml_conv_b, ml_gate_b, ml_head_norm, ml_w_out, ln_w, ln_b, a_norm_w_2, a_w_in_2,
    a_lb_logits_2, a_out_norm_w_2, a_w_out_2, kv_norm_w_2, kv_w_2, kv_f_bias_2, k_norm_w_2,
    b_norm_w_2, b_w_in_2, b_q_norm_w_2, b_out_norm_w_2, b_w_out_2,
):
    x = first_block(
        x, positions, mla_w_in, mla_q_norm, mla_w_qb, mla_kv_norm, mla_w_kvb, mla_w_out,
        ml_w_in, ml_conv_w, ml_conv_b, ml_gate_b, ml_head_norm, ml_w_out, ln_w, ln_b,
    )
    return second_block(
        x, a_norm_w_2, a_w_in_2, a_lb_logits_2, a_out_norm_w_2, a_w_out_2, kv_norm_w_2, kv_w_2,
        kv_f_bias_2, k_norm_w_2, b_norm_w_2, b_w_in_2, b_q_norm_w_2, b_out_norm_w_2, b_w_out_2,
    )


_drawn_inputs = setup_inputs


def setup_inputs(seed=0):
    import zlib

    import numpy as np

    out = dict(_drawn_inputs(seed))
    spreads = {}
    factors = {'mla_q_norm': 8.0,
     'mla_kv_norm': 8.0,
     'ml_conv_b': 3.538,
     'ml_head_norm': 8.0,
     'a_out_norm_w_2': 4.509,
     'kv_norm_w_2': 4.888,
     'kv_f_bias_2': 2.694,
     'k_norm_w_2': 8.0,
     'b_norm_w_2': 4.725,
     'b_q_norm_w_2': 8.0,
     'b_out_norm_w_2': 6.076}
    for name, (base, spread) in spreads.items():
        noise = np.random.default_rng([zlib.crc32(name.encode()), seed]).standard_normal(out[name].shape)
        drawn = base * np.exp(spread * noise) if base else spread * noise
        out[name] = __import__('jax').numpy.asarray(drawn.astype(out[name].dtype))
    for name, factor in factors.items():
        out[name] = (out[name] * factor).astype(out[name].dtype)
    return out
```

```python
from contextlib import ExitStack

import numpy as np
import concourse.bass as bass
from concourse import mybir

F32 = mybir.dt.float32
F32R = mybir.dt.float32r
I32 = mybir.dt.int32
U8 = mybir.dt.uint8
ALU = mybir.AluOpType
ACT = mybir.ActivationFunctionType
AX = mybir.AxisListType.X

P = 128
T = 256
TB = T // P
D = 2048
KT = D // P
COLS = 512
KU = 2
RAW = 8
SPLIT = 4
LAG = 3
EPS = 1e-6
NEG = -3.0e38
LN_EXP_SET = 6

H0, NOPE, ROPE, VH = 16, 128, 64, 128
LORA = 512
QH = NOPE + ROPE
THETA = 10000.0
H1, MQK, MV, CONV = 8, 128, 256, 4
H2, HD = 16, 128
ALPHA = 4 ** 0.25

COL_A = {"q_norm": (0, 4), "kv_norm": (4, 4), "conv_w": (8, 64), "conv_b": (72, 16), "head_norm": (88, 16)}
COL_B = {"a_norm": (0, 16), "a_out": (16, 16), "kvn": (32, 16), "b_norm": (48, 16), "b_out": (64, 16),
         "k_norm": (80, 1), "bq_norm": (81, 1)}
NA_ROWS, NB_ROWS = 104, 82


class Own:

    def __init__(self, eng, sem):
        self.eng, self.sem, self.n = eng, sem, 0
        self.it, self.per = 0, 0

    def mark(self, ins):
        ins.then_inc(self.sem, 1)
        self.n += 1

    def sync(self):
        self.eng.wait_ge(self.sem, self.n + self.it * self.per)

    def then(self, ins):
        self.mark(ins)
        self.sync()

    def enter(self, it, per):
        self.it, self.per, self.start = it, per, self.n
        self.n -= per

    def leave(self, runs):
        assert self.n + self.per - self.start == self.per, (self.n + self.per - self.start, self.per)
        self.n = self.start + runs * self.per
        self.it, self.per = 0, 0


def build(nc, a, out, depth=4):
    with ExitStack() as ctx:
        sb = lambda name, shape, dt=F32: ctx.enter_context(nc.sbuf_tensor(name, shape, dt))
        sem = lambda name: ctx.enter_context(nc.semaphore(name))

        x_res = sb("x_res", [P, TB, D])
        wraw = sb("wraw", [P, RAW, KU, COLS])
        whi = sb("whi", [P, SPLIT, KU, COLS], F32R)
        wlo = sb("wlo", [P, SPLIT, KU, COLS], F32R)
        TA = (sb("ta_hi", [P, KT, T], F32R), sb("ta_lo", [P, KT, T], F32R))
        TBf = (sb("tb_hi", [P, KT, T], F32R), sb("tb_lo", [P, KT, T], F32R))
        ident = sb("ident", [P, P])
        ones = sb("ones", [P, T])
        colA = sb("colA", [P, NA_ROWS])
        colB = sb("colB", [P, NB_ROWS])
        tmpT = sb("tmpT", [P, 2, COLS])
        bstat = sb("bstat", [P, TB, 4, 6])
        mv = sb("mv", [P, TB, 2])
        nrm = sb("nrm", [P, TB, 4])
        sm = sb("sm", [P, 64])
        mask = sb("mask", [P, 384])
        posi = sb("posi", [P, TB], I32)
        lvl = sb("lvl", [P, 7, 64], U8)
        gbias = sb("gbias", [P, 32])
        ARENA = 14080
        arena = sb("arena", [P, ARENA])

        acc = ctx.enter_context(nc.psum_tensor("acc", [P, 2, TB, COLS], F32))
        ps = ctx.enter_context(nc.psum_tensor("ps", [P, 4, COLS], F32))
        ps2 = lambda b: ps[:, b:b + 2, :].rearrange("p a n -> p (a n)")

        class Carve:

            def __init__(self):
                self.at = 0

            def __call__(self, *shape, rows=P):
                n = int(np.prod(shape))
                v = arena[0:rows, self.at:self.at + n]
                self.at += n + n % 2
                assert self.at <= ARENA, self.at
                if len(shape) == 2:
                    v = v.rearrange("p (a b) -> p a b", b=shape[1])
                elif len(shape) == 3:
                    v = v.rearrange("p (a b c) -> p a b c", b=shape[1], c=shape[2])
                return v

        w_loaded = [sem(f"w_loaded{i}") for i in range(RAW)]
        w_high = sem("w_high")
        w_low = sem("w_low")
        w_used = sem("w_used")
        out_act = sem("out_act")
        out_dve = sem("out_dve")
        x_in = sem("x_in")
        par_in = sem("par_in")
        bias_in = sem("bias_in")
        const_ok = sem("const_ok")
        pool_own, act_own, dve_own = sem("pool_own"), sem("act_own"), sem("dve_own")
        col_pe, col_ok = sem("col_pe"), sem("col_ok")
        rope_arg, rope_ok = sem("rope_arg"), sem("rope_ok")
        tr_src = sem("tr_src")
        tr_src_act = sem("tr_src_act")
        tr_pe = sem("tr_pe")
        tr_tmp = sem("tr_tmp")
        tr_hi, tr_lo = sem("tr_hi"), sem("tr_lo")
        y_act = sem("y_act")
        x_done = sem("x_done")
        lnp_in = sem("lnp_in")
        nrm_a, nrm_v = sem("nrm_a"), sem("nrm_v")
        st_out = sem("st_out")
        final_a = sem("final_a")

        L = [dict() for _ in range(4)]

        def S(layer, *names):
            for n in names:
                L[layer][n] = sem(f"l{layer}_{n}")
            return L[layer]

        W = {k: (a[k][0] if len(a[k].shape) == 3 else a[k]) for k in a if len(a[k].shape) >= 2 and a[k].shape[-1] > 500 and a[k].shape[-2] in (512, D)}
        Wv = {k: v.rearrange("(k p) n -> p k n", p=P) for k, v in W.items()}

        OUT_VIEWS = [Wv[k] for k in ("mla_w_out", "ml_w_out", "a_w_out_2", "b_w_out_2")]
        def first(it):
            return isinstance(it, int) and it == 0

        def units(tiles):
            return sum(t[1] for t in tiles) // KU

        def places(tiles):
            if any(tiles[0][0] is v for v in OUT_VIEWS):
                late = KT - KT // 4
                r = [(k, q) for k in (0, 1) for q in range(0, late, KU)]
                r += [(k, q) for k in (0, 1) for q in range(late, KT, KU)]
                return r + [(k, q) for k in (2, 3) for q in range(0, KT, KU)]
            return [(k, q) for k, t in enumerate(tiles) for q in range(0, t[1], KU)]

        def ends(name):
            tiles = PHD[name][1]
            at = places(tiles)
            return [max(i for i, (k, q) in enumerate(at) if k == n) for n in range(len(tiles))]

        UNIT, TILE = {}, {}
        PH = []
        u = t = 0

        def phase(name, tiles, runs):
            nonlocal u, t
            PH.append((name, tiles, runs))
            UNIT[name], TILE[name] = u, t
            u += units(tiles) * runs
            t += len(tiles) * runs
            assert units(tiles) % RAW == 0, name
            assert runs == 1 or len(tiles) % 2 == 0

        w_in, w_qb, w_kvb = Wv["mla_w_in"], Wv["mla_w_qb"], Wv["mla_w_kvb"]
        phase("l0_in", [(w_in, KT, 0, 0, 512), (w_in, KT, 512, 0, 512), (w_in, KT, 1024, 0, ROPE)], 1)
        for s in range(4):
            zs = [(w_in, KT, 1088 + 512 * j, 0, 512) for j in (2 * s, 2 * s + 1)] if s < 2 else []
            phase(f"l0_{s}", zs + [
                x for pr in range(2) for x in (
                    (w_qb, 4, (2 * s + pr) * 2 * QH, 0, 2 * QH),
                    (w_kvb, 4, (2 * s + pr) * 2 * (NOPE + VH), 0, 2 * (NOPE + VH)))], 1)
        out_tiles = lambda w: [(Wv[w], KT, c * COLS, 0, COLS) for c in range(4)]
        phase("l0_out", out_tiles("mla_w_out"), 1)
        w1 = Wv["ml_w_in"]
        phase("l1_gates", [(w1, KT, 6144, 0, 16)], 1)
        for s in range(2):
            phase(f"l1_{s}", [(w1, KT, 512 * s, 0, 512), (w1, KT, 1024 + 512 * s, 0, 512)]
                  + [(w1, KT, base + 1024 * s + 512 * j, 0, 512) for base in (2048, 4096, 6160) for j in range(2)], 1)
        phase("l1_out", out_tiles("ml_w_out"), 1)
        w2 = Wv["a_w_in_2"]
        phase("l2", [(w2, KT, D * j, COLS, COLS) for j in range(4)], 4)
        phase("l2_out", out_tiles("a_w_out_2"), 1)
        w3, w4 = Wv["kv_w_2"], Wv["b_w_in_2"]
        phase("l3_f", [(w3, KT, 2 * D, 0, 16)], 1)
        phase("l3_kv", [(w3, KT, D * j, COLS, COLS) for j in range(2)], 4)
        phase("l3_q", [(w4, KT, D * j, COLS, COLS) for j in range(2)], 4)
        phase("l3_out", out_tiles("b_w_out_2"), 1)
        PHD = {p[0]: p for p in PH}
        LAST = {1: "l0_out", 2: "l1_out", 3: "l2_out", 4: "l3_out"}[depth]

        def high(act, name, p, it=0):
            tiles = PHD[name][1]
            k, q = places(tiles)[p]
            w, nu, n = tiles[k][4], units(tiles), UNIT[name] + p
            act.wait_ge(w_loaded[n % RAW], 16 * (n // RAW + 1) + 16 * (nu // RAW) * it)
            if n >= SPLIT:
                act.wait_ge(w_used, n - SPLIT + 1 + nu * it)
            nc.scalar.activation(whi[:, n % SPLIT, :, 0:w], wraw[:, n % RAW, :, 0:w], ACT.Copy).then_inc(w_high, 1)

        def low(dve, name, p, it=0):
            tiles = PHD[name][1]
            k, q = places(tiles)[p]
            w, nu, n = tiles[k][4], units(tiles), UNIT[name] + p
            dve.wait_ge(w_high, n + 1 + nu * it)
            nc.vector.tensor_tensor(wlo[:, n % SPLIT, :, 0:w], wraw[:, n % RAW, :, 0:w],
                                    whi[:, n % SPLIT, :, 0:w].bitcast(F32), ALU.subtract).then_inc(w_low, 1)

        def products(pe, name, p, src, it=0):
            tiles = PHD[name][1]
            k, q = places(tiles)[p]
            w, kt, nu, n, tt = tiles[k][4], tiles[k][1], units(tiles), UNIT[name] + p, TILE[name] + k
            if q == 0:
                if tt >= 2:
                    pe.wait_ge(out_act, tt - 1 + len(tiles) * it)
                if tt >= 2:
                    pe.wait_ge(out_dve, tt - 1 + len(tiles) * it)
            pe.wait_ge(w_low, n + 1 + nu * it)
            for j in range(KU):
                for b in range(TB):
                    o = acc[:, tt % 2, b, 0:w]
                    hi, lo, kk = src(k, q + j)
                    xh, xl = hi[:, kk, b * P:(b + 1) * P], lo[:, kk, b * P:(b + 1) * P]
                    wh, wl = whi[:, n % SPLIT, j, 0:w], wlo[:, n % SPLIT, j, 0:w]
                    first, end = q + j == 0, q + j == kt - 1
                    nc.tensor.matmul(o, xh, wh, start=first, stop=False)
                    nc.tensor.matmul(o, xh, wl, start=False, stop=False)
                    m = nc.tensor.matmul(o, xl, wh, start=False, stop=end)
            m.then_inc(w_used, 1)

        def tile_done(eng, name, k, it=0):
            tiles = PHD[name][1]
            eng.wait_ge(w_used, UNIT[name] + ends(name)[k] + 1 + units(tiles) * it)

        def evac_act(act, name, k, dst, it=0):
            w = PHD[name][1][k][4]
            tile_done(act, name, k, it)
            nc.scalar.activation(dst, acc[:, (TILE[name] + k) % 2, 0, 0:w], ACT.Copy).then_inc(out_act, 1)

        def evac_dve(dve, name, k, dst, it=0):
            w = PHD[name][1][k][4]
            tile_done(dve, name, k, it)
            nc.vector.tensor_copy(dst, acc[:, (TILE[name] + k) % 2, 1, 0:w]).then_inc(out_dve, 1)

        def landed(eng, name, k, it=0):
            n = TILE[name] + k + 1
            eng.wait_ge(out_act, n + len(PHD[name][1]) * it)
            eng.wait_ge(out_dve, n + len(PHD[name][1]) * it)

        def carried(name):
            nu = length(name)
            return {e + LAG - nu: k for k, e in enumerate(ends(name)) if e + LAG >= nu}

        def length(name):
            return units(PHD[name][1])

        def late(name, at):
            return min(at + LAG, length(name) - 1)

        def step(eng, split, evac, name, p, it=0, prev=None):
            split(eng, name, p, it)
            if prev and p in carried(prev[0]):
                evac(prev[0], carried(prev[0])[p], prev[1])
            for k, e in enumerate(ends(name)):
                if p == e + LAG:
                    evac(name, k, it)

        def finish(evac, name, it=0):
            for p, k in sorted(carried(name).items()):
                evac(name, k, it)

        class Turn:
            def __init__(self):
                self.n, self.w = 0, 0

        def turn_pe(pe, cnt, srcs):
            c = cnt.n
            if c >= 4:
                pe.wait_ge(tr_lo, c - 3)
            for j, s in enumerate(srcs):
                m = nc.tensor.transpose(ps[:, c % 4, j * P:(j + 1) * P], s, ident[:])
            m.then_inc(tr_pe, 1)
            cnt.n += 1

        def turn_act(act, cnt, dst, weighted):
            c = cnt.n
            if weighted:
                act.wait_ge(tr_tmp, cnt.w + 1)
                src = tmpT[:, cnt.w % 2, :].rearrange("p (k t) -> p k t", t=P)
                cnt.w += 1
            else:
                act.wait_ge(tr_pe, c + 1)
                src = ps[:, c % 4, :].rearrange("p (k t) -> p k t", t=P)
            nc.scalar.activation(dst, src, ACT.Copy).then_inc(tr_hi, 1)
            cnt.n += 1

        def turn_dve(dve, cnt, dst_hi, dst_lo, col=None):
            c = cnt.n
            bank = ps[:, c % 4, :].rearrange("p (k t) -> p k t", t=P)
            if col is not None:
                dve.wait_ge(tr_pe, c + 1)
                src = tmpT[:, cnt.w % 2, :].rearrange("p (k t) -> p k t", t=P)
                nc.vector.tensor_tensor(src, bank, col.unsqueeze(2).to_broadcast([P, 4, P]), ALU.mult).then_inc(tr_tmp, 1)
                cnt.w += 1
            else:
                src = bank
            dve.wait_ge(tr_hi, c + 1)
            nc.vector.tensor_tensor(dst_lo, src, dst_hi.bitcast(F32), ALU.subtract).then_inc(tr_lo, 1)
            cnt.n += 1

        A = Carve()
        lat = A(2 * TB * LORA)
        cq = lat.rearrange("p (b n) -> p b n", b=TB)
        ez, og0 = [v.rearrange("p (b n) -> p b n", b=TB) for v in (lat[:, 0:1024], lat[:, 1024:2048])]
        krT, cos, sin = A(T), A(TB, 32), A(TB, 32)
        qw1 = A(TB * 2 * QH)
        krw = qw1[:, 0:128].rearrange("p (b n) -> p b n", b=TB)
        krd = qw1[:, 128:384].rearrange("p (b a n) -> p b a n", b=TB, a=2)
        qw = [A(TB, 2 * QH), qw1.rearrange("p (b n) -> p b n", b=TB)]
        kvw = [A(TB, 512) for _ in range(2)]
        zw = [A(TB, 512) for _ in range(4)]
        early = Carve()
        early.at = A.at - 2048
        stage_rows, posf, invf, lvf, angle = early(2, P), early(4), early(32), early(7, 64), early(6, TB * 32)
        qr, rt = A(TB, 2, ROPE), A(4, TB * 2 * 32)
        qT0, kT0, qrT0 = A(2, T), A(2, T), A(T)
        sS, sPT = A(2, 384), A(2, 384)

        A = Carve()
        A.at = 4 * D
        hn = A(TB, D)
        lnw, lnb = arena[:, 0:D], arena[:, D:2 * D]

        def sems(layer, names):
            return {n: sem(f"l{layer}_{n}") for n in names.split()}

        l0 = sems(0, "lat_sq lat_v lat_r lat_ok kr_ok kr_pe kr_T z_e z_ok rope tr trA trV sc msk mx ex pt ptc pv o")

        SMALL = 24

        class Heads:
            def __init__(self, l, scale, mask, qk, v, S, PT):
                self.l, self.scale, self.mask, self.qk, self.v, self.S, self.PT = l, scale, mask, qk, v, S, PT

            def scores(self, pe, g, hh):
                c, w = 4 * g + hh, hh % 2
                if hh >= 2:
                    pe.wait_ge(self.l["msk"], c - 1)
                for b in range(TB):
                    o = ps[:, w, b * P:b * P + (b + 1) * P]
                    parts = self.qk(c, b)
                    for i, (x, y) in enumerate(parts):
                        m = nc.tensor.matmul(o, x, y, start=i == 0, stop=i == len(parts) - 1)
                m.then_inc(self.l["sc"], 1)

            def mask_max(self, dve, own, g, hh):
                c, w = 4 * g + hh, hh % 2
                dve.wait_ge(self.l["sc"], c + 1)
                if hh >= 2:
                    dve.wait_ge(self.l["pt"], c - 1)
                s = self.S[:, w, :]
                nc.vector.scalar_tensor_tensor(s, ps[:, w, 0:384], self.scale, self.mask[:], ALU.mult,
                                               ALU.add).then_inc(self.l["msk"], 1)
                dve.wait_ge(self.l["msk"], c + 1)
                n = sm[:, 2 * w:2 * w + 2]
                nc.vector.tensor_reduce(n[:, 0:1], s[:, 0:P], AX, ALU.max, negate=True).then_inc(self.l["mx"], 1)
                nc.vector.tensor_reduce(n[:, 1:2], s[:, P:384], AX, ALU.max, negate=True).then_inc(self.l["mx"], 1)

            def weights(self, act, g, hh):
                c, w = 4 * g + hh, hh % 2
                act.wait_ge(self.l["mx"], 2 * c + 2)
                if hh >= 2:
                    act.wait_ge(self.l["o"], 2 * (c - 1))
                s = self.S[:, w, :]
                for b in range(TB):
                    v = s[:, 0:P] if b == 0 else s[:, P:384]
                    nc.scalar.activation(v, v, ACT.Exp, bias=sm[:, 2 * w + b:2 * w + b + 1],
                                         accum_out=sm[:, 4 + 2 * w + b:5 + 2 * w + b]).then_inc(self.l["ex"], 1)

            def turn(self, pe, g, hh):
                c, w = 4 * g + hh, hh % 2
                pe.wait_ge(self.l["ex"], 2 * c + 2)
                if c > 0:
                    pe.wait_ge(self.l["ptc"], c)
                for j in range(3):
                    m = nc.tensor.transpose(ps[:, 2, j * P:(j + 1) * P], self.S[:, w, j * P:(j + 1) * P], ident[:])
                m.then_inc(self.l["pt"], 1)

            def copy(self, act, g, hh):
                c, w = 4 * g + hh, hh % 2
                act.wait_ge(self.l["pt"], c + 1)
                if hh >= 2:
                    act.wait_ge(self.l["pv"], c - 1)
                nc.scalar.activation(self.PT[:, w, :], ps[:, 2, 0:384], ACT.Copy).then_inc(self.l["ptc"], 1)

            def values(self, pe, g, hh):
                c, w = 4 * g + hh, hh % 2
                pe.wait_ge(self.l["ptc"], c + 1)
                if c > 0:
                    pe.wait_ge(self.l["o"], 2 * c)
                pt = self.PT[:, w, :]
                nc.tensor.matmul(ps[:, 3, 0:P], pt[:, 0:P], self.v(c, 0), start=True, stop=True)
                nc.tensor.matmul(ps[:, 3, P:T], pt[:, P:T], self.v(c, 0), start=True, stop=False)
                nc.tensor.matmul(ps[:, 3, P:T], pt[:, T:384], self.v(c, 1), start=False, stop=True).then_inc(self.l["pv"], 1)

            def inverse(self, dve, own, g, hh):
                c, w = 4 * g + hh, hh % 2
                dve.wait_ge(self.l["pv"], c + 1)
                r = sm[:, 8 + 2 * w:10 + 2 * w]
                own.then(nc.vector.reciprocal(r, sm[:, 4 + 2 * w:6 + 2 * w]))
                return r

        def mla_qk(c, b):
            hh, n = c % 2, (b + 1) * P
            r = slice(hh * ROPE, (hh + 1) * ROPE)
            return [(qT0[:, hh, b * P:(b + 1) * P], kT0[:, hh, 0:n]),
                    (qrT0[r, b * P:(b + 1) * P], krT[r, 0:n])]

        mla = Heads(l0, QH ** -0.5, mask, mla_qk,
                    lambda c, b: kvw[c // 2 % 2][:, b, (c % 2) * 256 + NOPE:(c % 2) * 256 + 256], sS, sPT)

        def latent_src(k, q, s):
            z = 2 if s < 2 else 0
            if k < z:
                return TA[0], TA[1], q
            return TBf[0], TBf[1], q + 4 * ((k - z) % 2)

        def out0_src(k, q):
            return (TBf[0], TBf[1], 8 + q) if q < 8 else (TA[0], TA[1], q)

        def og0_dst(s, hl, b):
            t = TBf if s < 2 else TA
            return t[hl][:, (8 if s < 2 else 0) + 4 * s:(8 if s < 2 else 0) + 4 * s + 4, b * P:(b + 1) * P]

        def dst_l0(name, k, b, it):
            if name == "l0_in":
                return [cq[:, b, 0:LORA], cq[:, b, LORA:], krw[:, b, :]][k]
            s = int(name[3])
            z = 2 if s < 2 else 0
            if k < z:
                return zw[2 * s + k][:, b, :]
            return (qw if (k - z) % 2 == 0 else kvw)[(k - z) // 2][:, b, :]

        RES = {"l0_out": 0, "l1_out": 1, "l2_out": 2, "l3_out": 3}
        LN = {0: 0, 1: 1}
        NRM_AT = [0, 2, 4, 5]

        def DST(name, k, b, it, eng):
            return [dst_l0, dst_l1, dst_l2, dst_l3][int(name[1])](name, k, b, it)

        def FREE(eng, name, k, it):
            [free_l0, free_l1, free_l2, free_l3][int(name[1])](eng, name, k, it)

        def free_l0(eng, name, k, it):
            if name == "l0_in":
                return
            s = int(name[3])
            z = 2 if s < 2 else 0
            if k < z:
                eng.wait_ge(l0["lat_sq"], 4)
                eng.wait_ge(rope_ok, 2)
                return
            pr = (k - z) // 2
            if (k - z) % 2 == 0:
                if 2 * s + pr - 1 > 0:
                    eng.wait_ge(l0["tr"], 2 * s + pr - 1)
                eng.wait_ge(l0["kr_pe"], 1)
            else:
                if 4 * s + 2 * pr - 2 > 0:
                    eng.wait_ge(l0["pv"], 4 * s + 2 * pr - 2)

        def l0_tile(s, pr, kind):
            return (2 if s < 2 else 0) + 2 * pr + kind

        def spread(n, nu, first=0):
            return [first + i * (nu - first) // n for i in range(n)]

        L0_STAGES = 11
        L0_PHASES = ["l0_0", "l0_1", "l0_2", "l0_3", "l0_out"]

        def l0_at(name):
            return spread(L0_STAGES, 12 if name == "l0_out" else length(name))

        def l0_late(name):
            return [late(name, at) for at in l0_at(name)]

        A = Carve()
        qkw1 = A(2 * TB * COLS)
        qkw = [v.rearrange("p (b n) -> p b n", b=TB) for v in (qkw1[:, 0:1024], qkw1[:, 1024:2048])]
        hq = qkw1.rearrange("p (b h n) -> p b h n", b=TB, h=4)
        VW = MV + 2
        vw = A(TB, 4, VW)
        ow, zw1 = A(TB, 4 * MV), A(TB, COLS)
        PAD = 4
        cin = A(4, PAD + T)
        qkT = A(8 * T)
        qT1, kT1 = [v.rearrange("p (h t) -> p h t", t=T) for v in (qkT[:, 0:4 * T], qkT[:, 4 * T:])]
        esc = A(4 * T)
        arg = A(2, 384)
        gt = A(TB, 16)
        grow = qkT[0:8, 0:6 * T].rearrange("p (a t) -> p a t", t=T)
        negM = A(T, rows=8)
        acol, emcol = A(TB, 8), A(TB, 8)
        wst = A(384)
        l1 = sems(1, "g_in g_pe g_row g_e g_lf g_m g_pe2 g_col q_pe q_c y_ok y_e y_s q_r sc arg ex sel st nm "
                     "den h ssq var rs og ge z_ok pads")

        def dst_l1(name, k, b, it):
            if name == "l1_gates":
                return gt[:, b, :]
            if k < 2:
                return qkw[k][:, b, :]
            if k < 4:
                return vw[:, b, 2 * (k - 2):2 * (k - 2) + 2, 0:MV]
            if k < 6:
                return ow[:, b, (k - 4) * COLS:(k - 3) * COLS]
            return zw1[:, b, :]

        def free_l1(eng, name, k, it):
            if name == "l1_gates":
                return
            s = int(name[3])
            if k < 2:
                if s > 0:
                    eng.wait_ge(l1["og"], 8 * s)
                eng.wait_ge(tr_src, 2)
            elif k < 4:
                if s > 0 or k > 3:
                    eng.wait_ge(l1["nm"], 4 * s - 2 + 2 * (k - 2))
            elif k < 6:
                if s > 0:
                    eng.wait_ge(tr_pe, L1_TURNS[s][k - 4])
            else:
                if s > 0 or k > 6:
                    eng.wait_ge(l1["z_ok"], 2 * (2 * s + k - 6))

        L1_BASE = 8 + 4 + 8 + 8
        L1_TURNS = [[0, 0], [L1_BASE + 2, L1_BASE + 4]]
        L1_AT = {"q": 11, "k": 19, "ws": [25, 31, 37, 43], "nm": [29, 35, 41, 47], "g0": 59, "t0": 62}
        L1_PREV = {0: {"ga": 4, "gb": 5, "gc": 8}, 1: {"g1": 3, "t1": 6}}
        def out1_src(k, q):
            return TBf[0], TBf[1], q

        A = Carve()
        qw2, fw2, vw2, gw2 = [A(TB, COLS) for _ in range(4)]
        G4 = 4 * T
        qT2, kT2, bT2 = A(4, T), A(4, T), A(4, T)
        aT = A(8, P)
        a01 = A(4, P)
        dT = A(2, G4)
        qx = A(2, 2 * T)
        l2 = sems(2, "tq tf qT nf lf kx kt ge gs dg at df ee op lv sel pv sq ss v rs on og ogp tmp hi lo")

        def dst_l2(name, k, b, it):
            return (qw2, fw2, vw2, gw2)[k][:, b, :]

        def free_l2(eng, name, k, it):
            if k < 2:
                if not first(it):
                    eng.wait_ge(l2["tf"], it)
            elif k == 2:
                if not first(it):
                    eng.wait_ge(l2["pv"], it)
            else:
                if not first(it):
                    eng.wait_ge(l2["ogp"], TB * it)

        L2_AT = {"turn": 0, "diag": 5, "level": [7, 9, 11, 13, 15, 17, 19, 21], "pv": 24, "norm": 24, "back": 28}
        L2_OWN, L3_OWN = 9, 8
        L2_END = {"turn": 0, "diag": 1, "level": [2, 3, 4, 5, 6, 7, 8, 9], "pv": 10, "norm": 10, "back": 11}

        def group(first, g, n=4):
            return slice(first + n * g, first + n * g + n) if isinstance(g, int) else bass.ds(first + n * g, n)

        def heads_of(t, g, b):
            return t[:, group(0, g), b * P:(b + 1) * P]

        A = Carve()
        kT3, v3 = A(H2, T), A(TB, D)
        qw3, gw3 = A(TB, COLS), A(TB, COLS)
        qT3 = A(4, T)
        S3, PT3 = A(2, 384), A(2, 384)
        o3 = A(TB, COLS)
        negF = ones[0:16, 0:T]
        frow = kT3[0:16, 8:12, :]
        ft = A(TB, 16)
        sqj = A(P)
        l3 = sems(3, "f_in f_pe f_row f_e f_ok ksq kv_ krs kn kt kT qsq qv qrs qn qt qT sc msk mx ex pt ptc pv o "
                     "ge gs sq ss v rs on og ogp tmp hi lo")

        def dst_l3(name, k, b, it):
            if name == "l3_f":
                return ft[:, b, :]
            if name == "l3_kv" and k == 1:
                return v3[:, b, group_cols(it)]
            return (qw3, gw3)[k][:, b, :]

        def group_cols(it):
            return slice(COLS * it, COLS * it + COLS) if isinstance(it, int) else bass.ds(COLS * it, COLS)

        def free_l3(eng, name, k, it):
            if name == "l3_f":
                return
            if k == 0:
                if name == "l3_kv":
                    if not first(it):
                        eng.wait_ge(l3["kt"], it)
                    eng.wait_ge(tr_lo, T3)
                else:
                    eng.wait_ge(l3["kt"], 4)
                    if not first(it):
                        eng.wait_ge(l3["qt"], it)
            elif name == "l3_kv":
                eng.wait_ge(tr_lo, T3)
            else:
                if not first(it):
                    eng.wait_ge(l3["og"], it)

        T3 = L1_BASE + 8 + 8 + 16
        L3_Q = {"norm": 0, "turn": 2, "sc0": 4, "t0": 6, "v0": 7, "v1": 8, "t2": 9, "v2": 11, "v3": 12, "post": 12, "back": 15}
        L3_END = {"norm": 0, "turn": 1, "sc0": 2, "t0": 3, "v0": 4, "v1": 5, "t2": 6, "v2": 7, "v3": 8, "post": 8, "back": 11}

        def fox_qk(c, b):
            hh, n = c % 4, (b + 1) * P
            return [(qT3[:, hh, b * P:(b + 1) * P], kT3[:, c, 0:n]),
                    (ident[0:16, c:c + 1].to_broadcast([16, P]), negF[:, 0:n])]

        fox = Heads(l3, 1.0, mask, fox_qk, lambda c, b: v3[:, b, c * HD:(c + 1) * HD], S3, PT3)
        block = ctx.enter_context(nc.Block())

        @block.sync
        def _(sp):
            for b in range(TB):
                sp.dma_start(x_res[:, b, :], a["x"][0, b * P:(b + 1) * P, :]).then_inc(x_in, 16)

            def load(name, p, it=0):
                tiles = PHD[name][1]
                k, q = places(tiles)[p]
                view, kt, c0, step, w = tiles[k]
                nu, n = units(tiles), UNIT[name] + p
                if n >= RAW:
                    sp.wait_ge(w_low, n - RAW + 1 + nu * it)
                c = c0 + it * step
                cols = slice(c, c + w) if isinstance(it, int) else bass.ds(c, w)
                sp.dma_start(wraw[:, n % RAW, :, 0:w], view[:, q:q + KU, cols]).then_inc(w_loaded[n % RAW], 16)

            for name, tiles, runs in PH:
                if runs == 1:
                    for p in range(units(tiles)):
                        load(name, p)
                else:
                    with sp.Fori(0, runs) as it:
                        for p in range(units(tiles)):
                            load(name, p, it)
                if name == LAST:
                    break
            if depth < 3:
                sp.wait_ge(tr_src, 2 * depth)
            for k in range(4):
                sp.wait_ge(x_done, 2 * (4 * (depth - 1) + k + 1))
                for b in range(TB):
                    sp.dma_start(out[0, b * P:(b + 1) * P, k * COLS:(k + 1) * COLS],
                                 x_res[:, b, k * COLS:(k + 1) * COLS]).then_inc(st_out, 16)
            sp.wait_ge(st_out, 16 * 4 * TB)

        @block.gpsimd
        def _(pool):
            own = Own(pool, pool_own)
            pool.dma_start(stage_rows[0:4, 0, :], a["mla_q_norm"].rearrange("o (k p) -> (o k) p", p=P)).then_inc(par_in, 16)
            pool.dma_start(stage_rows[4:8, 0, :], a["mla_kv_norm"].rearrange("o (k p) -> (o k) p", p=P)).then_inc(par_in, 16)
            pool.dma_start(stage_rows[8:72, 0, :], a["ml_conv_w"].rearrange("o w (k p) -> (o w k) p", p=P)).then_inc(par_in, 16)
            pool.dma_start(stage_rows[72:88, 0, :], a["ml_conv_b"].rearrange("o (k p) -> (o k) p", p=P)).then_inc(par_in, 16)
            pool.dma_start(stage_rows[88:104, 0, :], a["ml_head_norm"].rearrange("o (k p) -> (o k) p", p=P)).then_inc(par_in, 16)
            for i, k in enumerate(("a_norm_w_2", "a_out_norm_w_2", "kv_norm_w_2", "b_norm_w_2", "b_out_norm_w_2")):
                v = a[k] if len(a[k].shape) == 2 else a[k].rearrange("(o n) -> o n", o=1)
                pool.dma_start(stage_rows[16 * i:16 * i + 16, 1, :], v.rearrange("o (k p) -> (o k) p", p=P)).then_inc(par_in, 16)
            pool.dma_start(stage_rows[80:81, 1, :], a["k_norm_w_2"].rearrange("(o n) -> o n", o=1)).then_inc(par_in, 16)
            pool.dma_start(stage_rows[81:82, 1, :], a["b_q_norm_w_2"]).then_inc(par_in, 16)
            with nc.allow_non_contiguous_dma(reason="256 positions"):
                pool.dma_start(posi[:], a["positions"].rearrange("o (b p) -> p (o b)", p=P)).then_inc(bias_in, 16)
            pool.dma_start(gbias[:, 0:16], a["ml_gate_b"].to_broadcast([P, 16])).then_inc(bias_in, 16)
            pool.dma_start(gbias[:, 16:32], a["kv_f_bias_2"].rearrange("(o n) -> o n", o=1).to_broadcast([P, 16])).then_inc(bias_in, 16)
            own.mark(nc.gpsimd.memset(ident[:], 0.0))
            own.mark(nc.gpsimd.memset(ones[:], 1.0))
            own.mark(nc.gpsimd.memset(mask[:], 0.0))
            own.mark(nc.gpsimd.memset(lvf, 1.0))
            for i in range(32):
                f = float(np.float32(THETA) ** (-np.float32(2 * i) / np.float32(ROPE)))
                own.mark(nc.gpsimd.memset(invf[:, i:i + 1], f))
            own.sync()
            own.mark(nc.gpsimd.affine_select(out=ident[:], in_=ident[:], compare_op=ALU.not_equal, fill=1.0, base=0,
                                             pattern=[[-1, P]], channel_multiplier=1))
            for part in (slice(0, P), slice(T, 384)):
                own.mark(nc.gpsimd.memset(mask[0:64, part.start + 64:part.stop], NEG))
            for i in range(7):
                h = 64 >> i
                v = lvf[:, i, :].rearrange("p (n r) -> p n r", r=h)
                own.then(nc.gpsimd.affine_select(out=v, in_=v, compare_op=ALU.is_ge, fill=0.0, base=0,
                                                 pattern=[[-2 * h, 64 // h], [0, h]], channel_multiplier=1))
                own.then(nc.gpsimd.affine_select(out=v, in_=v, compare_op=ALU.is_ge, fill=0.0, base=h - 1,
                                                 pattern=[[2 * h, 64 // h], [0, h]], channel_multiplier=-1))
                own.mark(nc.gpsimd.tensor_copy(lvl[:, i, :], lvf[:, i, :]))
            own.sync()
            nc.gpsimd.memset(posf[:, 2:3], 0.0).then_inc(const_ok, 1)
            if depth < 2:
                return
            pool.wait_ge(tr_src, 2)
            own.mark(nc.gpsimd.memset(cin[:, :, 0:PAD], 0.0))
            own.mark(nc.gpsimd.memset(mask[:], 0.0))
            own.mark(nc.gpsimd.memset(vw[:, :, :, MV:VW], 1.0))
            own.sync()
            for part in (slice(0, P), slice(T, 384)):
                nc.gpsimd.affine_select(out=mask[:, part], in_=mask[:, part], compare_op=ALU.is_ge, fill=NEG, base=0,
                                        pattern=[[-1, P]], channel_multiplier=1).then_inc(l1["pads"], 1)
            if True:
                for c in range(H1):
                    pool.wait_ge(l1["ex"], c + 1)
                    for part in (slice(0, P), slice(T, 384)):
                        v = arg[:, c % 2, part]
                        nc.gpsimd.affine_select(out=v, in_=v, compare_op=ALU.is_ge, fill=0.0, base=0,
                                                pattern=[[1, P]], channel_multiplier=-1).then_inc(l1["sel"], 1)

        @block.scalar
        def _(act):
            own = Own(act, act_own)
            turn = Turn()
            act.wait_ge(rope_arg, 2)
            nc.scalar.activation(sin.rearrange("p a b -> p (a b)"), angle[:, 4, :], ACT.Sin).then_inc(rope_ok, 1)
            nc.scalar.activation(cos.rearrange("p a b -> p (a b)"), angle[:, 5, :], ACT.Sin).then_inc(rope_ok, 1)
            nc.scalar.add_instruction(mybir.InstLoadActFuncSet(
                name=nc.get_next_instruction_name(), engine=mybir.EngineType.Activation,
                act_func_set_id=LN_EXP_SET, ins=[], outs=[]))

            def turn_x(dst, weighted):
                for i in range(8):
                    b, q = i // 4, i % 4
                    turn_act(act, turn, dst[0][:, 4 * q:4 * q + 4, b * P:(b + 1) * P], weighted)

            def residual(name, k, it=0):
                tile_done(act, name, k)
                n = 4 * RES[name] + k
                if n >= 2:
                    act.wait_ge(x_done, 2 * (n - 1))
                if k == 0:
                    act.wait_ge(tr_lo, turn.n)
                nc.scalar.activation(tmpT[:, k % 2, :], acc[:, (TILE[name] + k) % 2, 0, :], ACT.Copy).then_inc(out_act, 1)

            def rstd(v, lnv, r):
                own.then(nc.scalar.activation(lnv, v, ACT.Ln))
                return nc.scalar.activation(r, lnv, ACT.Exp, scale=-0.5)

            def evac(name, k, it=0):
                if name in RES:
                    return residual(name, k)
                FREE(act, name, k, it)
                evac_act(act, name, k, DST(name, k, 0, it, act), it)

            def norm_scalars(n):
                act.wait_ge(nrm_v, NRM_AT[n] + 1)
                rstd(nrm[:, :, 0], nrm[:, :, 1], nrm[:, :, 2]).then_inc(nrm_a, 1)

            turn_x(TA, False)

            for p in range(length("l0_in")):
                step(act, high, evac, "l0_in", p)

            def latents():
                landed(act, "l0_in", 1)
                for j in range(2):
                    for b in range(TB):
                        nc.scalar.activation(zw[2 + j][:, b, :], cq[:, b, j * LORA:(j + 1) * LORA], ACT.Square,
                                             accum_out=sm[:, SMALL + 2 * j + b:SMALL + 2 * j + b + 1]).then_inc(l0["lat_sq"], 1)

            def latents2():
                act.wait_ge(l0["lat_v"], 1)
                rstd(sm[:, SMALL + 4:SMALL + 8], sm[:, SMALL + 8:SMALL + 12], sm[:, SMALL + 12:SMALL + 16]).then_inc(l0["lat_r"], 1)

            def latents3():
                act.wait_ge(l0["kr_pe"], 1)
                nc.scalar.activation(krT, ps[:, 0, 0:T], ACT.Copy).then_inc(l0["kr_T"], 1)
                for j in range(2):
                    for b in range(TB):
                        turn_act(act, turn, TBf[0][:, 4 * j:4 * j + 4, b * P:(b + 1) * P], True)

            def l0_side(s, p, at):
                def z_exp():
                    landed(act, "l0_%d" % (s // 2), s % 2)
                    if s > 0:
                        act.wait_ge(l0["z_ok"], s)
                    act.wait_ge(tr_pe, turn.n)
                    nc.scalar.activation(ez, zw[s], ACT.Exp, scale=-1.0).then_inc(l0["z_e"], 1)

                def pair(pr):
                    c2 = 2 * s + pr
                    act.wait_ge(l0["tr"], c2 + 1)
                    if c2 > 0:
                        act.wait_ge(l0["sc"], 2 * c2)
                    nc.scalar.activation(qT0.rearrange("p a t -> p (a t)"), ps[:, 0, :], ACT.Copy).then_inc(l0["trA"], 1)
                    nc.scalar.activation(qrT0, ps[:, 2, 0:T], ACT.Copy).then_inc(l0["trA"], 1)

                def back():
                    for b in range(TB):
                        turn_act(act, turn, og0_dst(s, 0, b), False)

                if p == at[0]:
                    z_exp()
                if p == at[1]:
                    pair(0)
                if p == at[2]:
                    mla.weights(act, s, 0)
                    mla.weights(act, s, 1)
                if p == at[3]:
                    mla.copy(act, s, 0)
                if p == at[4]:
                    mla.copy(act, s, 1)
                if p == at[5]:
                    pair(1)
                if p == at[6]:
                    mla.weights(act, s, 2)
                    mla.weights(act, s, 3)
                if p == at[7]:
                    mla.copy(act, s, 2)
                if p == at[8]:
                    mla.copy(act, s, 3)
                if p == at[10]:
                    back()

            for p in range(length("l0_0")):
                step(act, high, evac, "l0_0", p, 0, ("l0_in", 0))
                if p == 4 + LAG:
                    latents()
                if p == 5 + LAG:
                    latents2()
                if p == 7 + LAG:
                    latents3()
            for s in range(1, 5):
                name = L0_PHASES[s]
                for p in range(length(name)):
                    step(act, high, evac, name, p, 0, (L0_PHASES[s - 1], 0))
                    l0_side(s - 1, p, l0_late(name))
            finish(evac, "l0_out")

            def stream_norm(n, center):
                norm_scalars(n)
                act.wait_ge(nrm_v, NRM_AT[n] + 2)
                nc.scalar.activation(x_res[:, 0, :], x_res[:, 0, :], ACT.Identity, scale=nrm[:, 0, 2:3],
                                     bias=nrm[:, 0, 3:4]).then_inc(final_a, 1)

            def ln_params(layer):
                act.wait_ge(tr_lo, turn.n)
                act.dma_start(lnw, a["ln_w"][layer:layer + 1, :].to_broadcast([P, D])).then_inc(lnp_in, 16)
                act.dma_start(lnb, a["ln_b"][layer:layer + 1, :].to_broadcast([P, D])).then_inc(lnp_in, 16)

            ln_params(0)
            stream_norm(0, True)
            if depth < 2:
                return
            turn_x(TA, False)

            for p in range(length("l1_gates")):
                step(act, high, evac, "l1_gates", p)

            def gates_b():
                act.wait_ge(l1["g_row"], 2)
                own.then(nc.scalar.activation(grow[:, 5, :], grow[:, 5, :], ACT.Exp))
                nc.scalar.activation(grow[:, 5, :], grow[:, 5, :], ACT.Ln, bias=1.0).then_inc(l1["g_e"], 1)

            def gates_c():
                act.wait_ge(l1["g_pe2"], 1)
                act.wait_ge(l1["g_col"], 1)
                nc.scalar.activation(emcol, ps[:, 3, 16:32].rearrange("p (b h) -> p b h", b=TB), ACT.Exp, scale=-1.0).then_inc(l1["g_col"], 1)

            def window_in(s, j):
                n = 2 * s + j
                act.wait_ge(l1["q_pe"], n + 1)
                if n > 0:
                    act.wait_ge(l1["y_ok"], 4 * n)
                act.wait_ge(l1["pads"], 2)
                nc.scalar.activation(cin[:, :, PAD:], ps2(0).rearrange("p (h t) -> p h t", t=T), ACT.Copy).then_inc(l1["q_c"], 1)
                act.wait_ge(l1["y_ok"], 4 * n + 4)
                y = (qT1, kT1)[j].rearrange("p h t -> p (h t)")
                if s > 0:
                    act.wait_ge(l1["z_ok"], 4 * s)
                if n > 0:
                    act.wait_ge(l1["q_r"], n)
                nc.scalar.activation(esc, y, ACT.Exp, scale=-1.0).then_inc(l1["y_e"], 1)

            def weigh(s, c):
                act.wait_ge(l1["arg"], 2 * c + 2)
                nc.scalar.activation(arg[:, c % 2, :], arg[:, c % 2, :], ACT.Exp).then_inc(l1["ex"], 1)

            def cell(s, c):
                act.wait_ge(l1["den"], c + 1)
                for b in range(TB):
                    if c > 0:
                        act.wait_ge(l1["rs"], c)
                    r = sm[:, 16 + 2 * (c % 2) + b:17 + 2 * (c % 2) + b]
                    nc.scalar.activation(hq[:, b, c % 4, :], ps[:, 2 + b, 0:MV], ACT.Copy, scale=r).then_inc(l1["h"], 1)
                act.wait_ge(l1["h"], 2 * c + 2)
                for b in range(TB):
                    nc.scalar.activation(esc[:, b * MV:(b + 1) * MV], hq[:, b, c % 4, :], ACT.Square,
                                         accum_out=sm[:, 20 + b:21 + b]).then_inc(l1["ssq"], 1)
                act.wait_ge(l1["var"], c + 1)
                if s > 0:
                    act.wait_ge(l1["og"], 8 * (s - 1) + 4 * (c % 4 // 2 + 1))
                rstd(sm[:, 24:26], sm[:, 26:28], sm[:, 28 + 2 * (c % 4):30 + 2 * (c % 4)]).then_inc(l1["rs"], 1)

            def gate_exp(s, j):
                landed(act, f"l1_{s}", 6 + j)
                act.wait_ge(l1["rs"], 4 * s + 4)
                if 2 * (2 * s + j) > 0:
                    act.wait_ge(l1["z_ok"], 2 * (2 * s + j))
                o = ow[:, :, j * COLS:(j + 1) * COLS]
                for b in range(TB):
                    if 2 * (2 * s + j) + b > 0:
                        act.wait_ge(l1["z_ok"], 2 * (2 * s + j) + b)
                    nc.scalar.activation(esc[:, 0:COLS], o[:, b, :], ACT.Exp, scale=-1.0).then_inc(l1["ge"], 1)
                    nc.scalar.activation(esc[:, COLS:], zw1[:, b, :], ACT.Exp, scale=-1.0).then_inc(l1["ge"], 1)

            def gated_turn(s, j):
                for b in range(TB):
                    k = 8 * s + 4 * j
                    turn_act(act, turn, TBf[0][:, k:k + 4, b * P:(b + 1) * P], True)


            def l1_side(s, p):
                if s == 0 and p == late("l1_0", 5):
                    gates_b()
                if s == 0 and p == late("l1_0", 8):
                    gates_c()
                if s == 1:
                    l1_rest(0, p)
                for j in range(2):
                    if p == late("l1_0", L1_AT["qk"[j]]):
                        window_in(s, j)
                for h in range(4):
                    if p == late("l1_0", L1_AT["ws"][h]):
                        weigh(s, 4 * s + h)
                    if p == late("l1_0", L1_AT["nm"][h]):
                        cell(s, 4 * s + h)
                if p == late("l1_0", L1_AT["g0"]):
                    gate_exp(s, 0)
                if p == late("l1_0", L1_AT["t0"]):
                    gated_turn(s, 0)

            def l1_rest(s, p):
                if p == 3 + LAG:
                    gate_exp(s, 1)
                if p == 6 + LAG:
                    gated_turn(s, 1)

            for s in range(2):
                for p in range(length("l1_0")):
                    step(act, high, evac, f"l1_{s}", p, 0, (("l1_gates", "l1_0")[s], 0))
                    l1_side(s, p)
            for p in range(length("l1_out")):
                step(act, high, evac, "l1_out", p, 0, ("l1_1", 0))
                l1_rest(1, p)
            finish(evac, "l1_out")
            ln_params(1)
            stream_norm(1, True)
            if depth < 3:
                return

            def rms_scale(n):
                norm_scalars(n)
                act.wait_ge(nrm_a, n + 1)
                nc.scalar.activation(hn[:, 0, :], x_res[:, 0, :], ACT.Copy, scale=nrm[:, 0, 2:3]).then_inc(tr_src_act, 1)

            rms_scale(2)
            turn_x(TA, True)

            def l2_side(g, p, name, at):
                def turned():
                    act.wait_ge(l2["tq"], 1 + 1 * g)
                    nc.scalar.activation(qT2.rearrange("p h t -> p (h t)"), ps2(0), ACT.Copy).then_inc(l2["qT"], 1)
                    act.wait_ge(l2["nf"], 1 + 1 * g)
                    nc.scalar.activation(dT[:, 0, :], dT[:, 0, :], ACT.Exp).then_inc(l2["lf"], 1)
                    act.wait_ge(l2["lf"], 1 + 2 * g)
                    nc.scalar.activation(dT[:, 0, :], dT[:, 0, :], ACT.Ln, bias=1.0).then_inc(l2["lf"], 1)
                    landed(act, "l2", 3, g)
                    nc.scalar.activation(qx.rearrange("p a n -> p (a n)"), gw2.rearrange("p b n -> p (b n)"), ACT.Exp,
                                         scale=-1.0).then_inc(l2["ge"], 1)

                def diag():
                    act.wait_ge(l2["kx"], 1 + 1 * g)
                    nc.scalar.activation(kT2.rearrange("p h t -> p (h t)"), dT[:, 0, :], ACT.Exp).then_inc(l2["kt"], 1)
                    decays(0)
                    decays(1)

                def decays(j):
                    if j > 7:
                        return
                    h = P >> j
                    act.wait_ge(l2["df"], j + 1 + 8 * g)
                    d = dT[:, j % 2, :].rearrange("p (n c r) -> p n c r", c=2, r=h)
                    for c in (0, 1):
                        nc.scalar.activation(d[:, :, c, :], d[:, :, c, :], ACT.Exp, scale=(-1.0, 1.0)[c]).then_inc(l2["ee"], 1)

                def norm():
                    act.wait_ge(l2["pv"], 1 + 1 * g)
                    for b in range(TB):
                        nc.scalar.activation(dT[:, 0, b * COLS:(b + 1) * COLS], ps[:, b, :], ACT.Square).then_inc(l2["sq"], 1)
                    act.wait_ge(l2["v"], 1 + 1 * g)
                    nc.scalar.activation(sm[:, 40:48], sm[:, 32:40], ACT.Ln).then_inc(l2["rs"], 1)
                    act.wait_ge(l2["rs"], 1 + 2 * g)
                    nc.scalar.activation(sm[:, 48:56], sm[:, 40:48], ACT.Exp, scale=-0.5).then_inc(l2["rs"], 1)

                def back():
                    for b in range(TB):
                        act.wait_ge(l2["tmp"], b + 1 + TB * g)
                        nc.scalar.activation(heads_of(TBf[0], g, b), tmpT[:, b, :].rearrange("p (k t) -> p k t", t=P), ACT.Copy).then_inc(l2["hi"], 1)

                if p == late(name, at["turn"]):
                    turned()
                if p == late(name, at["diag"]):
                    diag()
                for j in range(8):
                    if p == late(name, at["level"][j]):
                        decays(j + 2)
                if p == late(name, at["pv"]):
                    norm()
                if p == late(name, at["back"]):
                    back()

            for p in range(length("l2")):
                step(act, high, evac, "l2", p)
            with act.Fori(1, 4) as it:
                for p in range(length("l2")):
                    step(act, high, evac, "l2", p, it, ("l2", it - 1))
                    l2_side(it - 1, p, "l2", L2_AT)
            for p in range(length("l2_out")):
                step(act, high, evac, "l2_out", p, 0, ("l2", 3))
                l2_side(3, p, "l2_out", L2_END)
            finish(evac, "l2_out")
            if depth < 4:
                return
            rms_scale(3)
            turn_x(TA, True)
            turn_x(TBf, True)

            def forget():
                act.wait_ge(l3["f_row"], 1)
                nc.scalar.activation(frow[:, 1, :], frow[:, 1, :], ACT.Exp).then_inc(l3["f_e"], 1)
                act.wait_ge(l3["f_e"], 1)
                nc.scalar.activation(frow[:, 1, :], frow[:, 1, :], ACT.Ln, bias=1.0).then_inc(l3["f_e"], 1)

            def squares(pre, src, g):
                for b in range(TB):
                    for h in range(4):
                        n = 8 * g + 4 * b + h
                        if b or h:
                            act.wait_ge(l3[pre + "sq"], n)
                        nc.scalar.activation(sqj, src[:, b, h * HD:(h + 1) * HD], ACT.Square,
                                             accum_out=sm[:, 32 + 4 * b + h:33 + 4 * b + h]).then_inc(l3[pre + "sq"], 1)

            def inverse_root(v, rs, g):
                act.wait_ge(v, g + 1)
                nc.scalar.activation(sm[:, 40:48], sm[:, 32:40], ACT.Ln).then_inc(rs, 1)
                act.wait_ge(rs, 2 * g + 1)
                nc.scalar.activation(sm[:, 48:56], sm[:, 40:48], ACT.Exp, scale=-0.5).then_inc(rs, 1)

            def kv_side(g, p):
                def norm():
                    landed(act, "l3_kv", 0, g)
                    squares("k", qw3, g)
                    inverse_root(l3["kv_"], l3["krs"], g)

                def keys():
                    act.wait_ge(l3["kt"], g + 1)
                    act.wait_ge(l3["f_ok"], 2)
                    nc.scalar.activation(kT3[:, group(0, g), :].rearrange("p h t -> p (h t)"), ps2(0), ACT.Copy,
                                         scale=colB[:, 80:81]).then_inc(l3["kT"], 1)
                if p == late("l3_kv", 0):
                    norm()
                if p == late("l3_kv", 5):
                    keys()

            for p in range(length("l3_f")):
                step(act, high, evac, "l3_f", p)
            for p in range(length("l3_kv")):
                step(act, high, evac, "l3_kv", p, 0, ("l3_f", 0))
                if p == 1 + LAG:
                    forget()
            with act.Fori(1, 4) as it:
                for p in range(length("l3_kv")):
                    step(act, high, evac, "l3_kv", p, it, ("l3_kv", it - 1))
                    kv_side(it - 1, p)

            def q_side(g, p, name, at):
                c = 4 * g

                def norm():
                    landed(act, "l3_q", 0, g)
                    squares("q", qw3, g)
                    inverse_root(l3["qv"], l3["qrs"], g)

                def turned():
                    act.wait_ge(l3["qt"], g + 1)
                    nc.scalar.activation(qT3.rearrange("p h t -> p (h t)"), ps2(0), ACT.Copy, scale=sm[:, 56:57]).then_inc(l3["qT"], 1)

                def post():
                    act.wait_ge(l3["o"], 2 * (c + 4))
                    act.wait_ge(l3["qn"], 2 * g + 2)
                    for b in range(TB):
                        for h in range(4):
                            if b or h:
                                act.wait_ge(l3["sq"], 8 * g + 4 * b + h)
                            nc.scalar.activation(sqj, o3[:, b, h * HD:(h + 1) * HD], ACT.Square,
                                                 accum_out=sm[:, 32 + 4 * b + h:33 + 4 * b + h]).then_inc(l3["sq"], 1)
                    inverse_root(l3["v"], l3["rs"], g)

                def gate():
                    landed(act, "l3_q", 1, g)
                    for b in range(TB):
                        if b:
                            act.wait_ge(l3["gs"], 2 * g + b)
                        act.wait_ge(l3["ptc"], c + 2)
                        nc.scalar.activation(tmpT[:, 0, :], gw3[:, b, :], ACT.Exp, scale=-1.0).then_inc(l3["ge"], 1)

                def back():
                    for b in range(TB):
                        act.wait_ge(l3["tmp"], 2 * g + b + 1)
                        nc.scalar.activation(heads_of(TA[0], g, b), tmpT[:, b, :].rearrange("p (k t) -> p k t", t=P), ACT.Copy).then_inc(l3["hi"], 1)

                if p == late(name, at["norm"]):
                    norm()
                if p == late(name, at["turn"]):
                    turned()
                if p == late(name, at["sc0"]):
                    fox.weights(act, g, 0)
                    fox.weights(act, g, 1)
                if p == late(name, at["t0"]):
                    fox.copy(act, g, 0)
                if p == late(name, at["v0"]):
                    fox.copy(act, g, 1)
                if p == late(name, at["v1"]):
                    gate()
                    fox.weights(act, g, 2)
                    fox.weights(act, g, 3)
                if p == late(name, at["t2"]):
                    fox.copy(act, g, 2)
                if p == late(name, at["v2"]):
                    fox.copy(act, g, 3)
                if p == late(name, at["post"]):
                    post()
                if p == late(name, at["back"]):
                    back()

            for p in range(length("l3_q")):
                step(act, high, evac, "l3_q", p, 0, ("l3_kv", 3))
                kv_side(3, p)
            with act.Fori(1, 4) as it:
                for p in range(length("l3_q")):
                    step(act, high, evac, "l3_q", p, it, ("l3_q", it - 1))
                    q_side(it - 1, p, "l3_q", L3_Q)
            for p in range(length("l3_out")):
                step(act, high, evac, "l3_out", p, 0, ("l3_q", 3))
                q_side(3, p, "l3_out", L3_END)
            finish(evac, "l3_out")

        @block.vector
        def _(dve):
            own = Own(dve, dve_own)
            turn = Turn()
            dve.wait_ge(const_ok, 1)
            dve.wait_ge(bias_in, 48)
            dve.wait_ge(col_pe, 1)
            nc.vector.tensor_copy(colA[:], ps[:, 0, 0:NA_ROWS]).then_inc(col_ok, 1)
            nc.vector.tensor_copy(colB[:], ps[:, 0, P:P + NB_ROWS]).then_inc(col_ok, 1)
            dve.wait_ge(col_ok, 2)
            own.then(nc.vector.tensor_copy(posf[:, 0:TB], posi[:]))
            two_pi, magic = 2 * np.pi, float(1.5 * 2 ** 23)
            c1 = 6.28125
            c2 = float(np.float32(np.round((two_pi - c1) * 2 ** 22) / 2 ** 22))
            c3 = float(np.float32(two_pi - c1 - c2))
            for b in range(TB):
                own.mark(nc.vector.tensor_scalar(angle[:, 0, 32 * b:32 * b + 32], invf, posf[:, b:b + 1], None, ALU.mult))
            own.sync()
            for j, quarter in ((0, 0.0), (1, 0.25)):
                k, r = angle[:, 1, :], angle[:, 4 + j, :]
                own.then(nc.vector.tensor_scalar(k, angle[:, 0, :], float(1 / two_pi), quarter, ALU.mult, ALU.add))
                own.then(nc.vector.tensor_scalar(k, k, magic, None, ALU.add))
                own.then(nc.vector.tensor_scalar(k, k, -magic, None, ALU.add))
                own.then(nc.vector.scalar_tensor_tensor(r, k, -c1, angle[:, 0, :], ALU.mult, ALU.add))
                own.then(nc.vector.scalar_tensor_tensor(r, k, -c2, r, ALU.mult, ALU.add))
                own.then(nc.vector.scalar_tensor_tensor(r, k, -c3, r, ALU.mult, ALU.add))
                if j:
                    own.then(nc.vector.tensor_scalar(r, r, float(np.pi / 2), None, ALU.add))
                nc.vector.tensor_scalar(r, r, 3.1415925, -3.1415925, ALU.min, ALU.max).then_inc(rope_arg, 1)

            def turn_x(dst, col=None):
                for i in range(8):
                    b, q = i // 4, i % 4
                    turn_dve(dve, turn, dst[0][:, 4 * q:4 * q + 4, b * P:(b + 1) * P], dst[1][:, 4 * q:4 * q + 4, b * P:(b + 1) * P],
                             None if col is None else col[:, 4 * q:4 * q + 4])

            def residual(name, k, it=0):
                tile_done(dve, name, k)
                n, al = 4 * RES[name] + k, (ALPHA if RES[name] < 2 else 1.0)
                c = slice(k * COLS, (k + 1) * COLS)
                nc.vector.scalar_tensor_tensor(x_res[:, 1, c], x_res[:, 1, c], al, acc[:, (TILE[name] + k) % 2, 1, :],
                                               ALU.mult, ALU.add).then_inc(out_dve, 1)
                dve.wait_ge(out_act, TILE[name] + k + 1)
                own.mark(nc.vector.scalar_tensor_tensor(x_res[:, 0, c], x_res[:, 0, c], al, tmpT[:, k % 2, :], ALU.mult, ALU.add))
                own.sync()
                dve.wait_ge(out_dve, TILE[name] + k + 1)
                for b in range(TB):
                    nc.vector.bn_stats(bstat[:, b, k, :], x_res[:, b, c]).then_inc(x_done, 1)

            def evac(name, k, it=0):
                if name in RES:
                    return residual(name, k)
                FREE(dve, name, k, it)
                evac_dve(dve, name, k, DST(name, k, 1, it, dve), it)

            def scalars(n, center):
                own.sync()
                dve.wait_ge(x_done, 8 * min(n + 1, 3 if n == 3 else 2))
                for b in range(TB):
                    own.mark(nc.vector.bn_aggr(mv[:, b, :], bstat[:, b, :, :].rearrange("p k s -> p (k s)")))
                own.sync()
                if center:
                    nc.vector.tensor_scalar(nrm[:, :, 0], mv[:, :, 1], EPS, None, ALU.add).then_inc(nrm_v, 1)
                else:
                    own.then(nc.vector.tensor_tensor(nrm[:, :, 3], mv[:, :, 0], mv[:, :, 0], ALU.mult))
                    nc.vector.scalar_tensor_tensor(nrm[:, :, 0], mv[:, :, 1], EPS, nrm[:, :, 3], ALU.add, ALU.add).then_inc(nrm_v, 1)
                dve.wait_ge(nrm_a, n + 1)
                if center:
                    nc.vector.scalar_tensor_tensor(nrm[:, :, 3], mv[:, :, 0], -1.0, nrm[:, :, 2], ALU.mult, ALU.mult).then_inc(nrm_v, 1)
                    dve.wait_ge(nrm_v, NRM_AT[n] + 2)

            turn_x(TA)

            for p in range(length("l0_in")):
                step(dve, low, evac, "l0_in", p)

            def rotate(dst, x1, x2, n, heads):
                t = [rt[:, i, 0:TB * heads * 32].rearrange("p (b h f) -> p b h f", b=TB, f=32) for i in range(4)]
                cs = cos.unsqueeze(2).to_broadcast([P, TB, heads, 32])
                sn = sin.unsqueeze(2).to_broadcast([P, TB, heads, 32])
                for i, (x, y) in enumerate(((x1, cs), (x2, sn), (x1, sn), (x2, cs))):
                    own.mark(nc.vector.tensor_tensor(t[i], x, y, ALU.mult))
                own.sync()
                nc.vector.tensor_tensor(dst[..., 0:32], t[0], t[1], ALU.subtract).then_inc(*n)
                nc.vector.tensor_tensor(dst[..., 32:64], t[2], t[3], ALU.add).then_inc(*n)

            def latents():
                landed(dve, "l0_in", 2)
                dve.wait_ge(rope_ok, 2)
                k4 = krw.unsqueeze(2)
                rotate(krd[:, :, 0:1, :], k4[..., 0:32], k4[..., 32:64], (l0["kr_ok"], 1), 1)
                dve.wait_ge(l0["kr_ok"], 2)
                nc.vector.tensor_copy(krd[:, :, 1, :], krd[:, :, 0, :]).then_inc(l0["kr_ok"], 1)
                dve.wait_ge(l0["lat_sq"], 4)
                nc.vector.tensor_scalar(sm[:, SMALL + 4:SMALL + 8], sm[:, SMALL:SMALL + 4], 1.0 / LORA, EPS, ALU.mult, ALU.add).then_inc(l0["lat_v"], 1)

            def latents2():
                dve.wait_ge(l0["lat_r"], 1)
                for j in range(2):
                    for b in range(TB):
                        v = cq[:, b, j * LORA:(j + 1) * LORA]
                        i = SMALL + 12 + 2 * j + b
                        nc.vector.tensor_scalar(v, v, sm[:, i:i + 1], None, ALU.mult).then_inc(l0["lat_ok"], 1)

            def latents3():
                for j in range(2):
                    for b in range(TB):
                        d = (slice(4 * j, 4 * j + 4), slice(b * P, (b + 1) * P))
                        turn_dve(dve, turn, TBf[0][:, d[0], d[1]], TBf[1][:, d[0], d[1]], colA[:, 4 * j:4 * j + 4])

            def l0_side(s, p, at):
                name = f"l0_{s}"

                def rope(pr):
                    c2 = 2 * s + pr
                    landed(dve, name, l0_tile(s, pr, 0))
                    if c2 > 0:
                        dve.wait_ge(l0["tr"], c2)
                    q4 = qw[pr].rearrange("p b (h d) -> p b h d", d=QH)
                    rotate(qr, q4[..., NOPE:NOPE + 32], q4[..., NOPE + 32:QH], (l0["rope"], 1), 2)

                def silu():
                    dve.wait_ge(l0["z_e"], s + 1)
                    own.then(nc.vector.tensor_scalar(ez, ez, 1.0, None, ALU.add))
                    own.then(nc.vector.reciprocal(ez, ez))
                    nc.vector.tensor_tensor(zw[s], zw[s], ez, ALU.mult).then_inc(l0["z_ok"], 1)

                def pair(pr):
                    c2 = 2 * s + pr
                    dve.wait_ge(l0["tr"], c2 + 1)
                    if c2 > 0:
                        dve.wait_ge(l0["sc"], 2 * c2)
                    nc.vector.tensor_copy(kT0.rearrange("p a t -> p (a t)"), ps[:, 1, :]).then_inc(l0["trV"], 1)

                def out_(hh):
                    r = mla.inverse(dve, own, s, hh)
                    dve.wait_ge(l0["z_ok"], s + 1)
                    for b in range(TB):
                        h = slice(hh * VH, hh * VH + VH)
                        nc.vector.scalar_tensor_tensor(og0[:, b, h], ps[:, 3, b * P:(b + 1) * P], r[:, b:b + 1],
                                                       zw[s][:, b, h], ALU.mult, ALU.mult).then_inc(l0["o"], 1)

                def back():
                    for b in range(TB):
                        turn_dve(dve, turn, og0_dst(s, 0, b), og0_dst(s, 1, b))

                if p == at[0]:
                    rope(0)
                    silu()
                if p == at[1]:
                    pair(0)
                if p == at[2]:
                    mla.mask_max(dve, own, s, 0)
                    mla.mask_max(dve, own, s, 1)
                    rope(1)
                if p == at[4]:
                    out_(0)
                if p == at[5]:
                    out_(1)
                    pair(1)
                if p == at[6]:
                    mla.mask_max(dve, own, s, 2)
                    mla.mask_max(dve, own, s, 3)
                if p == at[8]:
                    out_(2)
                if p == at[9]:
                    out_(3)
                if p == at[10]:
                    back()

            for p in range(length("l0_0")):
                step(dve, low, evac, "l0_0", p, 0, ("l0_in", 0))
                if p == 4 + LAG:
                    latents()
                if p == 5 + LAG:
                    latents2()
                if p == 7 + LAG:
                    latents3()
            for s in range(1, 5):
                name = L0_PHASES[s]
                for p in range(length(name)):
                    step(dve, low, evac, name, p, 0, (L0_PHASES[s - 1], 0))
                    l0_side(s - 1, p, l0_late(name))
            finish(evac, "l0_out")

            def stream_norm(n):
                scalars(n, True)
                own.mark(nc.vector.tensor_scalar(x_res[:, 1, :], x_res[:, 1, :], nrm[:, 1, 2:3], nrm[:, 1, 3:4], ALU.mult, ALU.add))
                own.sync()
                dve.wait_ge(lnp_in, 32 * (LN[n] + 1))
                for b in (1, 0):
                    if b == 0:
                        dve.wait_ge(final_a, LN[n] + 1)
                    own.then(nc.vector.tensor_tensor(x_res[:, b, :], x_res[:, b, :], lnw, ALU.mult))
                    nc.vector.tensor_tensor(x_res[:, b, :], x_res[:, b, :], lnb, ALU.add).then_inc(tr_src, 1)

            stream_norm(0)
            if depth < 2:
                return
            turn_x(TA)

            for p in range(length("l1_gates")):
                step(dve, low, evac, "l1_gates", p)

            def gates_a():
                landed(dve, "l1_gates", 0)
                for b in range(TB):
                    nc.vector.tensor_tensor(gt[:, b, :], gt[:, b, :], gbias[:, 0:16], ALU.add).then_inc(l1["g_in"], 1)

            def gates_b():
                dve.wait_ge(l1["g_pe"], 1)
                f = ps[0:8, 2, T:2 * T]
                own.then(nc.vector.tensor_copy(grow[:, 1, :], f))
                own.then(nc.vector.tensor_scalar(grow[:, 5, :], grow[:, 1, :], -1.0, None, ALU.mult))
                nc.vector.tensor_tensor(grow[:, 5, :], grow[:, 5, :], grow[:, 1, :], ALU.min).then_inc(l1["g_row"], 1)
                nc.vector.tensor_copy(grow[:, 0, :], ps[0:8, 2, 0:T]).then_inc(l1["g_row"], 1)
                own.then(nc.vector.tensor_scalar(grow[:, 1, :], grow[:, 1, :], 0.0, None, ALU.min))
                dve.wait_ge(l1["g_e"], 1)
                dve.wait_ge(l1["g_row"], 2)
                own.then(nc.vector.tensor_tensor(grow[:, 1, :], grow[:, 1, :], grow[:, 5, :], ALU.subtract))
                own.then(nc.vector.tensor_tensor_scan(grow[:, 2, :], ones[0:8, 0:T], grow[:, 1, :], 0.0, ALU.mult, ALU.add))
                own.then(nc.vector.tensor_tensor(grow[:, 3, :], grow[:, 0, :], grow[:, 2, :], ALU.subtract))
                own.then(nc.vector.tensor_tensor_scan(grow[:, 4, :], grow[:, 3, :], grow[:, 3, :], 0.0, ALU.max, ALU.max))
                nc.vector.tensor_scalar(negM, grow[:, 4, :], -1.0, None, ALU.mult).then_inc(l1["g_m"], 1)
                nc.vector.tensor_tensor(grow[:, 5, :], grow[:, 2, :], grow[:, 4, :], ALU.add).then_inc(l1["g_m"], 1)

            def gates_c():
                dve.wait_ge(l1["g_pe2"], 1)
                nc.vector.tensor_copy(acol, ps[:, 3, 0:16].rearrange("p (b h) -> p b h", b=TB)).then_inc(l1["g_col"], 1)

            def conv(s, j):
                n = 2 * s + j
                dve.wait_ge(l1["q_c"], n + 1)
                if s > 0:
                    dve.wait_ge(l1["sc"], 4 * s)
                y = (qT1, kT1)[j]
                for h in range(4):
                    ch = 8 * j + 4 * s + h
                    cw = lambda w: colA[:, 8 + 16 * w + ch:9 + 16 * w + ch]
                    own.then(nc.vector.tensor_scalar(y[:, h, :], cin[:, h, PAD - 3:PAD - 3 + T], cw(0),
                                                     colA[:, 72 + ch:73 + ch], ALU.mult, ALU.add))
                    for w in (1, 2):
                        own.then(nc.vector.scalar_tensor_tensor(y[:, h, :], cin[:, h, PAD - 3 + w:PAD - 3 + w + T], cw(w),
                                                                y[:, h, :], ALU.mult, ALU.add))
                    nc.vector.scalar_tensor_tensor(y[:, h, :], cin[:, h, PAD:PAD + T], cw(3), y[:, h, :],
                                                   ALU.mult, ALU.add).then_inc(l1["y_ok"], 1)
                dve.wait_ge(l1["y_e"], n + 1)
                own.then(nc.vector.tensor_scalar(esc, esc, 1.0, None, ALU.add))
                own.then(nc.vector.reciprocal(esc, esc))
                yf = y.rearrange("p h t -> p (h t)")
                nc.vector.scalar_tensor_tensor(yf, yf, 1.0 if j == 0 else MQK ** -0.5, esc, ALU.mult,
                                               ALU.mult).then_inc(l1["q_r"], 1)

            def weigh(s, c):
                dve.wait_ge(l1["sc"], c + 1)
                dve.wait_ge(l1["g_col"], 2)
                if c >= 2:
                    dve.wait_ge(l1["st"], c - 1)
                g = arg[:, c % 2, :]
                for b in range(TB):
                    n = slice(0, T) if b == 0 else slice(T, 384)
                    nc.vector.tensor_scalar(g[:, n], ps[:, 0, b * P:T], acol[:, b, c:c + 1], 0.0, ALU.add,
                                            ALU.min).then_inc(l1["arg"], 1)
                dve.wait_ge(l1["sel"], 2 * c + 2)
                if c > 0:
                    dve.wait_ge(l1["nm"], c)
                nc.vector.tensor_tensor(wst, ps[:, 1, 0:384], g, ALU.mult).then_inc(l1["st"], 1)

            def cell(s, c):
                dve.wait_ge(l1["nm"], c + 1)
                d = sm[:, 16 + 2 * (c % 2):18 + 2 * (c % 2)]
                for b in range(TB):
                    own.mark(nc.vector.tensor_scalar(d[:, b:b + 1], ps[:, 2 + b, MV:MV + 1], -1.0, emcol[:, b, c:c + 1],
                                                     ALU.mult, ALU.max))
                own.sync()
                own.then(nc.vector.tensor_tensor(d, d, ps[:, 2:4, MV], ALU.max))
                nc.vector.reciprocal(d, d).then_inc(l1["den"], 1)
                dve.wait_ge(l1["ssq"], 2 * c + 2)
                if c > 0:
                    dve.wait_ge(l1["rs"], c)
                nc.vector.tensor_scalar(sm[:, 24:26], sm[:, 20:22], 1.0 / MV, EPS, ALU.mult, ALU.add).then_inc(l1["var"], 1)

            def gate(s, j):
                for b in range(TB):
                    n = 2 * (2 * s + j) + b
                    dve.wait_ge(l1["ge"], 2 * n + 2)
                    eo, e2 = esc[:, 0:COLS], esc[:, COLS:]
                    o = ow[:, b, j * COLS:(j + 1) * COLS]
                    own.then(nc.vector.tensor_scalar(eo, eo, 1.0, None, ALU.add))
                    own.then(nc.vector.scalar_tensor_tensor(e2, e2, 1.0, eo, ALU.add, ALU.mult))
                    own.then(nc.vector.reciprocal(e2, e2))
                    nc.vector.tensor_tensor(o, zw1[:, b, :], e2, ALU.mult).then_inc(l1["z_ok"], 1)
                    dve.wait_ge(l1["z_ok"], n + 1)
                    dve.wait_ge(l1["rs"], 4 * s + 2 * j + 2)
                    for h in (2 * j, 2 * j + 1):
                        oh = ow[:, b, h * MV:(h + 1) * MV]
                        nc.vector.scalar_tensor_tensor(oh, hq[:, b, h, :], sm[:, 28 + 2 * h + b:29 + 2 * h + b], oh,
                                                       ALU.mult, ALU.mult).then_inc(l1["og"], 1)

            def gated_turn(s, j):
                for b in range(TB):
                    k = 8 * s + 4 * j
                    d = (slice(k, k + 4), slice(b * P, (b + 1) * P))
                    turn_dve(dve, turn, TBf[0][:, d[0], d[1]], TBf[1][:, d[0], d[1]], colA[:, 88 + k:92 + k])


            def l1_side(s, p):
                if s == 0 and p == 4:
                    gates_a()
                if s == 0 and p == late("l1_0", 5):
                    gates_b()
                if s == 0 and p == late("l1_0", 8):
                    gates_c()
                if s == 1:
                    l1_rest(0, p)
                for j in range(2):
                    if p == late("l1_0", L1_AT["qk"[j]]):
                        conv(s, j)
                for h in range(4):
                    if p == late("l1_0", L1_AT["ws"][h]):
                        weigh(s, 4 * s + h)
                    if p == late("l1_0", L1_AT["nm"][h]):
                        cell(s, 4 * s + h)
                if p == late("l1_0", L1_AT["g0"]):
                    gate(s, 0)
                if p == late("l1_0", L1_AT["t0"]):
                    gated_turn(s, 0)

            def l1_rest(s, p):
                if p == 3 + LAG:
                    gate(s, 1)
                if p == 6 + LAG:
                    gated_turn(s, 1)

            for s in range(2):
                for p in range(length("l1_0")):
                    step(dve, low, evac, f"l1_{s}", p, 0, (("l1_gates", "l1_0")[s], 0))
                    l1_side(s, p)
            for p in range(length("l1_out")):
                step(dve, low, evac, "l1_out", p, 0, ("l1_1", 0))
                l1_rest(1, p)
            finish(evac, "l1_out")
            stream_norm(1)
            if depth < 3:
                return

            def rms_scale(n):
                scalars(n, False)
                dve.wait_ge(nrm_a, n + 1)
                nc.vector.tensor_scalar(hn[:, 1, :], x_res[:, 1, :], nrm[:, 1, 2:3], None, ALU.mult).then_inc(tr_src, 1)

            dve.wait_ge(tr_src, 4)
            for b in range(TB):
                for k in range(4):
                    own.mark(nc.vector.bn_stats(bstat[:, b, k, :], x_res[:, b, k * COLS:(k + 1) * COLS]))
            rms_scale(2)
            turn_x(TA, colB[:, 0:16])

            def l2_side(g, p, name, at):
                flat = lambda v: v.rearrange("p h t -> p (h t)")

                def turned():
                    f = ps2(2)
                    dve.wait_ge(l2["tf"], 1 + 1 * g)
                    own.then(nc.vector.tensor_scalar(dT[:, 0, :], f, -1.0, None, ALU.mult))
                    nc.vector.tensor_tensor(dT[:, 0, :], dT[:, 0, :], f, ALU.min).then_inc(l2["nf"], 1)
                    own.mark(nc.vector.tensor_scalar(dT[:, 1, :], f, 0.0, None, ALU.min))
                    own.sync()
                    dve.wait_ge(l2["lf"], 2 + 2 * g)
                    own.then(nc.vector.tensor_tensor(flat(kT2), dT[:, 1, :], dT[:, 0, :], ALU.subtract))
                    own.mark(nc.vector.tensor_tensor(dT[:, 0, :], flat(kT2), f, ALU.subtract))
                    for h in range(4):
                        own.mark(nc.vector.tensor_tensor_scan(bT2[:, h, :], ones[:], kT2[:, h, :], 0.0, ALU.mult, ALU.add))
                    own.sync()
                    dve.wait_ge(l2["ge"], 1 + 1 * g)
                    e, gw = qx.rearrange("p a n -> p (a n)"), gw2.rearrange("p b n -> p (b n)")
                    nc.vector.tensor_scalar(e, e, 1.0, None, ALU.add).then_inc(l2["kx"], 1)
                    dve.wait_ge(l2["kx"], 1 + 1 * g)
                    own.then(nc.vector.reciprocal(e, e))
                    nc.vector.tensor_tensor(gw, gw, e, ALU.mult).then_inc(l2["gs"], 1)

                def distance(j):
                    if j > 7:
                        return
                    h = P >> j
                    if j < 2:
                        dve.wait_ge(l2["kt"], 1 + 1 * g)
                    else:
                        dve.wait_ge(l2["lv"], j - 1 + 8 * g)
                    b = flat(bT2).rearrange("p (n r) -> p n r", r=2 * h)
                    nc.vector.tensor_tensor(dT[:, j % 2, :].rearrange("p (n r) -> p n r", r=2 * h), b,
                                            b[:, :, h - 1:h].to_broadcast([P, G4 // (2 * h), 2 * h]),
                                            ALU.subtract).then_inc(l2["df"], 1)

                def scale(j):
                    if j > 7:
                        return
                    h = P >> j
                    dve.wait_ge(l2["ee"], 2 * j + 2 + 16 * g)
                    if j == 0:
                        dve.wait_ge(l2["qT"], 1 + 1 * g)
                    if j < 2:
                        dve.wait_ge(l2["gs"], 1 + 1 * g)
                    half = lambda v, c: v.rearrange("p (n c r) -> p n c r", c=2, r=h)[:, :, c, :]
                    nc.vector.tensor_tensor(half(dT[:, j % 2, :], 0), half(dT[:, j % 2, :], 0), half(flat(kT2), 0),
                                            ALU.mult).then_inc(l2["op"], 1)
                    nc.vector.tensor_tensor(qx[:, j % 2, :].rearrange("p (n r) -> p n r", r=h), half(dT[:, j % 2, :], 1),
                                            half(flat(qT2), 1), ALU.mult).then_inc(l2["op"], 1)

                def diag():
                    distance(0)
                    distance(1)
                    dve.wait_ge(l2["dg"], 1 + 1 * g)
                    nc.vector.tensor_tensor(aT, ps2(0).rearrange("p (n t) -> p n t", t=P),
                                            ident[:].unsqueeze(1).to_broadcast([P, 8, P]), ALU.mult).then_inc(l2["at"], 1)
                    scale(0)

                def level(j):
                    h = P >> j
                    scale(j + 1)
                    dve.wait_ge(l2["lv"], j + 1 + 8 * g)
                    if j == 0:
                        nc.vector.tensor_copy(a01.rearrange("p h t -> p (h t)"), ps[:, 2, :]).then_inc(l2["sel"], 1)
                    else:
                        dve.wait_ge(l2["at"], 1 + 1 * g)
                        dve.wait_ge(l2["sel"], j + 8 * g)
                        nc.vector.memset(sm[:, 57:58], 0.0)
                        o = aT.rearrange("p n (m c r) -> p n m c r", c=2, r=h)[:, :, :, 1, :]
                        m = lvl[:, j - 1, :].rearrange("p (m r) -> p m r", r=h).unsqueeze(1).to_broadcast([P, 8, 64 // h, h])
                        nc.vector.copy_predicated(o, m, ps[:, 2 + j % 2, :].rearrange("p (n m r) -> p n m r", n=8, r=h)).then_inc(l2["sel"], 1)
                    distance(j + 2)

                def norm():
                    dve.wait_ge(l2["sq"], 2 + 2 * g)
                    nc.vector.tensor_reduce(sm[:, 32:40], dT[:, 0, :].rearrange("p (n d) -> p n d", d=HD), AX, ALU.add).then_inc(l2["ss"], 1)
                    dve.wait_ge(l2["ss"], 1 + 1 * g)
                    nc.vector.tensor_scalar(sm[:, 32:40], sm[:, 32:40], 1.0 / HD, EPS, ALU.mult, ALU.add).then_inc(l2["v"], 1)
                    dve.wait_ge(l2["rs"], 2 + 2 * g)
                    for b in range(TB):
                        nc.vector.tensor_tensor(dT[:, 1, b * COLS:(b + 1) * COLS].rearrange("p (h d) -> p h d", d=HD),
                                                ps[:, b, :].rearrange("p (h d) -> p h d", d=HD),
                                                sm[:, 48 + 4 * b:52 + 4 * b].unsqueeze(2).to_broadcast([P, 4, HD]),
                                                ALU.mult).then_inc(l2["on"], 1)
                    dve.wait_ge(l2["on"], 2 + 2 * g)
                    gw = gw2.rearrange("p b n -> p (b n)")
                    nc.vector.tensor_tensor(gw, gw, dT[:, 1, :], ALU.mult).then_inc(l2["og"], 1)

                def back():
                    for b in range(TB):
                        t = tmpT[:, b, :].rearrange("p (k t) -> p k t", t=P)
                        dve.wait_ge(l2["ogp"], b + 1 + TB * g)
                        nc.vector.tensor_tensor(t, ps[:, 2 + b, :].rearrange("p (k t) -> p k t", t=P),
                                                colB[:, group(16, g)].unsqueeze(2).to_broadcast([P, 4, P]), ALU.mult).then_inc(l2["tmp"], 1)
                    for b in range(TB):
                        t = tmpT[:, b, :].rearrange("p (k t) -> p k t", t=P)
                        dve.wait_ge(l2["hi"], b + 1 + TB * g)
                        nc.vector.tensor_tensor(heads_of(TBf[1], g, b), t, heads_of(TBf[0], g, b).bitcast(F32),
                                                ALU.subtract).then_inc(l2["lo"], 1)

                if p == late(name, at["turn"]):
                    turned()
                if p == late(name, at["diag"]):
                    diag()
                for j in range(8):
                    if p == late(name, at["level"][j]):
                        level(j)
                if p == late(name, at["pv"]):
                    norm()
                if p == late(name, at["back"]):
                    back()

            for p in range(length("l2")):
                step(dve, low, evac, "l2", p)
            with dve.Fori(1, 4) as it:
                own.enter(it, L2_OWN)
                for p in range(length("l2")):
                    step(dve, low, evac, "l2", p, it, ("l2", it - 1))
                    l2_side(it - 1, p, "l2", L2_AT)
            own.leave(3)
            for p in range(length("l2_out")):
                step(dve, low, evac, "l2_out", p, 0, ("l2", 3))
                l2_side(3, p, "l2_out", L2_END)
            finish(evac, "l2_out")
            if depth < 4:
                return
            rms_scale(3)
            turn_x(TA, colB[:, 32:48])
            turn_x(TBf, colB[:, 48:64])
            own.mark(nc.vector.tensor_scalar(sm[:, 56:57], colB[:, 81:82], HD ** -0.5, None, ALU.mult))

            dve.wait_ge(l1["pads"], 2)

            def forget_in():
                landed(dve, "l3_f", 0)
                for b in range(TB):
                    nc.vector.tensor_tensor(ft[:, b, :], ft[:, b, :], gbias[:, 16:32], ALU.add).then_inc(l3["f_in"], 1)

            def forget():
                dve.wait_ge(l3["f_pe"], 1)
                own.then(nc.vector.tensor_copy(frow[:, 0, :], ps[0:16, 3, 0:T]))
                own.then(nc.vector.tensor_scalar(frow[:, 1, :], frow[:, 0, :], -1.0, None, ALU.mult))
                nc.vector.tensor_tensor(frow[:, 1, :], frow[:, 1, :], frow[:, 0, :], ALU.min).then_inc(l3["f_row"], 1)
                own.then(nc.vector.tensor_scalar(frow[:, 2, :], frow[:, 0, :], 0.0, None, ALU.min))
                dve.wait_ge(l3["f_e"], 2)
                nc.vector.tensor_tensor(frow[:, 1, :], frow[:, 1, :], frow[:, 2, :], ALU.subtract).then_inc(l3["f_ok"], 1)
                dve.wait_ge(l3["f_ok"], 1)
                own.then(nc.vector.tensor_tensor_scan(frow[:, 3, :], ones[0:16, 0:T], frow[:, 1, :], 0.0, ALU.mult, ALU.add))
                nc.vector.tensor_copy(negF, frow[:, 3, :]).then_inc(l3["f_ok"], 1)

            def head_norm(dst, src, sq, vs, rs, on, g):
                dve.wait_ge(sq, 8 * g + 8)
                nc.vector.tensor_scalar(sm[:, 32:40], sm[:, 32:40], 1.0 / HD, EPS, ALU.mult, ALU.add).then_inc(vs, 1)
                dve.wait_ge(rs, 2 * g + 2)
                for b in range(TB):
                    nc.vector.tensor_tensor(dst[:, b, :].rearrange("p (h d) -> p h d", d=HD), src[:, b, :].rearrange("p (h d) -> p h d", d=HD),
                                            sm[:, 48 + 4 * b:52 + 4 * b].unsqueeze(2).to_broadcast([P, 4, HD]), ALU.mult).then_inc(on, 1)

            def kv_side(g, p):
                if p == late("l3_kv", 0):
                    head_norm(qw3, qw3, l3["ksq"], l3["kv_"], l3["krs"], l3["kn"], g)

            for p in range(length("l3_f")):
                step(dve, low, evac, "l3_f", p)
            for p in range(length("l3_kv")):
                step(dve, low, evac, "l3_kv", p, 0, ("l3_f", 0))
                if p == 4:
                    forget_in()
                    forget()
            with dve.Fori(1, 4) as it:
                for p in range(length("l3_kv")):
                    step(dve, low, evac, "l3_kv", p, it, ("l3_kv", it - 1))
                    kv_side(it - 1, p)

            def q_side(g, p, name, at):

                def norm():
                    head_norm(qw3, qw3, l3["qsq"], l3["qv"], l3["qrs"], l3["qn"], g)

                def out_(hh):
                    r = fox.inverse(dve, own, g, hh)
                    for b in range(TB):
                        nc.vector.tensor_scalar(o3[:, b, hh * HD:hh * HD + HD], ps[:, 3, b * P:(b + 1) * P], r[:, b:b + 1],
                                                None, ALU.mult).then_inc(l3["o"], 1)

                def gate():
                    e = tmpT[:, 0, :]
                    for b in range(TB):
                        dve.wait_ge(l3["ge"], 2 * g + b + 1)
                        own.then(nc.vector.tensor_scalar(e, e, 1.0, None, ALU.add))
                        own.then(nc.vector.reciprocal(e, e))
                        nc.vector.tensor_tensor(gw3[:, b, :], gw3[:, b, :], e, ALU.mult).then_inc(l3["gs"], 1)

                def post():
                    head_norm(o3, o3, l3["sq"], l3["v"], l3["rs"], l3["on"], g)
                    dve.wait_ge(l3["on"], 2 * g + 2)
                    dve.wait_ge(l3["gs"], 2 * g + 2)
                    flat = lambda v: v.rearrange("p b n -> p (b n)")
                    nc.vector.tensor_tensor(flat(o3), flat(gw3), flat(o3), ALU.mult).then_inc(l3["og"], 1)

                def back():
                    for b in range(TB):
                        t = tmpT[:, b, :].rearrange("p (k t) -> p k t", t=P)
                        dve.wait_ge(l3["ogp"], 2 * g + b + 1)
                        nc.vector.tensor_tensor(t, ps[:, b, :].rearrange("p (k t) -> p k t", t=P),
                                                colB[:, group(64, g)].unsqueeze(2).to_broadcast([P, 4, P]), ALU.mult).then_inc(l3["tmp"], 1)
                    for b in range(TB):
                        t = tmpT[:, b, :].rearrange("p (k t) -> p k t", t=P)
                        dve.wait_ge(l3["hi"], 2 * g + b + 1)
                        nc.vector.tensor_tensor(heads_of(TA[1], g, b), t, heads_of(TA[0], g, b).bitcast(F32), ALU.subtract).then_inc(l3["lo"], 1)

                if p == late(name, at["norm"]):
                    norm()
                if p == late(name, at["sc0"]):
                    fox.mask_max(dve, own, g, 0)
                    fox.mask_max(dve, own, g, 1)
                if p == late(name, at["v0"]):
                    out_(0)
                if p == late(name, at["v1"]):
                    out_(1)
                    gate()
                    fox.mask_max(dve, own, g, 2)
                    fox.mask_max(dve, own, g, 3)
                if p == late(name, at["v2"]):
                    out_(2)
                if p == late(name, at["v3"]):
                    out_(3)
                if p == late(name, at["post"]):
                    post()
                if p == late(name, at["back"]):
                    back()

            for p in range(length("l3_q")):
                step(dve, low, evac, "l3_q", p, 0, ("l3_kv", 3))
                kv_side(3, p)
            with dve.Fori(1, 4) as it:
                own.enter(it, L3_OWN)
                for p in range(length("l3_q")):
                    step(dve, low, evac, "l3_q", p, it, ("l3_q", it - 1))
                    q_side(it - 1, p, "l3_q", L3_Q)
            own.leave(3)
            for p in range(length("l3_out")):
                step(dve, low, evac, "l3_out", p, 0, ("l3_q", 3))
                q_side(3, p, "l3_out", L3_END)
            finish(evac, "l3_out")

        @block.tensor
        def _(pe):
            turn = Turn()

            def turn_x(src):
                for i in range(8):
                    b, q = i // 4, i % 4
                    turn_pe(pe, turn, [src[:, b, (4 * q + j) * P:(4 * q + j + 1) * P] for j in range(4)])

            pe.wait_ge(const_ok, 1)
            pe.wait_ge(par_in, 16 * 12)
            nc.tensor.transpose(ps[:, 0, 0:NA_ROWS], stage_rows[0:NA_ROWS, 0, :], ident[0:NA_ROWS, 0:NA_ROWS])
            nc.tensor.transpose(ps[:, 0, P:P + NB_ROWS], stage_rows[0:NB_ROWS, 1, :], ident[0:NB_ROWS, 0:NB_ROWS]).then_inc(col_pe, 1)
            pe.wait_ge(col_ok, 2)
            pe.wait_ge(x_in, 32)
            turn_x(x_res)

            def in_src(k, q):
                return TA[0], TA[1], q

            pe.wait_ge(tr_lo, 8)
            for p in range(length("l0_in")):
                products(pe, "l0_in", p, in_src)

            def latents():
                pe.wait_ge(l0["kr_ok"], 3)
                for b in range(TB):
                    m = nc.tensor.transpose(ps[:, 0, b * P:(b + 1) * P], krd[:, b, :, :].rearrange("p a f -> p (a f)"), ident[:])
                m.then_inc(l0["kr_pe"], 1)

            def latents2():
                pe.wait_ge(l0["lat_ok"], 4)
                pe.wait_ge(l0["kr_T"], 1)
                for j in range(2):
                    for b in range(TB):
                        turn_pe(pe, turn, [cq[:, b, (4 * j + i) * P:(4 * j + i + 1) * P] for i in range(4)])

            def l0_side(s, p, at):
                name = f"l0_{s}"

                def pair(pr):
                    c2 = 2 * s + pr
                    pe.wait_ge(l0["rope"], 2 * c2 + 2)
                    landed(pe, name, l0_tile(s, pr, 0))
                    landed(pe, name, l0_tile(s, pr, 1))
                    if c2 > 0:
                        pe.wait_ge(l0["msk"], 2 * c2)
                    if c2 > 0:
                        pe.wait_ge(l0["ptc"], 2 * c2)
                    pe.wait_ge(tr_lo, turn.n)
                    pe.wait_ge(l0["kr_T"], 1)
                    for hh in range(2):
                        for b in range(TB):
                            o = slice(hh * T + b * P, hh * T + (b + 1) * P)
                            nc.tensor.transpose(ps[:, 0, o], qw[pr][:, b, hh * QH:hh * QH + NOPE], ident[:])
                            nc.tensor.transpose(ps[:, 1, o], kvw[pr][:, b, hh * 256:hh * 256 + NOPE], ident[:])
                    for b in range(TB):
                        m = nc.tensor.transpose(ps[:, 2, b * P:(b + 1) * P], qr[:, b, :, :].rearrange("p h f -> p (h f)"), ident[:])
                    m.then_inc(l0["tr"], 1)

                def scores(pr):
                    pe.wait_ge(l0["trA"], 2 * (2 * s + pr) + 2)
                    pe.wait_ge(l0["trV"], 2 * s + pr + 1)
                    mla.scores(pe, s, 2 * pr)
                    mla.scores(pe, s, 2 * pr + 1)

                def back():
                    pe.wait_ge(l0["o"], 2 * (4 * s + 4))
                    for b in range(TB):
                        turn_pe(pe, turn, [og0[:, b, i * P:(i + 1) * P] for i in range(4)])

                if p == at[1]:
                    pair(0)
                if p == at[2]:
                    scores(0)
                if p == at[3]:
                    mla.turn(pe, s, 0)
                if p == at[4]:
                    mla.values(pe, s, 0)
                    mla.turn(pe, s, 1)
                if p == at[5]:
                    mla.values(pe, s, 1)
                    pair(1)
                if p == at[6]:
                    scores(1)
                if p == at[7]:
                    mla.turn(pe, s, 2)
                if p == at[8]:
                    mla.values(pe, s, 2)
                    mla.turn(pe, s, 3)
                if p == at[9]:
                    mla.values(pe, s, 3)
                if p == at[10]:
                    back()

            for p in range(length("l0_0")):
                if p == 16:
                    pe.wait_ge(tr_lo, 12)
                products(pe, "l0_0", p, lambda k, q: latent_src(k, q, 0))
                if p == 6:
                    latents()
                if p == 10:
                    latents2()
            for s in range(1, 4):
                for p in range(length(f"l0_{s}")):
                    products(pe, f"l0_{s}", p, lambda k, q: latent_src(k, q, s))
                    l0_side(s - 1, p, l0_at(f"l0_{s}"))
            for p in range(length("l0_out")):
                if p == 0:
                    pe.wait_ge(tr_lo, 18)
                if p == 12:
                    pe.wait_ge(tr_lo, 20)
                products(pe, "l0_out", p, out0_src)
                l0_side(3, p, l0_at("l0_out"))
            if depth < 2:
                return
            pe.wait_ge(tr_src, 2)
            turn_x(x_res)
            pe.wait_ge(tr_lo, turn.n)

            for p in range(length("l1_gates")):
                products(pe, "l1_gates", p, in_src)

            def gates_a():
                pe.wait_ge(l1["g_in"], 2)
                for b in range(TB):
                    nc.tensor.transpose(ps[0:8, 2, b * P:(b + 1) * P], gt[:, b, 0:8], ident[:])
                    m = nc.tensor.transpose(ps[0:8, 2, T + b * P:T + (b + 1) * P], gt[:, b, 8:16], ident[:])
                m.then_inc(l1["g_pe"], 1)

            def gates_c():
                pe.wait_ge(l1["g_m"], 2)
                for b in range(TB):
                    nc.tensor.transpose(ps[:, 3, 8 * b:8 * b + 8], grow[:, 3, b * P:(b + 1) * P], ident[0:8, 0:8])
                    m = nc.tensor.transpose(ps[:, 3, 16 + 8 * b:24 + 8 * b], grow[:, 5, b * P:(b + 1) * P], ident[0:8, 0:8])
                m.then_inc(l1["g_pe2"], 1)

            def window(s, j):
                landed(pe, f"l1_{s}", j)
                pe.wait_ge(tr_lo, turn.n)
                if 2 * s + j > 0:
                    pe.wait_ge(l1["q_c"], 2 * s + j)
                if s > 0:
                    pe.wait_ge(l1["st"], 4 * s)
                for h in range(4):
                    for b in range(TB):
                        m = nc.tensor.transpose(ps2(0)[:, h * T + b * P:h * T + (b + 1) * P], qkw[j][:, b, h * P:(h + 1) * P], ident[:])
                m.then_inc(l1["q_pe"], 1)

            def weigh(s, c):
                h = c % 4
                pe.wait_ge(l1["q_r"], 2 * s + 2)
                pe.wait_ge(l1["q_c"], 2 * s + 2)
                if c > 0:
                    pe.wait_ge(l1["st"], c)
                pe.wait_ge(l1["g_m"], 2)
                nc.tensor.matmul(ps[:, 0, 0:T], ident[0:8, c:c + 1].to_broadcast([8, P]), negM, start=True, stop=True)
                nc.tensor.matmul(ps[:, 1, 0:T], kT1[:, h, 0:P], qT1[:, h, :], start=True, stop=True)
                nc.tensor.matmul(ps[:, 1, T:384], kT1[:, h, P:T], qT1[:, h, P:T], start=True, stop=True).then_inc(l1["sc"], 1)

            def number(s, c):
                h = c % 4
                landed(pe, f"l1_{s}", 2 + h // 2)
                pe.wait_ge(l1["pads"], 2)
                pe.wait_ge(l1["st"], c + 1)
                if c > 0:
                    pe.wait_ge(l1["h"], 2 * c)
                pe.wait_ge(l1["g_col"], 2)
                v = lambda b: vw[:, b, h, 0:MV + 1]
                nc.tensor.matmul(ps[:, 2, 0:MV + 1], wst[:, 0:P], v(0), start=True, stop=True)
                nc.tensor.matmul(ps[:, 3, 0:MV + 1], wst[:, P:T], v(0), start=True, stop=False)
                nc.tensor.matmul(ps[:, 3, 0:MV + 1], wst[:, T:384], v(1), start=False, stop=True).then_inc(l1["nm"], 1)

            def gated_turn(s, j):
                pe.wait_ge(l1["og"], 8 * s + 4 * j + 4)
                pe.wait_ge(l1["h"], 8 * s + 8)
                for b in range(TB):
                    turn_pe(pe, turn, [ow[:, b, j * COLS + i * P:j * COLS + (i + 1) * P] for i in range(4)])


            def l1_side(s, p):
                if s == 0 and p == 5:
                    gates_a()
                if s == 0 and p == 8:
                    gates_c()
                if s == 1:
                    l1_rest(0, p)
                for j in range(2):
                    if p == L1_AT["qk"[j]]:
                        window(s, j)
                for h in range(4):
                    if p == L1_AT["ws"][h]:
                        weigh(s, 4 * s + h)
                    if p == L1_AT["nm"][h]:
                        number(s, 4 * s + h)
                if p == L1_AT["t0"]:
                    gated_turn(s, 0)

            def l1_rest(s, p):
                if p == 6:
                    gated_turn(s, 1)

            for s in range(2):
                for p in range(length("l1_0")):
                    products(pe, f"l1_{s}", p, in_src)
                    l1_side(s, p)
            for p in range(length("l1_out")):
                if p == 0:
                    pe.wait_ge(tr_lo, L1_BASE + 6)
                if p == 12:
                    pe.wait_ge(tr_lo, L1_BASE + 8)
                products(pe, "l1_out", p, out1_src)
                l1_rest(1, p)
            if depth < 3:
                return

            pe.wait_ge(tr_src, 5)
            pe.wait_ge(tr_src_act, 1)
            turn_x(hn)
            pe.wait_ge(tr_lo, turn.n)

            def l2_side(g, p, at):
                def turned():
                    landed(pe, "l2", 1, g)
                    for w, bank in ((qw2, 0), (fw2, 2)):
                        for h in range(4):
                            for b in range(TB):
                                m = nc.tensor.transpose(ps2(bank)[:, h * T + b * P:h * T + (b + 1) * P], w[:, b, h * P:(h + 1) * P], ident[:])
                        m.then_inc(l2["tq" if bank == 0 else "tf"], 1)

                def diag():
                    pe.wait_ge(l2["qT"], 1 + 1 * g)
                    pe.wait_ge(l2["kt"], 1 + 1 * g)
                    for h in range(4):
                        for b in range(TB):
                            c = slice(b * P, (b + 1) * P)
                            m = nc.tensor.matmul(ps2(0)[:, (2 * h + b) * P:(2 * h + b + 1) * P], kT2[:, h, c], qT2[:, h, c], start=True, stop=True)
                    m.then_inc(l2["dg"], 1)

                def level(j):
                    pe.wait_ge(l2["op"], 2 * j + 2 + 16 * g)
                    if j >= 2:
                        pe.wait_ge(l2["sel"], j - 1 + 8 * g)
                    k = dT[:, j % 2, :].rearrange("p (h t) -> p h t", t=T)
                    for h in range(4):
                        if j == 0:
                            m = nc.tensor.matmul(ps[:, 2, h * P:(h + 1) * P], k[:, h, 0:P], qx[:, 0, h * P:(h + 1) * P], start=True, stop=True)
                            continue
                        for b in range(TB):
                            n = 2 * h + b
                            m = nc.tensor.matmul(ps[:, 2 + j % 2, n * 64:(n + 1) * 64], k[:, h, b * P:(b + 1) * P],
                                                 qx[:, j % 2, n * 64:(n + 1) * 64], start=True, stop=True)
                    m.then_inc(l2["lv"], 1)

                def values():
                    pe.wait_ge(l2["sel"], 8 + 8 * g)
                    landed(pe, "l2", 2, g)
                    for h in range(4):
                        v = lambda b: vw2[:, b, h * HD:(h + 1) * HD]
                        o = slice(h * HD, (h + 1) * HD)
                        nc.tensor.matmul(ps[:, 0, o], aT[:, 2 * h, :], v(0), start=True, stop=True)
                        nc.tensor.matmul(ps[:, 1, o], a01[:, h, :], v(0), start=True, stop=False)
                        m = nc.tensor.matmul(ps[:, 1, o], aT[:, 2 * h + 1, :], v(1), start=False, stop=True)
                    m.then_inc(l2["pv"], 1)

                def back():
                    pe.wait_ge(l2["og"], 1 + 1 * g)
                    for b in range(TB):
                        for i in range(4):
                            m = nc.tensor.transpose(ps[:, 2 + b, i * P:(i + 1) * P], gw2[:, b, i * P:(i + 1) * P], ident[:])
                        m.then_inc(l2["ogp"], 1)

                if p == at["turn"]:
                    turned()
                if p == at["diag"]:
                    diag()
                for j in range(8):
                    if p == at["level"][j]:
                        level(j)
                if p == at["pv"]:
                    values()
                if p == at["back"]:
                    back()

            for p in range(length("l2")):
                products(pe, "l2", p, in_src)
            with pe.Fori(1, 4) as it:
                for p in range(length("l2")):
                    products(pe, "l2", p, in_src, it)
                    l2_side(it - 1, p, L2_AT)
            for p in range(length("l2_out")):
                if p == 0:
                    pe.wait_ge(l2["lo"], 6)
                if p == 12:
                    pe.wait_ge(l2["lo"], 8)
                products(pe, "l2_out", p, out1_src)
                l2_side(3, p, L2_END)
            if depth < 4:
                return

            pe.wait_ge(tr_src, 6)
            pe.wait_ge(tr_src_act, 2)
            pe.wait_ge(l2["lo"], 8)
            turn_x(hn)
            turn_x(hn)
            pe.wait_ge(tr_lo, turn.n - 8)

            for p in range(length("l3_f")):
                products(pe, "l3_f", p, in_src)

            def forget():
                pe.wait_ge(l3["f_in"], 2)
                pe.wait_ge(tr_lo, turn.n)
                for b in range(TB):
                    m = nc.tensor.transpose(ps[0:16, 3, b * P:(b + 1) * P], ft[:, b, :], ident[:])
                m.then_inc(l3["f_pe"], 1)

            def turn_window(done):
                for h in range(4):
                    for b in range(TB):
                        m = nc.tensor.transpose(ps2(0)[:, h * T + b * P:h * T + (b + 1) * P], qw3[:, b, h * HD:(h + 1) * HD], ident[:])
                m.then_inc(done, 1)

            def kv_side(g, p):
                if p == 5:
                    pe.wait_ge(l3["kn"], 2 * g + 2)
                    pe.wait_ge(tr_lo, turn.n)
                    turn_window(l3["kt"])

            for p in range(length("l3_kv")):
                products(pe, "l3_kv", p, in_src)
                if p == 4:
                    forget()
            with pe.Fori(1, 4) as it:
                for p in range(length("l3_kv")):
                    products(pe, "l3_kv", p, in_src, it)
                    kv_side(it - 1, p)

            def q_src(k, q):
                return TBf[0], TBf[1], q

            def q_side(g, p, at):
                def queries():
                    pe.wait_ge(l3["qn"], 2 * g + 2)
                    pe.wait_ge(l3["kT"], 4)
                    if g > 0:
                        pe.wait_ge(l3["lo"], 2 * g)
                    turn_window(l3["qt"])

                def scores(hh):
                    pe.wait_ge(l3["qT"], g + 1)
                    pe.wait_ge(l3["f_ok"], 2)
                    fox.scores(pe, g, hh)
                    fox.scores(pe, g, hh + 1)

                def back():
                    pe.wait_ge(l3["og"], g + 1)
                    pe.wait_ge(l3["msk"], 4 * g + 4)
                    for b in range(TB):
                        for i in range(4):
                            m = nc.tensor.transpose(ps[:, b, i * P:(i + 1) * P], o3[:, b, i * P:(i + 1) * P], ident[:])
                        m.then_inc(l3["ogp"], 1)

                if p == at["turn"]:
                    queries()
                if p == at["sc0"]:
                    scores(0)
                if p == at["t0"]:
                    fox.turn(pe, g, 0)
                if p == at["v0"]:
                    fox.values(pe, g, 0)
                    fox.turn(pe, g, 1)
                if p == at["v1"]:
                    fox.values(pe, g, 1)
                    scores(2)
                if p == at["t2"]:
                    fox.turn(pe, g, 2)
                if p == at["v2"]:
                    fox.values(pe, g, 2)
                    fox.turn(pe, g, 3)
                if p == at["v3"]:
                    fox.values(pe, g, 3)
                if p == at["back"]:
                    back()

            pe.wait_ge(tr_lo, turn.n)
            for p in range(length("l3_q")):
                products(pe, "l3_q", p, q_src)
                kv_side(3, p)
            for it in range(1, 4):
                for p in range(length("l3_q")):
                    products(pe, "l3_q", p, q_src, it)
                    q_side(it - 1, p, L3_Q)
            for p in range(length("l3_out")):
                if p == 0:
                    pe.wait_ge(l3["lo"], 6)
                if p == 12:
                    pe.wait_ge(l3["lo"], 8)
                products(pe, "l3_out", p, in_src)
                q_side(3, p, L3_END)


_INS = ["x", "positions", "mla_w_in", "mla_q_norm", "mla_w_qb", "mla_kv_norm", "mla_w_kvb", "mla_w_out", "ml_w_in",
        "ml_conv_w", "ml_conv_b", "ml_gate_b", "ml_head_norm", "ml_w_out", "ln_w", "ln_b", "a_norm_w_2", "a_w_in_2",
        "a_lb_logits_2", "a_out_norm_w_2", "a_w_out_2", "kv_norm_w_2", "kv_w_2", "kv_f_bias_2", "k_norm_w_2",
        "b_norm_w_2", "b_w_in_2", "b_q_norm_w_2", "b_out_norm_w_2", "b_w_out_2"]


def kernel(**inputs):
    import numpy as _np
    import concourse.bacc as _bacc
    from concourse.bass_utils import run_bass_kernel_spmd as _run

    nc = _bacc.Bacc("TRN2", target_bir_lowering=False, num_devices=1)
    arrays, args = {}, {}
    for name in _INS:
        v = _np.ascontiguousarray(inputs[name])
        arrays[f"in_{name}"] = v
        args[name] = nc.dram_tensor(f"in_{name}", v.shape, mybir.dt.from_np(v.dtype), kind="ExternalInput").ap()
    out = nc.dram_tensor("out_x", (1, T, D), F32, kind="ExternalOutput").ap()
    build(nc, args, out)
    r = _run(nc, [arrays], core_ids=[0])
    return r.results[0]["out_x"]
```

```python
from contextlib import ExitStack

import numpy as np
import concourse.bass as bass
from concourse import mybir

F32 = mybir.dt.float32
F32R = mybir.dt.float32r
I32 = mybir.dt.int32
U8 = mybir.dt.uint8
ALU = mybir.AluOpType
ACT = mybir.ActivationFunctionType
AX = mybir.AxisListType.X

P = 128
T = 256
TB = T // P
D = 2048
KT = D // P
COLS = 512
KU = 2
RAW = 8
SPLIT = 4
NARROW = 64
LAG = 3
EPS = 1e-6
NEG = -3.0e38
LN_EXP_SET = 6

H0, NOPE, ROPE, VH = 16, 128, 64, 128
LORA = 512
QH = NOPE + ROPE
THETA = 10000.0
H1, MQK, MV, CONV = 8, 128, 256, 4
H2, HD = 16, 128
ALPHA = 4 ** 0.25

NA_ROWS, NB_ROWS = 104, 82


class Own:

    def __init__(self, eng, sem):
        self.eng, self.sem, self.n = eng, sem, 0
        self.it, self.per = 0, 0

    def mark(self, ins):
        ins.then_inc(self.sem, 1)
        self.n += 1

    def sync(self):
        self.eng.wait_ge(self.sem, self.n + self.it * self.per)

    def then(self, ins):
        self.mark(ins)
        self.sync()

    def enter(self, it, per):
        self.it, self.per, self.start = it, per, self.n
        self.n -= per

    def leave(self, runs):
        assert self.n + self.per - self.start == self.per, (self.n + self.per - self.start, self.per)
        self.n = self.start + runs * self.per
        self.it, self.per = 0, 0


def build(nc, a, out):
    with ExitStack() as ctx:
        sb = lambda name, shape, dt=F32: ctx.enter_context(nc.sbuf_tensor(name, shape, dt))
        sem = lambda name: ctx.enter_context(nc.semaphore(name))

        x_res = sb("x_res", [P, TB, D])
        wraw = sb("wraw", [P, RAW, KU, COLS])
        whi = sb("whi", [P, SPLIT, KU, COLS], F32R)
        wlo = sb("wlo", [P, SPLIT, KU, COLS], F32R)
        TA = (sb("ta_hi", [P, KT, T], F32R), sb("ta_lo", [P, KT, T], F32R))
        TBf = (sb("tb_hi", [P, KT, T], F32R), sb("tb_lo", [P, KT, T], F32R))
        ident = sb("ident", [P, P])
        ones = sb("ones", [P, T])
        colA = sb("colA", [P, NA_ROWS])
        colB = sb("colB", [P, NB_ROWS])
        tmpT = sb("tmpT", [P, 2, COLS])
        bstat = sb("bstat", [P, TB, 4, 6])
        mv = sb("mv", [P, TB, 2])
        nrm = sb("nrm", [P, TB, 4])
        sm = sb("sm", [P, 64])
        eps_col = sm[:, 58:59]
        mask = sb("mask", [P, 384])
        posi = sb("posi", [P, TB], I32)
        lvl = sb("lvl", [P, 7, 64], U8)
        gbias = sb("gbias", [16, 2])
        ARENA = 14080
        arena = sb("arena", [P, ARENA])

        acc = ctx.enter_context(nc.psum_tensor("acc", [P, 2, TB, COLS], F32))
        ps = ctx.enter_context(nc.psum_tensor("ps", [P, 4, COLS], F32))
        ps2 = lambda b: ps[:, b:b + 2, :].rearrange("p a n -> p (a n)")

        class Carve:

            def __init__(self):
                self.at = 0

            def __call__(self, *shape, rows=P):
                n = int(np.prod(shape))
                v = arena[0:rows, self.at:self.at + n]
                self.at += n + n % 2
                assert self.at <= ARENA, self.at
                if len(shape) == 2:
                    v = v.rearrange("p (a b) -> p a b", b=shape[1])
                elif len(shape) == 3:
                    v = v.rearrange("p (a b c) -> p a b c", b=shape[1], c=shape[2])
                return v

        w_loaded = [sem(f"w_loaded{i}") for i in range(RAW)]
        w_high = sem("w_high")
        w_low = sem("w_low")
        w_used = sem("w_used")
        out_b0 = sem("out_b0")
        out_b1 = sem("out_b1")
        x_in = [sem(f"x_in{b}") for b in range(TB)]
        par_in = sem("par_in")
        bias_in = sem("bias_in")
        const_ok = sem("const_ok")
        pool_own, act_own, dve_own = sem("pool_own"), sem("act_own"), sem("dve_own")
        col_pe, col_ok = sem("col_pe"), sem("col_ok")
        rope_arg, rope_ok = sem("rope_arg"), sem("rope_ok")
        tr_src = sem("tr_src")
        half_used = sem("half_used")
        ident_ok = sem("ident_ok")
        tr_pe = sem("tr_pe")
        tr_tmp = sem("tr_tmp")
        tr_hi, tr_lo = sem("tr_hi"), sem("tr_lo")
        x_done = sem("x_done")
        lnp_in = sem("lnp_in")
        nrm_a, nrm_v = sem("nrm_a"), sem("nrm_v")
        st_out = sem("st_out")

        Wv = {k: (a[k][0] if len(a[k].shape) == 3 else a[k]).rearrange("(k p) n -> p k n", p=P)
              for k in ("mla_w_in", "mla_w_qb", "mla_w_kvb", "mla_w_out", "ml_w_in", "ml_w_out", "a_w_in_2",
                        "a_w_out_2",
                        "kv_w_2", "b_w_in_2", "b_w_out_2")}

        OUT_VIEWS = [Wv[k] for k in ("mla_w_out", "ml_w_out", "a_w_out_2", "b_w_out_2")]
        def first(it):
            return isinstance(it, int) and it == 0

        def units(tiles):
            return sum(t[1] for t in tiles) // KU

        def places(tiles):
            if any(tiles[0][0] is v for v in OUT_VIEWS):
                late = KT - KT // 4
                r = [(k, q) for k in (0, 1) for q in range(0, late, KU)]
                r += [(k, q) for k in (0, 1) for q in range(late, KT, KU)]
                return r + [(k, q) for k in (2, 3) for q in range(0, KT, KU)]
            return [(k, q) for k, t in enumerate(tiles) for q in range(0, t[1], KU)]

        def ends(name):
            tiles = PHD[name][1]
            at = places(tiles)
            return [max(i for i, (k, q) in enumerate(at) if k == n) for n in range(len(tiles))]

        UNIT, TILE = {}, {}
        PH = []
        u = t = 0

        def phase(name, tiles, runs):
            nonlocal u, t
            PH.append((name, tiles, runs))
            UNIT[name], TILE[name] = u, t
            u += units(tiles) * runs
            t += len(tiles) * runs
            assert units(tiles) % RAW == 0, name
            assert runs == 1 or len(tiles) % 2 == 0

        Z_FIRST = [0, 2, 3, 4, 4]
        w_in, w_qb, w_kvb = Wv["mla_w_in"], Wv["mla_w_qb"], Wv["mla_w_kvb"]
        phase("l0_in", [(w_in, KT, 0, 0, 512), (w_in, KT, 512, 0, 512), (w_in, KT, 1024, 0, ROPE)], 1)
        for s in range(4):
            zs = [(w_in, KT, 1088 + 512 * j, 0, 512) for j in range(Z_FIRST[s], Z_FIRST[s + 1])]
            phase(f"l0_{s}", zs + [
                x for pr in range(2) for x in (
                    (w_qb, 4, (2 * s + pr) * 2 * QH, 0, 2 * QH),
                    (w_kvb, 4, (2 * s + pr) * 2 * (NOPE + VH), 0, 2 * (NOPE + VH)))], 1)
        out_tiles = lambda w: [(Wv[w], KT, c * COLS, 0, COLS) for c in range(4)]
        phase("l0_out", out_tiles("mla_w_out"), 1)
        w1 = Wv["ml_w_in"]
        phase("l1_gates", [(w1, KT, 6144, 0, NARROW)], 1)
        for s in range(2):
            phase(f"l1_{s}", [(w1, KT, 512 * s, 0, 512), (w1, KT, 1024 + 512 * s, 0, 512)]
                  + [(w1, KT, base + 1024 * s + 512 * j, 0, 512) for base in (2048, 4096, 6160) for j in range(2)], 1)
        phase("l1_out", out_tiles("ml_w_out"), 1)
        w2 = Wv["a_w_in_2"]
        phase("l2", [(w2, KT, D * j, COLS, COLS) for j in range(4)], 4)
        phase("l2_out", out_tiles("a_w_out_2"), 1)
        w3, w4 = Wv["kv_w_2"], Wv["b_w_in_2"]
        phase("l3_f", [(w3, KT, 2 * D, 0, 16)], 1)
        phase("l3_kv", [(w3, KT, D * j, COLS, COLS) for j in range(2)], 4)
        phase("l3_q", [(w4, KT, D * j, COLS, COLS) for j in range(2)], 4)
        phase("l3_out", out_tiles("b_w_out_2"), 1)
        PHD = {p[0]: p for p in PH}

        def high(act, name, p, it=0):
            tiles = PHD[name][1]
            k, q = places(tiles)[p]
            w, nu, n = tiles[k][4], units(tiles), UNIT[name] + p
            act.wait_ge(w_loaded[n % RAW], 16 * (n // RAW + 1) + 16 * (nu // RAW) * it)
            if n >= SPLIT:
                act.wait_ge(w_used, n - SPLIT + 1 + nu * it)
            nc.scalar.activation(whi[:, n % SPLIT, :, 0:w], wraw[:, n % RAW, :, 0:w], ACT.Copy).then_inc(w_high, 1)

        def low(dve, name, p, it=0):
            tiles = PHD[name][1]
            k, q = places(tiles)[p]
            w, nu, n = tiles[k][4], units(tiles), UNIT[name] + p
            dve.wait_ge(w_high, n + 1 + nu * it)
            nc.vector.tensor_tensor(wlo[:, n % SPLIT, :, 0:w], wraw[:, n % RAW, :, 0:w],
                                    whi[:, n % SPLIT, :, 0:w].bitcast(F32), ALU.subtract).then_inc(w_low, 1)

        def products(pe, name, p, src, it=0, blocks=(0, 1)):
            tiles = PHD[name][1]
            k, q = places(tiles)[p]
            w, kt, nu, n, tt = tiles[k][4], tiles[k][1], units(tiles), UNIT[name] + p, TILE[name] + k
            if q == 0 and tt >= 2:
                for b in blocks:
                    pe.wait_ge((out_b0, out_b1)[b], tt - 1 + len(tiles) * it)
            pe.wait_ge(w_low, n + 1 + nu * it)
            if w <= NARROW:
                for j in range(KU):
                    o = acc[0:w, tt % 2, 0, 0:T]
                    hi, lo, kk = src(k, q + j)
                    wh, wl = whi[:, n % SPLIT, j, 0:w], wlo[:, n % SPLIT, j, 0:w]
                    nc.tensor.matmul(o, wh, hi[:, kk, :], start=q + j == 0, stop=False)
                    nc.tensor.matmul(o, wl, hi[:, kk, :], start=False, stop=False)
                    m = nc.tensor.matmul(o, wh, lo[:, kk, :], start=False, stop=q + j == kt - 1)
                m.then_inc(w_used, 1)
                return
            for j in range(KU):
                for b in blocks:
                    o = acc[:, tt % 2, b, 0:w]
                    hi, lo, kk = src(k, q + j)
                    xh, xl = hi[:, kk, b * P:(b + 1) * P], lo[:, kk, b * P:(b + 1) * P]
                    wh, wl = whi[:, n % SPLIT, j, 0:w], wlo[:, n % SPLIT, j, 0:w]
                    first, end = q + j == 0, q + j == kt - 1
                    nc.tensor.matmul(o, xh, wh, start=first, stop=False)
                    nc.tensor.matmul(o, xh, wl, start=False, stop=False)
                    m = nc.tensor.matmul(o, xl, wh, start=False, stop=end)
            if blocks[-1] == TB - 1:
                m.then_inc(w_used, 1)
            elif end:
                m.then_inc(half_used, 1)

        def first_products(pe, name, src, turned):
            if PHD[name][1][0][4] <= NARROW:
                for p in range(SPLIT):
                    pe.wait_ge(tr_lo, turned - 4 + p // 2 + 1)
                    products(pe, name, p, src)
                return
            for b in range(TB):
                for p in range(SPLIT):
                    if p % 2 == 0:
                        pe.wait_ge(tr_lo, turned - 8 + 4 * b + p // 2 + 1)
                    products(pe, name, p, src, 0, (b,))

        def last_products(pe, name, src):
            nu = length(name)
            for b in range(TB):
                for p in range(nu - SPLIT, nu):
                    products(pe, name, p, src, 0, (b,))

        def tile_done(eng, name, k, it=0):
            tiles = PHD[name][1]
            eng.wait_ge(w_used, UNIT[name] + ends(name)[k] + 1 + units(tiles) * it)

        def result(name, k, b, rows):
            w, bank = PHD[name][1][k][4], (TILE[name] + k) % 2
            return acc[0:rows, bank, 0, b * P:(b + 1) * P] if w <= NARROW else acc[:, bank, b, 0:w]

        def evac_act(act, name, k, dst, it=0):
            tile_done(act, name, k, it)
            nc.scalar.activation(dst, result(name, k, 0, dst.shape[0]), ACT.Copy).then_inc(out_b0, 1)

        def evac_dve(dve, name, k, dst, it=0):
            tile_done(dve, name, k, it)
            if PHD[name][1][k][4] <= NARROW:
                dve.wait_ge(out_b0, TILE[name] + k + 1)
            nc.vector.tensor_copy(dst, result(name, k, 1, dst.shape[0])).then_inc(out_b1, 1)

        def landed(eng, name, k, it=0):
            n = TILE[name] + k + 1
            eng.wait_ge(out_b0, n + len(PHD[name][1]) * it)
            eng.wait_ge(out_b1, n + len(PHD[name][1]) * it)

        def carried(name):
            nu = length(name)
            return {e + LAG - nu: k for k, e in enumerate(ends(name)) if e + LAG >= nu}

        def length(name):
            return units(PHD[name][1])

        def late(name, at):
            return min(at + LAG, length(name) - 1)

        def step(eng, split, evac, name, p, it=0, prev=None):
            split(eng, name, p, it)
            if prev and p in carried(prev[0]):
                evac(prev[0], carried(prev[0])[p], prev[1])
            for k, e in enumerate(ends(name)):
                if p == e + LAG:
                    evac(name, k, it)

        def finish(evac, name, it=0):
            for p, k in sorted(carried(name).items()):
                evac(name, k, it)

        class Turn:
            def __init__(self):
                self.n, self.w = 0, 0

        def turn_pe(pe, cnt, srcs):
            c = cnt.n
            if c >= 4:
                pe.wait_ge(tr_lo, c - 3)
            for j, s in enumerate(srcs):
                m = nc.tensor.transpose(ps[:, c % 4, j * P:(j + 1) * P], s, ident[:])
            m.then_inc(tr_pe, 1)
            cnt.n += 1

        def turn_act(act, cnt, dst, weighted):
            c = cnt.n
            if weighted:
                act.wait_ge(tr_tmp, cnt.w + 1)
                src = tmpT[:, cnt.w % 2, :].rearrange("p (k t) -> p k t", t=P)
                cnt.w += 1
            else:
                act.wait_ge(tr_pe, c + 1)
                src = ps[:, c % 4, :].rearrange("p (k t) -> p k t", t=P)
            nc.scalar.activation(dst, src, ACT.Copy).then_inc(tr_hi, 1)
            cnt.n += 1

        def turn_dve(dve, cnt, dst_hi, dst_lo, col=None):
            c = cnt.n
            bank = ps[:, c % 4, :].rearrange("p (k t) -> p k t", t=P)
            if col is not None:
                dve.wait_ge(tr_pe, c + 1)
                src = tmpT[:, cnt.w % 2, :].rearrange("p (k t) -> p k t", t=P)
                nc.vector.tensor_tensor(src, bank, col.unsqueeze(2).to_broadcast([P, 4, P]),
                                        ALU.mult).then_inc(tr_tmp, 1)
                cnt.w += 1
            else:
                src = bank
            dve.wait_ge(tr_hi, c + 1)
            nc.vector.tensor_tensor(dst_lo, src, dst_hi.bitcast(F32), ALU.subtract).then_inc(tr_lo, 1)
            cnt.n += 1

        A = Carve()
        lat = A(2 * TB * LORA)
        cq = lat.rearrange("p (b n) -> p b n", b=TB)
        ez, og0 = [v.rearrange("p (b n) -> p b n", b=TB) for v in (lat[:, 0:1024], lat[:, 1024:2048])]
        krT, cos, sin = A(T), A(TB, 32), A(TB, 32)
        qw1 = A(TB * 2 * QH)
        krf = qw1[0:ROPE, 384:384 + T]
        krw = qw1[:, 0:128].rearrange("p (b n) -> p b n", b=TB)
        krd = qw1[:, 128:384].rearrange("p (b a n) -> p b a n", b=TB, a=2)
        qw = [A(TB, 2 * QH), qw1.rearrange("p (b n) -> p b n", b=TB)]
        kvw = [A(TB, 512) for _ in range(2)]
        zw = [A(TB, 512) for _ in range(4)]
        early = Carve()
        early.at = A.at - 2048
        stage_rows, posf, invf, lvf, angle = early(2, P), early(4), early(32), early(7, 64), early(6, TB * 32)
        qr, rt = A(TB, 2, ROPE), A(4, TB * 2 * 32)
        qT0, kT0, qrT0 = A(2, T), A(2, T), A(T)
        sS, sPT = A(2, 384), A(2, 384)

        A = Carve()
        A.at = 4 * D
        hn = A(TB, D)
        lnw, lnb = arena[:, 0:D], arena[:, D:2 * D]

        def sems(layer, names):
            return {n: sem(f"l{layer}_{n}") for n in names.split()}

        l0 = sems(0,
                  "kr_in lat_sq lat_v lat_r lat_ok kr_ok kr_pe kr_T z_e z_ok rope tr trA trV sc msk mx ex pt ptc pv o")

        SMALL = 24

        class Heads:
            def __init__(self, l, scale, mask, qk, v, S, PT):
                self.l, self.scale, self.mask, self.qk, self.v, self.S, self.PT = l, scale, mask, qk, v, S, PT

            def scores(self, pe, g, hh):
                c, w = 4 * g + hh, hh % 2
                if hh >= 2:
                    pe.wait_ge(self.l["msk"], c - 1)
                for b in range(TB):
                    o = ps[:, w, b * P:b * P + (b + 1) * P]
                    parts = self.qk(c, b)
                    for i, (x, y) in enumerate(parts):
                        m = nc.tensor.matmul(o, x, y, start=i == 0, stop=i == len(parts) - 1)
                m.then_inc(self.l["sc"], 1)

            def mask_max(self, dve, own, g, hh):
                c, w = 4 * g + hh, hh % 2
                dve.wait_ge(self.l["sc"], c + 1)
                if hh >= 2:
                    dve.wait_ge(self.l["pt"], c - 1)
                s = self.S[:, w, :]
                nc.vector.scalar_tensor_tensor(s, ps[:, w, 0:384], self.scale, self.mask[:], ALU.mult,
                                               ALU.add).then_inc(self.l["msk"], 1)
                dve.wait_ge(self.l["msk"], c + 1)
                n = sm[:, 2 * w:2 * w + 2]
                nc.vector.tensor_reduce(n[:, 0:1], s[:, 0:P], AX, ALU.max, negate=True).then_inc(self.l["mx"], 1)
                nc.vector.tensor_reduce(n[:, 1:2], s[:, P:384], AX, ALU.max, negate=True).then_inc(self.l["mx"], 1)

            def weights(self, act, g, hh):
                c, w = 4 * g + hh, hh % 2
                act.wait_ge(self.l["mx"], 2 * c + 2)
                if hh >= 2:
                    act.wait_ge(self.l["o"], 2 * (c - 1))
                s = self.S[:, w, :]
                for b in range(TB):
                    v = s[:, 0:P] if b == 0 else s[:, P:384]
                    nc.scalar.activation(v, v, ACT.Exp, bias=sm[:, 2 * w + b:2 * w + b + 1],
                                         accum_out=sm[:, 4 + 2 * w + b:5 + 2 * w + b]).then_inc(self.l["ex"], 1)

            def turn(self, pe, g, hh):
                c, w = 4 * g + hh, hh % 2
                pe.wait_ge(self.l["ex"], 2 * c + 2)
                if c > 0:
                    pe.wait_ge(self.l["ptc"], c)
                for j in range(3):
                    m = nc.tensor.transpose(ps[:, 2, j * P:(j + 1) * P], self.S[:, w, j * P:(j + 1) * P], ident[:])
                m.then_inc(self.l["pt"], 1)

            def copy(self, act, g, hh):
                c, w = 4 * g + hh, hh % 2
                act.wait_ge(self.l["pt"], c + 1)
                if hh >= 2:
                    act.wait_ge(self.l["pv"], c - 1)
                nc.scalar.activation(self.PT[:, w, :], ps[:, 2, 0:384], ACT.Copy).then_inc(self.l["ptc"], 1)

            def values(self, pe, g, hh):
                c, w = 4 * g + hh, hh % 2
                pe.wait_ge(self.l["ptc"], c + 1)
                if c > 0:
                    pe.wait_ge(self.l["o"], 2 * c)
                pt = self.PT[:, w, :]
                nc.tensor.matmul(ps[:, 3, 0:P], pt[:, 0:P], self.v(c, 0), start=True, stop=True)
                nc.tensor.matmul(ps[:, 3, P:T], pt[:, P:T], self.v(c, 0), start=True, stop=False)
                nc.tensor.matmul(ps[:, 3, P:T], pt[:, T:384], self.v(c, 1), start=False,
                                 stop=True).then_inc(self.l["pv"], 1)

            def inverse(self, dve, own, g, hh):
                c, w = 4 * g + hh, hh % 2
                dve.wait_ge(self.l["pv"], c + 1)
                r = sm[:, 8 + 2 * w:10 + 2 * w]
                own.then(nc.vector.reciprocal(r, sm[:, 4 + 2 * w:6 + 2 * w]))
                return r

        def mla_qk(c, b):
            hh, n = c % 2, (b + 1) * P
            r = slice(hh * ROPE, (hh + 1) * ROPE)
            return [(qT0[:, hh, b * P:(b + 1) * P], kT0[:, hh, 0:n]),
                    (qrT0[r, b * P:(b + 1) * P], krT[r, 0:n])]

        mla = Heads(l0, QH ** -0.5, mask, mla_qk,
                    lambda c, b: kvw[c // 2 % 2][:, b, (c % 2) * 256 + NOPE:(c % 2) * 256 + 256], sS, sPT)

        def latent_src(k, q, s):
            z = Z_FIRST[s + 1] - Z_FIRST[s]
            if k < z:
                return TA[0], TA[1], q
            return TBf[0], TBf[1], q + 4 * ((k - z) % 2)

        def out0_src(k, q):
            return (TBf[0], TBf[1], 8 + q) if q < 8 else (TA[0], TA[1], q)

        def og0_dst(s, hl, b):
            t = TBf if s < 2 else TA
            return t[hl][:, (8 if s < 2 else 0) + 4 * s:(8 if s < 2 else 0) + 4 * s + 4, b * P:(b + 1) * P]

        def dst_l0(name, k, b, it):
            if name == "l0_in":
                return [cq[:, b, 0:LORA], cq[:, b, LORA:], krf[:, b * P:(b + 1) * P]][k]
            s = int(name[3])
            z = Z_FIRST[s + 1] - Z_FIRST[s]
            if k < z:
                return zw[Z_FIRST[s] + k][:, b, :]
            return (qw if (k - z) % 2 == 0 else kvw)[(k - z) // 2][:, b, :]

        RES = {"l0_out": 0, "l1_out": 1, "l2_out": 2, "l3_out": 3}

        def DST(name, k, b, it, eng):
            return [dst_l0, dst_l1, dst_l2, dst_l3][int(name[1])](name, k, b, it)

        def FREE(eng, name, k, it):
            [free_l0, free_l1, free_l2, free_l3][int(name[1])](eng, name, k, it)

        def free_l0(eng, name, k, it):
            if name == "l0_in":
                return
            s = int(name[3])
            z = Z_FIRST[s + 1] - Z_FIRST[s]
            if k < z:
                eng.wait_ge(l0["lat_sq"], 4)
                eng.wait_ge(rope_ok, 2)
                return
            pr = (k - z) // 2
            if (k - z) % 2 == 0:
                if 2 * s + pr - 1 > 0:
                    eng.wait_ge(l0["tr"], 2 * s + pr - 1)
                eng.wait_ge(l0["kr_pe"], 1)
            else:
                if 4 * s + 2 * pr - 2 > 0:
                    eng.wait_ge(l0["pv"], 4 * s + 2 * pr - 2)

        def z_landed(eng, s):
            at = max(i for i in range(4) if Z_FIRST[i] <= s < Z_FIRST[i + 1])
            landed(eng, f"l0_{at}", s - Z_FIRST[at])

        def l0_tile(s, pr, kind):
            return Z_FIRST[s + 1] - Z_FIRST[s] + 2 * pr + kind

        def spread(n, nu, first=0):
            return [first + i * (nu - first) // n for i in range(n)]

        L0_STAGES = 11
        L0_PHASES = ["l0_0", "l0_1", "l0_2", "l0_3", "l0_out"]

        def l0_at(name):
            return spread(L0_STAGES, 12 if name == "l0_out" else length(name))

        def l0_late(s):
            return [at + LAG for at in l0_at(L0_PHASES[s + 1])]

        A = Carve()
        qkw1 = A(2 * TB * COLS)
        qkw = [v.rearrange("p (b n) -> p b n", b=TB) for v in (qkw1[:, 0:1024], qkw1[:, 1024:2048])]
        hq = qkw1.rearrange("p (b h n) -> p b h n", b=TB, h=4)
        VW = MV + 2
        vw = A(TB, 4, VW)
        ow, zw1 = A(TB, 4 * MV), A(TB, COLS)
        PAD = 4
        cin = A(4, PAD + T)
        qkT = A(8 * T)
        qT1, kT1 = [v.rearrange("p (h t) -> p h t", t=T) for v in (qkT[:, 0:4 * T], qkT[:, 4 * T:])]
        esc = A(4 * T)
        arg = A(2, 384)
        gt = qkT[0:16, 6 * T:7 * T]
        grow = qkT[0:8, 0:6 * T].rearrange("p (a t) -> p a t", t=T)
        negM = A(T, rows=8)
        acol, emcol = A(TB, 8), A(TB, 8)
        wst = A(384)
        l1 = sems(1, "g_in g_pe g_row g_e g_m g_pe2 g_col q_pe q_c y_ok y_e q_r sc arg ex sel st nm "
                     "den h ssq var rs og ge z_ok pads")

        def dst_l1(name, k, b, it):
            if name == "l1_gates":
                return gt[:, b * P:(b + 1) * P]
            if k < 2:
                return qkw[k][:, b, :]
            if k < 4:
                return vw[:, b, 2 * (k - 2):2 * (k - 2) + 2, 0:MV]
            if k < 6:
                return ow[:, b, (k - 4) * COLS:(k - 3) * COLS]
            return zw1[:, b, :]

        def free_l1(eng, name, k, it):
            if name == "l1_gates":
                return
            s = int(name[3])
            if k < 2:
                if s > 0:
                    eng.wait_ge(l1["og"], 8 * s)
                eng.wait_ge(tr_src, 2)
            elif k < 4:
                if s > 0 or k > 3:
                    eng.wait_ge(l1["nm"], 4 * s - 2 + 2 * (k - 2))
            elif k < 6:
                if s > 0:
                    eng.wait_ge(tr_pe, L1_TURNS[s][k - 4])
            else:
                if s > 0 or k > 6:
                    eng.wait_ge(l1["z_ok"], 2 * (2 * s + k - 6))

        L1_BASE = 8 + 4 + 8 + 8
        L1_TURNS = [[0, 0], [L1_BASE + 2, L1_BASE + 4]]
        L1_AT = {"q": 11, "k": 19, "ws": [27, 33, 39, 45], "nm": [31, 37, 43, 49], "g0": 56, "t0": 60}

        def out1_src(k, q):
            return TBf[0], TBf[1], q

        A = Carve()
        qw2, fw2, vw2, gw2 = [A(TB, COLS) for _ in range(4)]
        G4 = 4 * T
        qT2, kT2, bT2 = A(4, T), A(4, T), A(4, T)
        aT = A(8, P)
        a01 = A(4, P)
        dT = A(2, G4)
        qx = A(2, 2 * T)
        l2 = sems(2, "tq tf qT nf lf kx kt ge gs dg at df ee op lv sel pv sq ss v rs on og ogp tmp hi lo")

        def dst_l2(name, k, b, it):
            return (qw2, fw2, vw2, gw2)[k][:, b, :]

        def free_l2(eng, name, k, it):
            if k < 2:
                if not first(it):
                    eng.wait_ge(l2["tf"], it)
            elif k == 2:
                if not first(it):
                    eng.wait_ge(l2["pv"], it)
            else:
                if not first(it):
                    eng.wait_ge(l2["ogp"], TB * it)

        L2_AT = {"turn": 16, "decay": 18, "diag": 21, "level": [23, 25, 27, 29, 31, 33, 35, 37], "gate": 38, "pv": 39,
                 "norm": 39, "back": 42}
        L2_OWN, L3_OWN = 4, 4

        def group(first, g, n=4):
            return slice(first + n * g, first + n * g + n) if isinstance(g, int) else bass.ds(first + n * g, n)

        def heads_of(t, g, b):
            return t[:, group(0, g), b * P:(b + 1) * P]

        def query_banks(p):
            return {1: (0, 1), 2: (2, 3), 3: (4,), 4: (5,), 5: (6,), 6: (7,)}.get(p, ())

        A = Carve()
        kT3, v3 = A(H2, T), A(TB, D)
        qw3, gw3 = A(TB, COLS), A(TB, COLS)
        qT3 = A(4, T)
        S3, PT3 = A(2, 384), A(2, 384)
        o3 = A(TB, COLS)
        negF = ones[0:16, 0:T]
        frow = kT3[0:16, 8:12, :]
        ft = kT3[0:16, 12, :]
        sqj = A(P)
        l3 = sems(3, "f_row f_e f_ok ksq kv_ krs kn kt kT qsq qv qrs qn qt qT sc msk mx ex pt ptc pv o "
                     "ge gs sq v rs on og ogp tmp hi lo")

        def dst_l3(name, k, b, it):
            if name == "l3_f":
                return ft[:, b * P:(b + 1) * P]
            if name == "l3_kv" and k == 1:
                return v3[:, b, group_cols(it)]
            return (qw3, gw3)[k][:, b, :]

        def group_cols(it):
            return slice(COLS * it, COLS * it + COLS) if isinstance(it, int) else bass.ds(COLS * it, COLS)

        def free_l3(eng, name, k, it):
            if name == "l3_f":
                return
            if k == 0:
                if name == "l3_kv":
                    if not first(it):
                        eng.wait_ge(l3["kt"], it)
                    eng.wait_ge(tr_lo, T3 - 4 if first(it) else T3)
                else:
                    eng.wait_ge(l3["kt"], 4)
                    if not first(it):
                        eng.wait_ge(l3["qt"], it)
            elif name == "l3_kv":
                eng.wait_ge(tr_lo, T3)
            else:
                if not first(it):
                    eng.wait_ge(l3["og"], it)

        T3 = L1_BASE + 8 + 8 + 16
        L3_AT = {"norm": 8, "turn": 12, "sc0": 13, "t0": 15, "v0": 16, "gate": (16, 18), "v1": 18, "t2": 20, "v2": 21,
                 "v3": 22, "post": 22, "back": 25}

        def fox_qk(c, b):
            hh, n = c % 4, (b + 1) * P
            return [(qT3[:, hh, b * P:(b + 1) * P], kT3[:, c, 0:n]),
                    (ident[0:16, c:c + 1].to_broadcast([16, P]), negF[:, 0:n])]

        fox = Heads(l3, 1.0, mask, fox_qk, lambda c, b: v3[:, b, c * HD:(c + 1) * HD], S3, PT3)
        block = ctx.enter_context(nc.Block())

        @block.sync
        def _(sp):
            for b in range(TB):
                sp.dma_start(x_res[:, b, :], a["x"][0, b * P:(b + 1) * P, :]).then_inc(x_in[b], 16)

            def load(name, p, it=0):
                tiles = PHD[name][1]
                k, q = places(tiles)[p]
                view, kt, c0, step, w = tiles[k]
                nu, n = units(tiles), UNIT[name] + p
                if n >= RAW:
                    sp.wait_ge(w_low, n - RAW + 1 + nu * it)
                c = c0 + it * step
                cols = slice(c, c + w) if isinstance(it, int) else bass.ds(c, w)
                sp.dma_start(wraw[:, n % RAW, :, 0:w], view[:, q:q + KU, cols]).then_inc(w_loaded[n % RAW], 16)

            for name, tiles, runs in PH:
                if runs == 1:
                    for p in range(units(tiles)):
                        load(name, p)
                else:
                    with sp.Fori(0, runs) as it:
                        for p in range(units(tiles)):
                            load(name, p, it)
            for k in range(4):
                for b, done in enumerate((out_b0, out_b1)):
                    sp.wait_ge(done, TILE["l3_out"] + k + 1)
                    sp.dma_start(out[0, b * P:(b + 1) * P, k * COLS:(k + 1) * COLS],
                                 x_res[:, b, k * COLS:(k + 1) * COLS]).then_inc(st_out, 16)
            sp.wait_ge(st_out, 16 * 4 * TB)

        @block.gpsimd
        def _(pool):
            own = Own(pool, pool_own)
            own.then(nc.gpsimd.memset(ident[:], 0.0))
            nc.gpsimd.affine_select(out=ident[:], in_=ident[:], compare_op=ALU.not_equal, fill=1.0, base=0,
                                    pattern=[[-1, P]], channel_multiplier=1).then_inc(ident_ok, 1)
            own.mark(nc.gpsimd.memset(eps_col, EPS))
            pool.dma_start(stage_rows[0:4, 0, :],
                           a["mla_q_norm"].rearrange("o (k p) -> (o k) p", p=P)).then_inc(par_in, 16)
            pool.dma_start(stage_rows[4:8, 0, :],
                           a["mla_kv_norm"].rearrange("o (k p) -> (o k) p", p=P)).then_inc(par_in, 16)
            pool.dma_start(stage_rows[8:72, 0, :],
                           a["ml_conv_w"].rearrange("o w (k p) -> (o w k) p", p=P)).then_inc(par_in, 16)
            pool.dma_start(stage_rows[72:88, 0, :],
                           a["ml_conv_b"].rearrange("o (k p) -> (o k) p", p=P)).then_inc(par_in, 16)
            pool.dma_start(stage_rows[88:104, 0, :],
                           a["ml_head_norm"].rearrange("o (k p) -> (o k) p", p=P)).then_inc(par_in, 16)
            for i, k in enumerate(("a_norm_w_2", "a_out_norm_w_2", "kv_norm_w_2", "b_norm_w_2", "b_out_norm_w_2")):
                v = a[k] if len(a[k].shape) == 2 else a[k].rearrange("(o n) -> o n", o=1)
                pool.dma_start(stage_rows[16 * i:16 * i + 16, 1, :],
                               v.rearrange("o (k p) -> (o k) p", p=P)).then_inc(par_in, 16)
            pool.dma_start(stage_rows[80:81, 1, :], a["k_norm_w_2"].rearrange("(o n) -> o n", o=1)).then_inc(par_in, 16)
            pool.dma_start(stage_rows[81:82, 1, :], a["b_q_norm_w_2"]).then_inc(par_in, 16)
            with nc.allow_non_contiguous_dma(reason="256 positions"):
                pool.dma_start(posi[:], a["positions"].rearrange("o (b p) -> p (o b)", p=P)).then_inc(bias_in, 16)
            with nc.allow_non_contiguous_dma(reason="two columns of 16"):
                pool.dma_start(gbias[:, 0:1], a["ml_gate_b"].rearrange("o n -> n o")).then_inc(bias_in, 16)
                pool.dma_start(gbias[:, 1:2], a["kv_f_bias_2"].rearrange("(n o) -> n o", o=1)).then_inc(bias_in, 16)
            own.mark(nc.gpsimd.memset(ones[:], 1.0))
            own.mark(nc.gpsimd.memset(mask[:], 0.0))
            own.mark(nc.gpsimd.memset(lvf, 1.0))
            for i in range(32):
                f = float(np.float32(THETA) ** (-np.float32(2 * i) / np.float32(ROPE)))
                own.mark(nc.gpsimd.memset(invf[:, i:i + 1], f))
            own.sync()
            for part in (slice(0, P), slice(T, 384)):
                own.mark(nc.gpsimd.memset(mask[0:64, part.start + 64:part.stop], NEG))
            for i in range(7):
                h = 64 >> i
                v = lvf[:, i, :].rearrange("p (n r) -> p n r", r=h)
                own.then(nc.gpsimd.affine_select(out=v, in_=v, compare_op=ALU.is_ge, fill=0.0, base=0,
                                                 pattern=[[-2 * h, 64 // h], [0, h]], channel_multiplier=1))
                own.then(nc.gpsimd.affine_select(out=v, in_=v, compare_op=ALU.is_ge, fill=0.0, base=h - 1,
                                                 pattern=[[2 * h, 64 // h], [0, h]], channel_multiplier=-1))
                own.mark(nc.gpsimd.tensor_copy(lvl[:, i, :], lvf[:, i, :]))
            own.sync()
            nc.gpsimd.memset(posf[:, 2:3], 0.0).then_inc(const_ok, 1)
            pool.wait_ge(tr_src, 2)
            own.mark(nc.gpsimd.memset(cin[:, :, 0:PAD], 0.0))
            own.mark(nc.gpsimd.memset(mask[:], 0.0))
            own.mark(nc.gpsimd.memset(vw[:, :, :, MV:VW], 1.0))
            own.sync()
            for part in (slice(0, P), slice(T, 384)):
                nc.gpsimd.affine_select(out=mask[:, part], in_=mask[:, part], compare_op=ALU.is_ge, fill=NEG, base=0,
                                        pattern=[[-1, P]], channel_multiplier=1).then_inc(l1["pads"], 1)
            for c in range(H1):
                pool.wait_ge(l1["ex"], c + 1)
                for part in (slice(0, P), slice(T, 384)):
                    v = arg[:, c % 2, part]
                    nc.gpsimd.affine_select(out=v, in_=v, compare_op=ALU.is_ge, fill=0.0, base=0,
                                            pattern=[[1, P]], channel_multiplier=-1).then_inc(l1["sel"], 1)

        @block.scalar
        def _(act):
            own = Own(act, act_own)
            turn = Turn()
            def turn_x(dst, weighted, b):
                for q in range(4):
                    turn_act(act, turn, dst[0][:, 4 * q:4 * q + 4, b * P:(b + 1) * P], weighted)

            def first_step(name, dst, weighted):
                turn_x(dst, weighted, 0)
                for p in range(SPLIT):
                    step(act, high, evac, name, p)
                turn_x(dst, weighted, 1)

            def rstd(v, lnv, r):
                own.then(nc.scalar.activation(lnv, v, ACT.Ln))
                return nc.scalar.activation(r, lnv, ACT.Exp, scale=-0.5)

            def evac(name, k, it=0):
                if name in RES:
                    return
                FREE(act, name, k, it)
                evac_act(act, name, k, DST(name, k, 0, it, act), it)

            def norm_scalars(n):
                act.wait_ge(nrm_v, n + 1)
                rstd(nrm[:, :, 0], nrm[:, :, 1], nrm[:, :, 2]).then_inc(nrm_a, 1)

            first_step("l0_in", TA, False)
            for p in range(SPLIT, length("l0_in")):
                step(act, high, evac, "l0_in", p)
                if p == 12 + LAG:
                    act.wait_ge(rope_arg, 2)
                    nc.scalar.activation(sin.rearrange("p a b -> p (a b)"), angle[:, 4, :], ACT.Sin).then_inc(rope_ok, 1)
                    nc.scalar.activation(cos.rearrange("p a b -> p (a b)"), angle[:, 5, :], ACT.Sin).then_inc(rope_ok, 1)
                    nc.scalar.add_instruction(mybir.InstLoadActFuncSet(
                        name=nc.get_next_instruction_name(), engine=mybir.EngineType.Activation,
                        act_func_set_id=LN_EXP_SET, ins=[], outs=[]))

            def latents():
                landed(act, "l0_in", 1)
                for j in range(2):
                    for b in range(TB):
                        nc.scalar.activation(zw[2 + j][:, b, :], cq[:, b, j * LORA:(j + 1) * LORA], ACT.Square,
                                             accum_out=sm[:,
                                                          SMALL + 2 * j + b:SMALL + 2 * j + b + 1]).then_inc(l0["lat_sq"], 1)

            def latents2():
                act.wait_ge(l0["lat_v"], 1)
                rstd(sm[:, SMALL + 4:SMALL + 8], sm[:, SMALL + 8:SMALL + 12],
                     sm[:, SMALL + 12:SMALL + 16]).then_inc(l0["lat_r"], 1)

            def latents3():
                act.wait_ge(l0["kr_pe"], 1)
                nc.scalar.activation(krT, ps[:, 0, 0:T], ACT.Copy).then_inc(l0["kr_T"], 1)
                for j in range(2):
                    for b in range(TB):
                        turn_act(act, turn, TBf[0][:, 4 * j:4 * j + 4, b * P:(b + 1) * P], True)

            def ln_params(layer):
                act.wait_ge(tr_lo, turn.n)
                act.dma_start(lnw, a["ln_w"][layer:layer + 1, :].to_broadcast([P, D])).then_inc(lnp_in, 16)
                act.dma_start(lnb, a["ln_b"][layer:layer + 1, :].to_broadcast([P, D])).then_inc(lnp_in, 16)

            def l0_side(s, p, at):
                def z_exp():
                    z_landed(act, s)
                    if s > 0:
                        act.wait_ge(l0["z_ok"], s)
                    act.wait_ge(tr_pe, turn.n)
                    own.then(nc.scalar.activation(ez, zw[s], ACT.Exp, scale=-1.0))
                    own.then(nc.scalar.activation(ez, ez, ACT.Ln, bias=1.0))
                    nc.scalar.activation(ez, ez, ACT.Exp, scale=-1.0).then_inc(l0["z_e"], 1)

                def pair(pr):
                    c2 = 2 * s + pr
                    act.wait_ge(l0["tr"], c2 + 1)
                    if c2 > 0:
                        act.wait_ge(l0["sc"], 2 * c2)
                    nc.scalar.activation(qT0.rearrange("p a t -> p (a t)"), ps[:, 0, :], ACT.Copy).then_inc(l0["trA"], 1)
                    nc.scalar.activation(qrT0, ps[:, 2, 0:T], ACT.Copy).then_inc(l0["trA"], 1)

                def back():
                    for b in range(TB):
                        turn_act(act, turn, og0_dst(s, 0, b), False)

                if p == at[0]:
                    z_exp()
                if p == at[1]:
                    pair(0)
                if p == at[2]:
                    mla.weights(act, s, 0)
                    mla.weights(act, s, 1)
                if p == at[3]:
                    mla.copy(act, s, 0)
                if p == at[4]:
                    mla.copy(act, s, 1)
                if p == at[5]:
                    pair(1)
                if p == at[6]:
                    mla.weights(act, s, 2)
                    mla.weights(act, s, 3)
                if p == at[7]:
                    mla.copy(act, s, 2)
                if p == at[8]:
                    mla.copy(act, s, 3)
                if p == at[10]:
                    back()

            for p in range(length("l0_0")):
                step(act, high, evac, "l0_0", p, 0, ("l0_in", 0))
                if p == 4:
                    latents()
                if p == 6:
                    latents2()
                if p == 10:
                    latents3()
            for s in range(1, 5):
                name = L0_PHASES[s]
                for p in range(length(name)):
                    step(act, high, evac, name, p, 0, (L0_PHASES[s - 1], 0))
                    if s >= 2:
                        l0_side(s - 2, p + length(L0_PHASES[s - 1]), l0_late(s - 2))
                    l0_side(s - 1, p, l0_late(s - 1))
                    if name == "l0_out" and p == 22:
                        ln_params(0)

            norm_scalars(0)

            first_step("l1_gates", TA, False)
            for p in range(SPLIT, length("l1_gates")):
                step(act, high, evac, "l1_gates", p)

            def gates_b():
                act.wait_ge(l1["g_row"], 2)
                own.then(nc.scalar.activation(grow[:, 5, :], grow[:, 5, :], ACT.Exp))
                nc.scalar.activation(grow[:, 5, :], grow[:, 5, :], ACT.Ln, bias=1.0).then_inc(l1["g_e"], 1)

            def gates_c():
                act.wait_ge(l1["g_pe2"], 1)
                act.wait_ge(l1["g_col"], 1)
                nc.scalar.activation(emcol, ps[:, 3, 16:32].rearrange("p (b h) -> p b h", b=TB), ACT.Exp,
                                     scale=-1.0).then_inc(l1["g_col"], 1)

            def window_in(s, j):
                n = 2 * s + j
                act.wait_ge(l1["q_pe"], n + 1)
                if n > 0:
                    act.wait_ge(l1["y_ok"], 4 * n)
                act.wait_ge(l1["pads"], 2)
                nc.scalar.activation(cin[:, :, PAD:], ps2(0).rearrange("p (h t) -> p h t", t=T),
                                     ACT.Copy).then_inc(l1["q_c"], 1)

            def conv_sigmoid(s, j):
                n = 2 * s + j
                act.wait_ge(l1["y_ok"], 4 * n + 4)
                y = (qT1, kT1)[j].rearrange("p h t -> p (h t)")
                if s > 0:
                    act.wait_ge(l1["z_ok"], 4 * s)
                if n > 0:
                    act.wait_ge(l1["q_r"], n)
                own.then(nc.scalar.activation(esc, y, ACT.Exp, scale=-1.0))
                own.then(nc.scalar.activation(esc, esc, ACT.Ln, bias=1.0))
                nc.scalar.activation(esc, esc, ACT.Exp, scale=-1.0).then_inc(l1["y_e"], 1)

            def weigh(s, c):
                act.wait_ge(l1["arg"], 2 * c + 2)
                nc.scalar.activation(arg[:, c % 2, :], arg[:, c % 2, :], ACT.Exp).then_inc(l1["ex"], 1)

            def cell(s, c):
                act.wait_ge(l1["den"], c + 1)
                for b in range(TB):
                    if c > 0:
                        act.wait_ge(l1["rs"], c)
                    r = sm[:, 16 + 2 * (c % 2) + b:17 + 2 * (c % 2) + b]
                    nc.scalar.activation(hq[:, b, c % 4, :], ps[:, 2 + b, 0:MV], ACT.Copy, scale=r).then_inc(l1["h"], 1)
                act.wait_ge(l1["h"], 2 * c + 2)
                for b in range(TB):
                    nc.scalar.activation(esc[:, b * MV:(b + 1) * MV], hq[:, b, c % 4, :], ACT.Square,
                                         accum_out=sm[:, 20 + b:21 + b]).then_inc(l1["ssq"], 1)
                act.wait_ge(l1["var"], c + 1)
                if s > 0:
                    act.wait_ge(l1["og"], 8 * (s - 1) + 4 * (c % 4 // 2 + 1))
                rstd(sm[:, 24:26], sm[:, 26:28], sm[:, 28 + 2 * (c % 4):30 + 2 * (c % 4)]).then_inc(l1["rs"], 1)

            def gate_exp(s, j, b):
                landed(act, f"l1_{s}", 6 + j)
                act.wait_ge(l1["rs"], 4 * s + 4)
                if s or j or b:
                    act.wait_ge(l1["z_ok"], 2 * (2 * s + j) + b)
                own.mark(nc.scalar.activation(esc[:, 0:COLS], ow[:, b, j * COLS:(j + 1) * COLS], ACT.Exp, scale=-1.0))
                own.then(nc.scalar.activation(esc[:, COLS:], zw1[:, b, :], ACT.Exp, scale=-1.0))
                own.then(nc.scalar.activation(esc, esc, ACT.Ln, bias=1.0))
                nc.scalar.activation(esc, esc, ACT.Exp, scale=-1.0).then_inc(l1["ge"], 1)

            def gated_turn(s, j):
                for b in range(TB):
                    k = 8 * s + 4 * j
                    turn_act(act, turn, TBf[0][:, k:k + 4, b * P:(b + 1) * P], True)

            def l1_side(s, p):
                if s == 0 and p == late("l1_0", 5):
                    gates_b()
                if s == 0 and p == late("l1_0", 8):
                    gates_c()
                if s == 1:
                    l1_rest(0, p)
                for j in range(2):
                    if p == late("l1_0", L1_AT["qk"[j]]):
                        window_in(s, j)
                    if p == late("l1_0", L1_AT["qk"[j]]) + 3:
                        conv_sigmoid(s, j)
                for h in range(4):
                    if p == late("l1_0", L1_AT["ws"][h]):
                        weigh(s, 4 * s + h)
                    if p == late("l1_0", L1_AT["nm"][h]):
                        cell(s, 4 * s + h)
                for b in range(TB):
                    if p == late("l1_0", L1_AT["g0"] + 2 * b):
                        gate_exp(s, 0, b)
                if p == late("l1_0", L1_AT["t0"]):
                    gated_turn(s, 0)

            def l1_rest(s, p):
                for b in range(TB):
                    if p == 3 + 2 * b:
                        gate_exp(s, 1, b)
                if p == 6 + LAG:
                    gated_turn(s, 1)

            for s in range(2):
                for p in range(length("l1_0")):
                    step(act, high, evac, f"l1_{s}", p, 0, (("l1_gates", "l1_0")[s], 0))
                    l1_side(s, p)
            for p in range(length("l1_out")):
                step(act, high, evac, "l1_out", p, 0, ("l1_1", 0))
                l1_rest(1, p)
                if p == 22:
                    ln_params(1)
            norm_scalars(1)

            for b in range(TB):
                act.wait_ge(tr_src, 2 + b + 1)
                own.then(nc.scalar.activation(hn[:, b, :], x_res[:, b, :], ACT.Square, accum_out=nrm[:, b, 3:4]))
                own.then(nc.scalar.activation(nrm[:, b, 1:2], nrm[:, b, 3:4], ACT.Ln, scale=1.0 / D, bias=eps_col))
                nc.scalar.activation(nrm[:, b, 2:3], nrm[:, b, 1:2], ACT.Exp, scale=-0.5).then_inc(nrm_a, 1)

            first_step("l2", TA, True)

            def l2_side(g, u):
                def turned():
                    act.wait_ge(l2["tq"], 1 + g)
                    nc.scalar.activation(qT2.rearrange("p h t -> p (h t)"), ps2(0), ACT.Copy).then_inc(l2["qT"], 1)
                    act.wait_ge(l2["nf"], 1 + g)
                    nc.scalar.activation(dT[:, 0, :], dT[:, 0, :], ACT.Exp).then_inc(l2["lf"], 1)
                    act.wait_ge(l2["lf"], 1 + 2 * g)
                    nc.scalar.activation(dT[:, 0, :], dT[:, 0, :], ACT.Ln, bias=1.0).then_inc(l2["lf"], 1)

                def gate():
                    landed(act, "l2", 3, g)
                    act.wait_ge(l2["lv"], 8 + 8 * g)
                    e = qx.rearrange("p a n -> p (a n)")
                    nc.scalar.activation(e, gw2.rearrange("p b n -> p (b n)"), ACT.Exp, scale=-1.0).then_inc(l2["ge"], 1)
                    act.wait_ge(l2["ge"], 1 + 3 * g)
                    nc.scalar.activation(e, e, ACT.Ln, bias=1.0).then_inc(l2["ge"], 1)
                    act.wait_ge(l2["ge"], 2 + 3 * g)
                    nc.scalar.activation(e, e, ACT.Exp, scale=-1.0).then_inc(l2["ge"], 1)

                def diag():
                    act.wait_ge(l2["kx"], 4 + 4 * g)
                    nc.scalar.activation(kT2.rearrange("p h t -> p (h t)"), dT[:, 0, :], ACT.Exp).then_inc(l2["kt"], 1)
                    decays(0)
                    decays(1)

                def decays(j):
                    if j > 7:
                        return
                    h = P >> j
                    act.wait_ge(l2["df"], j + 1 + 8 * g)
                    d = dT[:, j % 2, :].rearrange("p (n c r) -> p n c r", c=2, r=h)
                    for c in (0, 1):
                        nc.scalar.activation(d[:, :, c, :], d[:, :, c, :], ACT.Exp,
                                             scale=(-1.0, 1.0)[c]).then_inc(l2["ee"], 1)

                def norm():
                    act.wait_ge(l2["pv"], 1 + g)
                    for b in range(TB):
                        nc.scalar.activation(dT[:, 0, b * COLS:(b + 1) * COLS], ps[:, b, :],
                                             ACT.Square).then_inc(l2["sq"], 1)
                    act.wait_ge(l2["v"], 1 + g)
                    nc.scalar.activation(sm[:, 40:48], sm[:, 32:40], ACT.Ln).then_inc(l2["rs"], 1)
                    act.wait_ge(l2["rs"], 1 + 2 * g)
                    nc.scalar.activation(sm[:, 48:56], sm[:, 40:48], ACT.Exp, scale=-0.5).then_inc(l2["rs"], 1)

                def back():
                    for b in range(TB):
                        act.wait_ge(l2["tmp"], b + 1 + TB * g)
                        nc.scalar.activation(heads_of(TBf[0], g, b), tmpT[:, b, :].rearrange("p (k t) -> p k t", t=P),
                                             ACT.Copy).then_inc(l2["hi"], 1)

                if u == L2_AT["turn"] + LAG:
                    turned()
                if u == L2_AT["diag"] + LAG:
                    diag()
                for j in range(8):
                    if u == L2_AT["level"][j] + LAG:
                        decays(j + 2)
                if u == L2_AT["gate"] + LAG:
                    gate()
                if u == L2_AT["norm"] + LAG:
                    norm()
                if u == L2_AT["back"] + LAG:
                    back()

            for p in range(SPLIT, length("l2")):
                step(act, high, evac, "l2", p)
                l2_side(0, p)
            with act.Fori(1, 4) as it:
                for p in range(length("l2")):
                    step(act, high, evac, "l2", p, it, ("l2", it - 1))
                    l2_side(it - 1, p + length("l2"))
                    l2_side(it, p)
            for p in range(length("l2_out")):
                step(act, high, evac, "l2_out", p, 0, ("l2", 3))
                l2_side(3, p + length("l2"))
            norm_scalars(2)

            first_step("l3_f", TA, True)

            def forget():
                act.wait_ge(l3["f_row"], 1)
                nc.scalar.activation(frow[:, 1, :], frow[:, 1, :], ACT.Exp).then_inc(l3["f_e"], 1)
                act.wait_ge(l3["f_e"], 1)
                nc.scalar.activation(frow[:, 1, :], frow[:, 1, :], ACT.Ln, bias=1.0).then_inc(l3["f_e"], 1)

            def squares(pre, src, g):
                for b in range(TB):
                    for h in range(4):
                        n = 8 * g + 4 * b + h
                        if b or h:
                            act.wait_ge(l3[pre + "sq"], n)
                        nc.scalar.activation(sqj, src[:, b, h * HD:(h + 1) * HD], ACT.Square,
                                             accum_out=sm[:, 32 + 4 * b + h:33 + 4 * b + h]).then_inc(l3[pre + "sq"], 1)

            def inverse_root(v, rs, g):
                act.wait_ge(v, g + 1)
                nc.scalar.activation(sm[:, 40:48], sm[:, 32:40], ACT.Ln).then_inc(rs, 1)
                act.wait_ge(rs, 2 * g + 1)
                nc.scalar.activation(sm[:, 48:56], sm[:, 40:48], ACT.Exp, scale=-0.5).then_inc(rs, 1)

            def kv_side(g, p):
                def norm():
                    landed(act, "l3_kv", 0, g)
                    squares("k", qw3, g)
                    inverse_root(l3["kv_"], l3["krs"], g)

                def keys():
                    act.wait_ge(l3["kt"], g + 1)
                    act.wait_ge(l3["f_ok"], 2)
                    nc.scalar.activation(kT3[:, group(0, g), :].rearrange("p h t -> p (h t)"), ps2(0), ACT.Copy,
                                         scale=colB[:, 80:81]).then_inc(l3["kT"], 1)
                if p == late("l3_kv", 0):
                    norm()
                if p == late("l3_kv", 5):
                    keys()

            for p in range(SPLIT, length("l3_f")):
                step(act, high, evac, "l3_f", p)
            for p in range(length("l3_kv")):
                step(act, high, evac, "l3_kv", p, 0, ("l3_f", 0))
                if p == 12:
                    forget()
                for n in query_banks(p - LAG):
                    b, q = n // 4, n % 4
                    turn_act(act, turn, TBf[0][:, 4 * q:4 * q + 4, b * P:(b + 1) * P], True)
            with act.Fori(1, 4) as it:
                for p in range(length("l3_kv")):
                    step(act, high, evac, "l3_kv", p, it, ("l3_kv", it - 1))
                    kv_side(it - 1, p)

            def q_side(g, u):
                c = 4 * g

                def norm():
                    landed(act, "l3_q", 0, g)
                    squares("q", qw3, g)
                    inverse_root(l3["qv"], l3["qrs"], g)

                def turned():
                    act.wait_ge(l3["qt"], g + 1)
                    nc.scalar.activation(qT3.rearrange("p h t -> p (h t)"), ps2(0), ACT.Copy,
                                         scale=sm[:, 56:57]).then_inc(l3["qT"], 1)

                def post():
                    act.wait_ge(l3["o"], 2 * (c + 4))
                    act.wait_ge(l3["qn"], 2 * g + 2)
                    for b in range(TB):
                        for h in range(4):
                            if b or h:
                                act.wait_ge(l3["sq"], 8 * g + 4 * b + h)
                            nc.scalar.activation(sqj, o3[:, b, h * HD:(h + 1) * HD], ACT.Square,
                                                 accum_out=sm[:, 32 + 4 * b + h:33 + 4 * b + h]).then_inc(l3["sq"], 1)
                    inverse_root(l3["v"], l3["rs"], g)

                def gate(b):
                    if b == 0:
                        landed(act, "l3_q", 1, g)
                    else:
                        act.wait_ge(l3["gs"], 2 * g + b)
                    e = tmpT[:, 0, :]
                    nc.scalar.activation(e, gw3[:, b, :], ACT.Exp, scale=-1.0).then_inc(l3["ge"], 1)
                    act.wait_ge(l3["ge"], 3 * (2 * g + b) + 1)
                    nc.scalar.activation(e, e, ACT.Ln, bias=1.0).then_inc(l3["ge"], 1)
                    act.wait_ge(l3["ge"], 3 * (2 * g + b) + 2)
                    nc.scalar.activation(e, e, ACT.Exp, scale=-1.0).then_inc(l3["ge"], 1)

                def back():
                    for b in range(TB):
                        act.wait_ge(l3["tmp"], 2 * g + b + 1)
                        nc.scalar.activation(heads_of(TA[0], g, b), tmpT[:, b, :].rearrange("p (k t) -> p k t", t=P),
                                             ACT.Copy).then_inc(l3["hi"], 1)

                for b in range(TB):
                    if u == L3_AT["gate"][b] + LAG:
                        gate(b)
                if u == L3_AT["norm"] + LAG:
                    norm()
                if u == L3_AT["turn"] + LAG:
                    turned()
                if u == L3_AT["sc0"] + LAG:
                    fox.weights(act, g, 0)
                    fox.weights(act, g, 1)
                if u == L3_AT["t0"] + LAG:
                    fox.copy(act, g, 0)
                if u == L3_AT["v0"] + LAG:
                    fox.copy(act, g, 1)
                if u == L3_AT["v1"] + LAG:
                    fox.weights(act, g, 2)
                    fox.weights(act, g, 3)
                if u == L3_AT["t2"] + LAG:
                    fox.copy(act, g, 2)
                if u == L3_AT["v2"] + LAG:
                    fox.copy(act, g, 3)
                if u == L3_AT["post"] + LAG:
                    post()
                if u == L3_AT["back"] + LAG:
                    back()

            for p in range(length("l3_q")):
                step(act, high, evac, "l3_q", p, 0, ("l3_kv", 3))
                kv_side(3, p)
                q_side(0, p)
            with act.Fori(1, 4) as it:
                for p in range(length("l3_q")):
                    step(act, high, evac, "l3_q", p, it, ("l3_q", it - 1))
                    q_side(it - 1, p + length("l3_q"))
                    q_side(it, p)
            for p in range(length("l3_out")):
                step(act, high, evac, "l3_out", p, 0, ("l3_q", 3))
                q_side(3, p + length("l3_q"))

        @block.vector
        def _(dve):
            own = Own(dve, dve_own)
            turn = Turn()
            def constants():
                dve.wait_ge(const_ok, 1)
                dve.wait_ge(bias_in, 48)
                dve.wait_ge(col_pe, 1)
                nc.vector.tensor_copy(colA[:], ps[:, 0, 0:NA_ROWS]).then_inc(col_ok, 1)
                nc.vector.tensor_copy(colB[:], ps[:, 0, P:P + NB_ROWS]).then_inc(col_ok, 1)
                dve.wait_ge(col_ok, 2)
                own.then(nc.vector.tensor_copy(posf[:, 0:TB], posi[:]))
                two_pi, magic = 2 * np.pi, float(1.5 * 2 ** 23)
                c1 = 6.28125
                c2 = float(np.float32(np.round((two_pi - c1) * 2 ** 22) / 2 ** 22))
                c3 = float(np.float32(two_pi - c1 - c2))
                for b in range(TB):
                    own.mark(nc.vector.tensor_scalar(angle[:, 0, 32 * b:32 * b + 32], invf, posf[:, b:b + 1], None,
                                                     ALU.mult))
                own.sync()
                for j, quarter in ((0, 0.0), (1, 0.25)):
                    k, r = angle[:, 1, :], angle[:, 4 + j, :]
                    own.then(nc.vector.tensor_scalar(k, angle[:, 0, :], float(1 / two_pi), quarter, ALU.mult, ALU.add))
                    own.then(nc.vector.tensor_scalar(k, k, magic, None, ALU.add))
                    own.then(nc.vector.tensor_scalar(k, k, -magic, None, ALU.add))
                    own.then(nc.vector.scalar_tensor_tensor(r, k, -c1, angle[:, 0, :], ALU.mult, ALU.add))
                    own.then(nc.vector.scalar_tensor_tensor(r, k, -c2, r, ALU.mult, ALU.add))
                    own.then(nc.vector.scalar_tensor_tensor(r, k, -c3, r, ALU.mult, ALU.add))
                    if j:
                        own.then(nc.vector.tensor_scalar(r, r, float(np.pi / 2), None, ALU.add))
                    nc.vector.tensor_scalar(r, r, 3.1415925, -3.1415925, ALU.min, ALU.max).then_inc(rope_arg, 1)

            def turn_x(dst, col, b):
                for q in range(4):
                    turn_dve(dve, turn, dst[0][:, 4 * q:4 * q + 4, b * P:(b + 1) * P],
                             dst[1][:, 4 * q:4 * q + 4, b * P:(b + 1) * P],
                             None if col is None else col[:, 4 * q:4 * q + 4])

            def first_step(name, dst, col=None):
                turn_x(dst, col, 0)
                for p in range(SPLIT):
                    step(dve, low, evac, name, p)
                turn_x(dst, col, 1)

            def residual(name, k):
                al = ALPHA if RES[name] < 2 else 1.0
                c = slice(k * COLS, (k + 1) * COLS)
                for b, done in enumerate((out_b0, out_b1)):
                    if k == 3 and b == 0:
                        dve.wait_ge(half_used, RES[name] + 1)
                    else:
                        tile_done(dve, name, k)
                    nc.vector.scalar_tensor_tensor(x_res[:, b, c], x_res[:, b, c], al,
                                                   acc[:, (TILE[name] + k) % 2, b, :],
                                                   ALU.mult, ALU.add).then_inc(done, 1)
                    if RES[name] < 3 and k == 3:
                        dve.wait_ge(done, TILE[name] + k + 1)
                        nc.vector.bn_stats(bstat[:, b, k, :], x_res[:, b, c]).then_inc(x_done, 1)
                if RES[name] < 3 and k < 3:
                    for b, done in enumerate((out_b0, out_b1)):
                        dve.wait_ge(done, TILE[name] + k + 1)
                        nc.vector.bn_stats(bstat[:, b, k, :], x_res[:, b, c]).then_inc(x_done, 1)

            def evac(name, k, it=0):
                if name in RES:
                    return residual(name, k)
                FREE(dve, name, k, it)
                evac_dve(dve, name, k, DST(name, k, 1, it, dve), it)

            def statistics(n):
                dve.wait_ge(x_done, 8 * (n + 1))
                for b in range(TB):
                    own.mark(nc.vector.bn_aggr(mv[:, b, :], bstat[:, b, :, :].rearrange("p k s -> p (k s)")))
                own.sync()

            def layer_norm(n):
                statistics(n)
                nc.vector.tensor_scalar(nrm[:, :, 0], mv[:, :, 1], EPS, None, ALU.add).then_inc(nrm_v, 1)
                dve.wait_ge(lnp_in, 32 * (n + 1))
                for b in range(TB):
                    own.mark(nc.vector.scalar_tensor_tensor(x_res[:, b, :], x_res[:, b, :], mv[:, b, 0:1], lnw,
                                                            ALU.subtract, ALU.mult))
                own.sync()
                dve.wait_ge(nrm_a, n + 1)
                for b in range(TB):
                    nc.vector.scalar_tensor_tensor(x_res[:, b, :], x_res[:, b, :], nrm[:, b, 2:3], lnb, ALU.mult,
                                                   ALU.add).then_inc(tr_src, 1)

            first_step("l0_in", TA)
            for p in range(SPLIT, length("l0_in")):
                step(dve, low, evac, "l0_in", p)
                if p == 8 + LAG:
                    constants()

            def rotate(dst, x1, x2, n, heads):
                t = [rt[:, i, 0:TB * heads * 32].rearrange("p (b h f) -> p b h f", b=TB, f=32) for i in range(4)]
                cs = cos.unsqueeze(2).to_broadcast([P, TB, heads, 32])
                sn = sin.unsqueeze(2).to_broadcast([P, TB, heads, 32])
                for i, (x, y) in enumerate(((x1, cs), (x2, sn), (x1, sn), (x2, cs))):
                    own.mark(nc.vector.tensor_tensor(t[i], x, y, ALU.mult))
                own.sync()
                nc.vector.tensor_tensor(dst[..., 0:32], t[0], t[1], ALU.subtract).then_inc(*n)
                nc.vector.tensor_tensor(dst[..., 32:64], t[2], t[3], ALU.add).then_inc(*n)

            def latents():
                dve.wait_ge(l0["kr_in"], 1)
                own.then(nc.vector.tensor_copy(krw, ps[:, 0, 0:2 * ROPE].rearrange("p (b n) -> p b n", b=TB)))
                dve.wait_ge(rope_ok, 2)
                k4 = krw.unsqueeze(2)
                rotate(krd[:, :, 0:1, :], k4[..., 0:32], k4[..., 32:64], (l0["kr_ok"], 1), 1)
                dve.wait_ge(l0["kr_ok"], 2)
                nc.vector.tensor_copy(krd[:, :, 1, :], krd[:, :, 0, :]).then_inc(l0["kr_ok"], 1)
                dve.wait_ge(l0["lat_sq"], 4)
                nc.vector.tensor_scalar(sm[:, SMALL + 4:SMALL + 8], sm[:, SMALL:SMALL + 4], 1.0 / LORA, EPS, ALU.mult,
                                        ALU.add).then_inc(l0["lat_v"], 1)

            def latents2():
                dve.wait_ge(l0["lat_r"], 1)
                for j in range(2):
                    for b in range(TB):
                        v = cq[:, b, j * LORA:(j + 1) * LORA]
                        i = SMALL + 12 + 2 * j + b
                        nc.vector.tensor_scalar(v, v, sm[:, i:i + 1], None, ALU.mult).then_inc(l0["lat_ok"], 1)

            def latents3():
                for j in range(2):
                    for b in range(TB):
                        d = (slice(4 * j, 4 * j + 4), slice(b * P, (b + 1) * P))
                        turn_dve(dve, turn, TBf[0][:, d[0], d[1]], TBf[1][:, d[0], d[1]], colA[:, 4 * j:4 * j + 4])

            def l0_side(s, p, at):
                name = f"l0_{s}"

                def rope(pr):
                    c2 = 2 * s + pr
                    landed(dve, name, l0_tile(s, pr, 0))
                    if c2 > 0:
                        dve.wait_ge(l0["tr"], c2)
                    q4 = qw[pr].rearrange("p b (h d) -> p b h d", d=QH)
                    rotate(qr, q4[..., NOPE:NOPE + 32], q4[..., NOPE + 32:QH], (l0["rope"], 1), 2)

                def silu():
                    dve.wait_ge(l0["z_e"], s + 1)
                    nc.vector.tensor_tensor(zw[s], zw[s], ez, ALU.mult).then_inc(l0["z_ok"], 1)

                def pair(pr):
                    c2 = 2 * s + pr
                    dve.wait_ge(l0["tr"], c2 + 1)
                    if c2 > 0:
                        dve.wait_ge(l0["sc"], 2 * c2)
                    nc.vector.tensor_copy(kT0.rearrange("p a t -> p (a t)"), ps[:, 1, :]).then_inc(l0["trV"], 1)

                def out_(hh):
                    r = mla.inverse(dve, own, s, hh)
                    dve.wait_ge(l0["z_ok"], s + 1)
                    for b in range(TB):
                        h = slice(hh * VH, hh * VH + VH)
                        nc.vector.scalar_tensor_tensor(og0[:, b, h], ps[:, 3, b * P:(b + 1) * P], r[:, b:b + 1],
                                                       zw[s][:, b, h], ALU.mult, ALU.mult).then_inc(l0["o"], 1)

                def back():
                    for b in range(TB):
                        turn_dve(dve, turn, og0_dst(s, 0, b), og0_dst(s, 1, b))

                if p == at[0]:
                    rope(0)
                    silu()
                if p == at[1]:
                    pair(0)
                if p == at[2]:
                    mla.mask_max(dve, own, s, 0)
                    mla.mask_max(dve, own, s, 1)
                    rope(1)
                if p == at[4]:
                    out_(0)
                if p == at[5]:
                    out_(1)
                    pair(1)
                if p == at[6]:
                    mla.mask_max(dve, own, s, 2)
                    mla.mask_max(dve, own, s, 3)
                if p == at[8]:
                    out_(2)
                if p == at[9]:
                    out_(3)
                if p == at[10]:
                    back()

            for p in range(length("l0_0")):
                step(dve, low, evac, "l0_0", p, 0, ("l0_in", 0))
                if p == 4:
                    latents()
                if p == 6:
                    latents2()
                if p == 10:
                    latents3()
            for s in range(1, 5):
                name = L0_PHASES[s]
                for p in range(length(name)):
                    step(dve, low, evac, name, p, 0, (L0_PHASES[s - 1], 0))
                    if s >= 2:
                        l0_side(s - 2, p + length(L0_PHASES[s - 1]), l0_late(s - 2))
                    l0_side(s - 1, p, l0_late(s - 1))
            finish(evac, "l0_out")

            layer_norm(0)

            dve.wait_ge(tr_src, 2)
            first_step("l1_gates", TA)
            for p in range(SPLIT, length("l1_gates")):
                step(dve, low, evac, "l1_gates", p)

            def gates_a():
                landed(dve, "l1_gates", 0)
                nc.vector.tensor_scalar(gt, gt, gbias[:, 0:1], None, ALU.add).then_inc(l1["g_in"], 1)

            def gates_b():
                dve.wait_ge(l1["g_pe"], 1)
                f = ps[0:8, 2, T:2 * T]
                own.then(nc.vector.tensor_copy(grow[:, 1, :], f))
                own.then(nc.vector.tensor_scalar(grow[:, 5, :], grow[:, 1, :], -1.0, None, ALU.mult))
                nc.vector.tensor_tensor(grow[:, 5, :], grow[:, 5, :], grow[:, 1, :], ALU.min).then_inc(l1["g_row"], 1)
                nc.vector.tensor_copy(grow[:, 0, :], ps[0:8, 2, 0:T]).then_inc(l1["g_row"], 1)
                own.then(nc.vector.tensor_scalar(grow[:, 1, :], grow[:, 1, :], 0.0, None, ALU.min))
                dve.wait_ge(l1["g_e"], 1)
                dve.wait_ge(l1["g_row"], 2)
                own.then(nc.vector.tensor_tensor(grow[:, 1, :], grow[:, 1, :], grow[:, 5, :], ALU.subtract))
                own.then(nc.vector.tensor_tensor_scan(grow[:, 2, :], ones[0:8, 0:T], grow[:, 1, :], 0.0, ALU.mult,
                                                      ALU.add))
                own.then(nc.vector.tensor_tensor(grow[:, 3, :], grow[:, 0, :], grow[:, 2, :], ALU.subtract))
                own.then(nc.vector.tensor_tensor_scan(grow[:, 4, :], grow[:, 3, :], grow[:, 3, :], 0.0, ALU.max,
                                                      ALU.max))
                nc.vector.tensor_scalar(negM, grow[:, 4, :], -1.0, None, ALU.mult).then_inc(l1["g_m"], 1)
                nc.vector.tensor_tensor(grow[:, 5, :], grow[:, 2, :], grow[:, 4, :], ALU.add).then_inc(l1["g_m"], 1)

            def gates_c():
                dve.wait_ge(l1["g_pe2"], 1)
                nc.vector.tensor_copy(acol, ps[:, 3, 0:16].rearrange("p (b h) -> p b h", b=TB)).then_inc(l1["g_col"], 1)

            def conv(s, j, heads):
                n = 2 * s + j
                dve.wait_ge(l1["q_c"], n + 1)
                if s > 0:
                    dve.wait_ge(l1["sc"], 4 * s)
                y = (qT1, kT1)[j]
                ch = lambda h: 8 * j + 4 * s + h
                cw = lambda w, h: colA[:, 8 + 16 * w + ch(h):9 + 16 * w + ch(h)]
                for h in heads:
                    own.mark(nc.vector.tensor_scalar(y[:, h, :], cin[:, h, PAD - 3:PAD - 3 + T], cw(0, h),
                                                     colA[:, 72 + ch(h):73 + ch(h)], ALU.mult, ALU.add))
                for w in (1, 2):
                    own.sync()
                    for h in heads:
                        own.mark(nc.vector.scalar_tensor_tensor(y[:, h, :], cin[:, h, PAD - 3 + w:PAD - 3 + w + T],
                                                                cw(w, h), y[:, h, :], ALU.mult, ALU.add))
                own.sync()
                for h in heads:
                    nc.vector.scalar_tensor_tensor(y[:, h, :], cin[:, h, PAD:PAD + T], cw(3, h), y[:, h, :],
                                                   ALU.mult, ALU.add).then_inc(l1["y_ok"], 1)

            def conv_gate(s, j):
                n = 2 * s + j
                y = (qT1, kT1)[j]
                dve.wait_ge(l1["y_e"], n + 1)
                own.sync()
                yf = y.rearrange("p h t -> p (h t)")
                nc.vector.scalar_tensor_tensor(yf, yf, 1.0 if j == 0 else MQK ** -0.5, esc, ALU.mult,
                                               ALU.mult).then_inc(l1["q_r"], 1)

            def weigh(s, c):
                dve.wait_ge(l1["sc"], c + 1)
                dve.wait_ge(l1["g_col"], 2)
                if c >= 2:
                    dve.wait_ge(l1["st"], c - 1)
                g = arg[:, c % 2, :]
                for b in range(TB):
                    n = slice(0, T) if b == 0 else slice(T, 384)
                    nc.vector.tensor_scalar(g[:, n], ps[:, 0, b * P:T], acol[:, b, c:c + 1], 0.0, ALU.add,
                                            ALU.min).then_inc(l1["arg"], 1)
                dve.wait_ge(l1["sel"], 2 * c + 2)
                if c > 0:
                    dve.wait_ge(l1["nm"], c)
                nc.vector.tensor_tensor(wst, ps[:, 1, 0:384], g, ALU.mult).then_inc(l1["st"], 1)

            def cell(s, c):
                dve.wait_ge(l1["nm"], c + 1)
                d = sm[:, 16 + 2 * (c % 2):18 + 2 * (c % 2)]
                for b in range(TB):
                    own.mark(nc.vector.tensor_scalar(d[:, b:b + 1], ps[:, 2 + b, MV:MV + 1], -1.0, emcol[:, b, c:c + 1],
                                                     ALU.mult, ALU.max))
                own.sync()
                own.then(nc.vector.tensor_tensor(d, d, ps[:, 2:4, MV], ALU.max))
                nc.vector.reciprocal(d, d).then_inc(l1["den"], 1)
                dve.wait_ge(l1["ssq"], 2 * c + 2)
                if c > 0:
                    dve.wait_ge(l1["rs"], c)
                nc.vector.tensor_scalar(sm[:, 24:26], sm[:, 20:22], 1.0 / MV, EPS, ALU.mult,
                                        ALU.add).then_inc(l1["var"], 1)

            def gate(s, j, b):
                n = 2 * (2 * s + j) + b
                dve.wait_ge(l1["ge"], n + 1)
                eo, e2 = esc[:, 0:COLS], esc[:, COLS:]
                o = ow[:, b, j * COLS:(j + 1) * COLS]
                own.then(nc.vector.tensor_tensor(e2, e2, eo, ALU.mult))
                nc.vector.tensor_tensor(o, zw1[:, b, :], e2, ALU.mult).then_inc(l1["z_ok"], 1)
                dve.wait_ge(l1["z_ok"], n + 1)
                dve.wait_ge(l1["rs"], 4 * s + 2 * j + 2)
                for h in (2 * j, 2 * j + 1):
                    oh = ow[:, b, h * MV:(h + 1) * MV]
                    nc.vector.scalar_tensor_tensor(oh, hq[:, b, h, :], sm[:, 28 + 2 * h + b:29 + 2 * h + b], oh,
                                                   ALU.mult, ALU.mult).then_inc(l1["og"], 1)

            def gated_turn(s, j):
                for b in range(TB):
                    k = 8 * s + 4 * j
                    d = (slice(k, k + 4), slice(b * P, (b + 1) * P))
                    turn_dve(dve, turn, TBf[0][:, d[0], d[1]], TBf[1][:, d[0], d[1]], colA[:, 88 + k:92 + k])

            def l1_side(s, p):
                if s == 0 and p == 4:
                    gates_a()
                if s == 0 and p == late("l1_0", 5):
                    gates_b()
                if s == 0 and p == late("l1_0", 8):
                    gates_c()
                if s == 1:
                    l1_rest(0, p)
                for j in range(2):
                    if p == late("l1_0", L1_AT["qk"[j]]):
                        conv(s, j, (0, 1))
                    if p == late("l1_0", L1_AT["qk"[j]]) + 1:
                        conv(s, j, (2, 3))
                    if p == late("l1_0", L1_AT["qk"[j]]) + 4:
                        conv_gate(s, j)
                for h in range(4):
                    if p == late("l1_0", L1_AT["ws"][h]):
                        weigh(s, 4 * s + h)
                    if p == late("l1_0", L1_AT["nm"][h]):
                        cell(s, 4 * s + h)
                for b in range(TB):
                    if p == late("l1_0", L1_AT["g0"] + 2 * b):
                        gate(s, 0, b)
                if p == late("l1_0", L1_AT["t0"]):
                    gated_turn(s, 0)

            def l1_rest(s, p):
                for b in range(TB):
                    if p == 3 + 2 * b:
                        gate(s, 1, b)
                if p == 6 + LAG:
                    gated_turn(s, 1)

            for s in range(2):
                for p in range(length("l1_0")):
                    step(dve, low, evac, f"l1_{s}", p, 0, (("l1_gates", "l1_0")[s], 0))
                    l1_side(s, p)
            for p in range(length("l1_out")):
                step(dve, low, evac, "l1_out", p, 0, ("l1_1", 0))
                l1_rest(1, p)
            finish(evac, "l1_out")
            layer_norm(1)
            for b in range(TB):
                dve.wait_ge(nrm_a, 3 + b)
                nc.vector.tensor_scalar(hn[:, b, :], x_res[:, b, :], nrm[:, b, 2:3], None, ALU.mult).then_inc(tr_src, 1)

            first_step("l2", TA, colB[:, 0:16])

            def l2_side(g, u):
                flat = lambda v: v.rearrange("p h t -> p (h t)")

                def turned():
                    f = ps2(2)
                    dve.wait_ge(l2["tf"], 1 + g)
                    own.then(nc.vector.tensor_scalar(dT[:, 0, :], f, -1.0, None, ALU.mult))
                    nc.vector.tensor_tensor(dT[:, 0, :], dT[:, 0, :], f, ALU.min).then_inc(l2["nf"], 1)
                    own.mark(nc.vector.tensor_scalar(dT[:, 1, :], f, 0.0, None, ALU.min))

                def decay():
                    f = ps2(2)
                    own.sync()
                    dve.wait_ge(l2["lf"], 2 + 2 * g)
                    own.then(nc.vector.tensor_tensor(flat(kT2), dT[:, 1, :], dT[:, 0, :], ALU.subtract))
                    own.mark(nc.vector.tensor_tensor(dT[:, 0, :], flat(kT2), f, ALU.subtract))
                    for h in range(4):
                        nc.vector.tensor_tensor_scan(bT2[:, h, :], ones[:], kT2[:, h, :], 0.0, ALU.mult,
                                                     ALU.add).then_inc(l2["kx"], 1)
                    own.sync()
                    dve.wait_ge(l2["kx"], 4 + 4 * g)

                def gate():
                    dve.wait_ge(l2["ge"], 3 + 3 * g)
                    e, gw = qx.rearrange("p a n -> p (a n)"), gw2.rearrange("p b n -> p (b n)")
                    nc.vector.tensor_tensor(gw, gw, e, ALU.mult).then_inc(l2["gs"], 1)

                def distance(j):
                    if j > 7:
                        return
                    h = P >> j
                    if j < 2:
                        dve.wait_ge(l2["kt"], 1 + g)
                    else:
                        dve.wait_ge(l2["lv"], j - 1 + 8 * g)
                    b = flat(bT2).rearrange("p (n r) -> p n r", r=2 * h)
                    nc.vector.tensor_tensor(dT[:, j % 2, :].rearrange("p (n r) -> p n r", r=2 * h), b,
                                            b[:, :, h - 1:h].to_broadcast([P, G4 // (2 * h), 2 * h]),
                                            ALU.subtract).then_inc(l2["df"], 1)

                def scale(j):
                    if j > 7:
                        return
                    h = P >> j
                    dve.wait_ge(l2["ee"], 2 * j + 2 + 16 * g)
                    if j == 0:
                        dve.wait_ge(l2["qT"], 1 + g)
                    half = lambda v, c: v.rearrange("p (n c r) -> p n c r", c=2, r=h)[:, :, c, :]
                    nc.vector.tensor_tensor(half(dT[:, j % 2, :], 0), half(dT[:, j % 2, :], 0), half(flat(kT2), 0),
                                            ALU.mult).then_inc(l2["op"], 1)
                    nc.vector.tensor_tensor(qx[:, j % 2, :].rearrange("p (n r) -> p n r", r=h),
                                            half(dT[:, j % 2, :], 1),
                                            half(flat(qT2), 1), ALU.mult).then_inc(l2["op"], 1)

                def diag():
                    distance(0)
                    distance(1)
                    dve.wait_ge(l2["dg"], 1 + g)
                    nc.vector.tensor_tensor(aT, ps2(0).rearrange("p (n t) -> p n t", t=P),
                                            ident[:].unsqueeze(1).to_broadcast([P, 8,
                                                                                P]), ALU.mult).then_inc(l2["at"], 1)
                    scale(0)

                def level(j):
                    h = P >> j
                    scale(j + 1)
                    dve.wait_ge(l2["lv"], j + 1 + 8 * g)
                    if j == 0:
                        nc.vector.tensor_copy(a01.rearrange("p h t -> p (h t)"), ps[:, 2, :]).then_inc(l2["sel"], 1)
                    else:
                        dve.wait_ge(l2["at"], 1 + g)
                        dve.wait_ge(l2["sel"], j + 8 * g)
                        nc.vector.memset(sm[:, 57:58], 0.0)
                        o = aT.rearrange("p n (m c r) -> p n m c r", c=2, r=h)[:, :, :, 1, :]
                        m = lvl[:, j - 1, :].rearrange("p (m r) -> p m r",
                                                       r=h).unsqueeze(1).to_broadcast([P, 8, 64 // h, h])
                        nc.vector.copy_predicated(o, m,
                                                  ps[:, 2 + j % 2, :].rearrange("p (n m r) -> p n m r", n=8,
                                                                                r=h)).then_inc(l2["sel"], 1)
                    distance(j + 2)

                def norm():
                    dve.wait_ge(l2["sq"], 2 + 2 * g)
                    nc.vector.tensor_reduce(sm[:, 32:40], dT[:, 0, :].rearrange("p (n d) -> p n d", d=HD), AX,
                                            ALU.add).then_inc(l2["ss"], 1)
                    dve.wait_ge(l2["ss"], 1 + g)
                    nc.vector.tensor_scalar(sm[:, 32:40], sm[:, 32:40], 1.0 / HD, EPS, ALU.mult,
                                            ALU.add).then_inc(l2["v"], 1)
                    dve.wait_ge(l2["rs"], 2 + 2 * g)
                    for b in range(TB):
                        nc.vector.tensor_tensor(dT[:, 1, b * COLS:(b + 1) * COLS].rearrange("p (h d) -> p h d", d=HD),
                                                ps[:, b, :].rearrange("p (h d) -> p h d", d=HD),
                                                sm[:, 48 + 4 * b:52 + 4 * b].unsqueeze(2).to_broadcast([P, 4, HD]),
                                                ALU.mult).then_inc(l2["on"], 1)
                    dve.wait_ge(l2["on"], 2 + 2 * g)
                    dve.wait_ge(l2["gs"], 1 + g)
                    gw = gw2.rearrange("p b n -> p (b n)")
                    nc.vector.tensor_tensor(gw, gw, dT[:, 1, :], ALU.mult).then_inc(l2["og"], 1)

                def back():
                    for b in range(TB):
                        t = tmpT[:, b, :].rearrange("p (k t) -> p k t", t=P)
                        dve.wait_ge(l2["ogp"], b + 1 + TB * g)
                        nc.vector.tensor_tensor(t, ps[:, 2 + b, :].rearrange("p (k t) -> p k t", t=P),
                                                colB[:,
                                                     group(16,
                                                           g)].unsqueeze(2).to_broadcast([P, 4,
                                                                                          P]), ALU.mult).then_inc(l2["tmp"], 1)
                    for b in range(TB):
                        t = tmpT[:, b, :].rearrange("p (k t) -> p k t", t=P)
                        dve.wait_ge(l2["hi"], b + 1 + TB * g)
                        nc.vector.tensor_tensor(heads_of(TBf[1], g, b), t, heads_of(TBf[0], g, b).bitcast(F32),
                                                ALU.subtract).then_inc(l2["lo"], 1)

                if u == L2_AT["turn"] + LAG:
                    turned()
                if u == L2_AT["decay"] + LAG:
                    decay()
                if u == L2_AT["diag"] + LAG:
                    diag()
                for j in range(8):
                    if u == L2_AT["level"][j] + LAG:
                        level(j)
                if u == L2_AT["gate"] + LAG:
                    gate()
                if u == L2_AT["norm"] + LAG:
                    norm()
                if u == L2_AT["back"] + LAG:
                    back()

            for p in range(SPLIT, length("l2")):
                step(dve, low, evac, "l2", p)
                l2_side(0, p)
            with dve.Fori(1, 4) as it:
                own.enter(it, L2_OWN)
                for p in range(length("l2")):
                    step(dve, low, evac, "l2", p, it, ("l2", it - 1))
                    l2_side(it - 1, p + length("l2"))
                    l2_side(it, p)
            own.leave(3)
            for p in range(length("l2_out")):
                step(dve, low, evac, "l2_out", p, 0, ("l2", 3))
                l2_side(3, p + length("l2"))
            finish(evac, "l2_out")
            statistics(2)
            own.then(nc.vector.tensor_tensor(nrm[:, :, 3], mv[:, :, 0], mv[:, :, 0], ALU.mult))
            nc.vector.scalar_tensor_tensor(nrm[:, :, 0], mv[:, :, 1], EPS, nrm[:, :, 3], ALU.add,
                                           ALU.add).then_inc(nrm_v, 1)
            for b in range(TB):
                dve.wait_ge(nrm_a, 5)
                nc.vector.tensor_scalar(hn[:, b, :], x_res[:, b, :], nrm[:, b, 2:3], None, ALU.mult).then_inc(tr_src, 1)

            first_step("l3_f", TA, colB[:, 32:48])
            own.mark(nc.vector.tensor_scalar(sm[:, 56:57], colB[:, 81:82], HD ** -0.5, None, ALU.mult))

            dve.wait_ge(l1["pads"], 2)

            def forget():
                landed(dve, "l3_f", 0)
                own.then(nc.vector.tensor_scalar(frow[:, 0, :], ft, gbias[:, 1:2], None, ALU.add))
                own.then(nc.vector.tensor_scalar(frow[:, 1, :], frow[:, 0, :], -1.0, None, ALU.mult))
                nc.vector.tensor_tensor(frow[:, 1, :], frow[:, 1, :], frow[:, 0, :], ALU.min).then_inc(l3["f_row"], 1)
                own.then(nc.vector.tensor_scalar(frow[:, 2, :], frow[:, 0, :], 0.0, None, ALU.min))
                dve.wait_ge(l3["f_e"], 2)
                nc.vector.tensor_tensor(frow[:, 1, :], frow[:, 1, :], frow[:, 2, :],
                                        ALU.subtract).then_inc(l3["f_ok"], 1)
                dve.wait_ge(l3["f_ok"], 1)
                own.then(nc.vector.tensor_tensor_scan(frow[:, 3, :], ones[0:16, 0:T], frow[:, 1, :], 0.0, ALU.mult,
                                                      ALU.add))
                nc.vector.tensor_copy(negF, frow[:, 3, :]).then_inc(l3["f_ok"], 1)

            def head_norm(dst, src, sq, vs, rs, on, g):
                dve.wait_ge(sq, 8 * g + 8)
                nc.vector.tensor_scalar(sm[:, 32:40], sm[:, 32:40], 1.0 / HD, EPS, ALU.mult, ALU.add).then_inc(vs, 1)
                dve.wait_ge(rs, 2 * g + 2)
                for b in range(TB):
                    nc.vector.tensor_tensor(dst[:, b, :].rearrange("p (h d) -> p h d", d=HD),
                                            src[:, b, :].rearrange("p (h d) -> p h d", d=HD),
                                            sm[:,
                                               48 + 4 * b:52 + 4 * b].unsqueeze(2).to_broadcast([P, 4, HD]), ALU.mult).then_inc(on, 1)

            def kv_side(g, p):
                if p == late("l3_kv", 0):
                    head_norm(qw3, qw3, l3["ksq"], l3["kv_"], l3["krs"], l3["kn"], g)

            for p in range(SPLIT, length("l3_f")):
                step(dve, low, evac, "l3_f", p)
            for p in range(length("l3_kv")):
                step(dve, low, evac, "l3_kv", p, 0, ("l3_f", 0))
                if p == 12:
                    forget()
                for n in query_banks(p - LAG):
                    b, q = n // 4, n % 4
                    d = (slice(4 * q, 4 * q + 4), slice(b * P, (b + 1) * P))
                    turn_dve(dve, turn, TBf[0][:, d[0], d[1]], TBf[1][:, d[0], d[1]], colB[:, 48 + 4 * q:52 + 4 * q])
            with dve.Fori(1, 4) as it:
                for p in range(length("l3_kv")):
                    step(dve, low, evac, "l3_kv", p, it, ("l3_kv", it - 1))
                    kv_side(it - 1, p)

            def q_side(g, u):

                def norm():
                    head_norm(qw3, qw3, l3["qsq"], l3["qv"], l3["qrs"], l3["qn"], g)

                def out_(hh):
                    r = fox.inverse(dve, own, g, hh)
                    for b in range(TB):
                        nc.vector.tensor_scalar(o3[:, b, hh * HD:hh * HD + HD], ps[:, 3, b * P:(b + 1) * P],
                                                r[:, b:b + 1],
                                                None, ALU.mult).then_inc(l3["o"], 1)

                def gate(b):
                    dve.wait_ge(l3["ge"], 3 * (2 * g + b) + 3)
                    nc.vector.tensor_tensor(gw3[:, b, :], gw3[:, b, :], tmpT[:, 0, :], ALU.mult).then_inc(l3["gs"], 1)

                def post():
                    head_norm(o3, o3, l3["sq"], l3["v"], l3["rs"], l3["on"], g)
                    dve.wait_ge(l3["on"], 2 * g + 2)
                    dve.wait_ge(l3["gs"], 2 * g + 2)
                    flat = lambda v: v.rearrange("p b n -> p (b n)")
                    nc.vector.tensor_tensor(flat(o3), flat(gw3), flat(o3), ALU.mult).then_inc(l3["og"], 1)

                def back():
                    for b in range(TB):
                        t = tmpT[:, b, :].rearrange("p (k t) -> p k t", t=P)
                        dve.wait_ge(l3["ogp"], 2 * g + b + 1)
                        nc.vector.tensor_tensor(t, ps[:, b, :].rearrange("p (k t) -> p k t", t=P),
                                                colB[:,
                                                     group(64,
                                                           g)].unsqueeze(2).to_broadcast([P, 4,
                                                                                          P]), ALU.mult).then_inc(l3["tmp"], 1)
                    for b in range(TB):
                        t = tmpT[:, b, :].rearrange("p (k t) -> p k t", t=P)
                        dve.wait_ge(l3["hi"], 2 * g + b + 1)
                        nc.vector.tensor_tensor(heads_of(TA[1], g, b), t, heads_of(TA[0], g, b).bitcast(F32),
                                                ALU.subtract).then_inc(l3["lo"], 1)

                for b in range(TB):
                    if u == L3_AT["gate"][b] + LAG:
                        gate(b)
                if u == L3_AT["norm"] + LAG:
                    norm()
                if u == L3_AT["sc0"] + LAG:
                    fox.mask_max(dve, own, g, 0)
                    fox.mask_max(dve, own, g, 1)
                if u == L3_AT["v0"] + LAG:
                    out_(0)
                if u == L3_AT["v1"] + LAG:
                    out_(1)
                    fox.mask_max(dve, own, g, 2)
                    fox.mask_max(dve, own, g, 3)
                if u == L3_AT["v2"] + LAG:
                    out_(2)
                if u == L3_AT["v3"] + LAG:
                    out_(3)
                if u == L3_AT["post"] + LAG:
                    post()
                if u == L3_AT["back"] + LAG:
                    back()

            for p in range(length("l3_q")):
                step(dve, low, evac, "l3_q", p, 0, ("l3_kv", 3))
                kv_side(3, p)
                q_side(0, p)
            with dve.Fori(1, 4) as it:
                own.enter(it, L3_OWN)
                for p in range(length("l3_q")):
                    step(dve, low, evac, "l3_q", p, it, ("l3_q", it - 1))
                    q_side(it - 1, p + length("l3_q"))
                    q_side(it, p)
            own.leave(3)
            for p in range(length("l3_out")):
                step(dve, low, evac, "l3_out", p, 0, ("l3_q", 3))
                q_side(3, p + length("l3_q"))
            finish(evac, "l3_out")

        @block.tensor
        def _(pe):
            turn = Turn()

            def turn_block(src, b, q):
                turn_pe(pe, turn, [src[:, b, (4 * q + j) * P:(4 * q + j + 1) * P] for j in range(4)])

            pe.wait_ge(ident_ok, 1)
            for b in range(TB):
                pe.wait_ge(x_in[b], 16)
                for q in range(4):
                    turn_block(x_res, b, q)

            def in_src(k, q):
                return TA[0], TA[1], q

            first_products(pe, "l0_in", in_src, turn.n)
            pe.wait_ge(tr_lo, turn.n)
            for p in range(SPLIT, length("l0_in")):
                products(pe, "l0_in", p, in_src)
                if p == 8:
                    pe.wait_ge(par_in, 16 * 12)
                    nc.tensor.transpose(ps[:, 0, 0:NA_ROWS], stage_rows[0:NA_ROWS, 0, :], ident[0:NA_ROWS, 0:NA_ROWS])
                    nc.tensor.transpose(ps[:, 0, P:P + NB_ROWS], stage_rows[0:NB_ROWS, 1, :],
                                        ident[0:NB_ROWS, 0:NB_ROWS]).then_inc(col_pe, 1)

            def key_part():
                landed(pe, "l0_in", 2)
                pe.wait_ge(col_ok, 2)
                for b in range(TB):
                    m = nc.tensor.transpose(ps[:, 0, b * ROPE:(b + 1) * ROPE], krf[:, b * P:(b + 1) * P],
                                            ident[0:ROPE, 0:ROPE])
                m.then_inc(l0["kr_in"], 1)

            def latents():
                pe.wait_ge(l0["kr_ok"], 3)
                for b in range(TB):
                    m = nc.tensor.transpose(ps[:, 0, b * P:(b + 1) * P],
                                            krd[:, b, :, :].rearrange("p a f -> p (a f)"), ident[:])
                m.then_inc(l0["kr_pe"], 1)

            def latents2():
                pe.wait_ge(l0["lat_ok"], 4)
                pe.wait_ge(l0["kr_T"], 1)
                for j in range(2):
                    for b in range(TB):
                        turn_pe(pe, turn, [cq[:, b, (4 * j + i) * P:(4 * j + i + 1) * P] for i in range(4)])

            def l0_side(s, p, at):
                name = f"l0_{s}"

                def pair(pr):
                    c2 = 2 * s + pr
                    pe.wait_ge(l0["rope"], 2 * c2 + 2)
                    landed(pe, name, l0_tile(s, pr, 0))
                    landed(pe, name, l0_tile(s, pr, 1))
                    if c2 > 0:
                        pe.wait_ge(l0["msk"], 2 * c2)
                    if c2 > 0:
                        pe.wait_ge(l0["ptc"], 2 * c2)
                    pe.wait_ge(tr_lo, turn.n)
                    pe.wait_ge(l0["kr_T"], 1)
                    for hh in range(2):
                        for b in range(TB):
                            o = slice(hh * T + b * P, hh * T + (b + 1) * P)
                            nc.tensor.transpose(ps[:, 0, o], qw[pr][:, b, hh * QH:hh * QH + NOPE], ident[:])
                            nc.tensor.transpose(ps[:, 1, o], kvw[pr][:, b, hh * 256:hh * 256 + NOPE], ident[:])
                    for b in range(TB):
                        m = nc.tensor.transpose(ps[:, 2, b * P:(b + 1) * P],
                                                qr[:, b, :, :].rearrange("p h f -> p (h f)"), ident[:])
                    m.then_inc(l0["tr"], 1)

                def scores(pr):
                    pe.wait_ge(l0["trA"], 2 * (2 * s + pr) + 2)
                    pe.wait_ge(l0["trV"], 2 * s + pr + 1)
                    mla.scores(pe, s, 2 * pr)
                    mla.scores(pe, s, 2 * pr + 1)

                def back():
                    pe.wait_ge(l0["o"], 2 * (4 * s + 4))
                    for b in range(TB):
                        turn_pe(pe, turn, [og0[:, b, i * P:(i + 1) * P] for i in range(4)])

                if p == at[1]:
                    pair(0)
                if p == at[2]:
                    scores(0)
                if p == at[3]:
                    mla.turn(pe, s, 0)
                if p == at[4]:
                    mla.values(pe, s, 0)
                    mla.turn(pe, s, 1)
                if p == at[5]:
                    mla.values(pe, s, 1)
                    pair(1)
                if p == at[6]:
                    scores(1)
                if p == at[7]:
                    mla.turn(pe, s, 2)
                if p == at[8]:
                    mla.values(pe, s, 2)
                    mla.turn(pe, s, 3)
                if p == at[9]:
                    mla.values(pe, s, 3)
                if p == at[10]:
                    back()

            for p in range(length("l0_0")):
                if p == 16:
                    pe.wait_ge(tr_lo, 12)
                products(pe, "l0_0", p, lambda k, q: latent_src(k, q, 0))
                if p == 1:
                    key_part()
                if p == 4:
                    latents()
                if p == 7:
                    latents2()
            for s in range(1, 4):
                for p in range(length(f"l0_{s}")):
                    products(pe, f"l0_{s}", p, lambda k, q: latent_src(k, q, s))
                    l0_side(s - 1, p, l0_at(f"l0_{s}"))
            for p in range(length("l0_out") - SPLIT):
                if p == 0:
                    pe.wait_ge(tr_lo, 18)
                if p == 12:
                    pe.wait_ge(tr_lo, 20)
                products(pe, "l0_out", p, out0_src)
                l0_side(3, p, l0_at("l0_out"))
            last_products(pe, "l0_out", out0_src)
            for b in range(TB):
                pe.wait_ge(tr_src, b + 1)
                for q in range(4):
                    turn_block(x_res, b, q)

            first_products(pe, "l1_gates", in_src, turn.n)
            pe.wait_ge(tr_lo, turn.n)
            for p in range(SPLIT, length("l1_gates")):
                products(pe, "l1_gates", p, in_src)

            def gates_a():
                pe.wait_ge(l1["g_in"], 1)
                pe.wait_ge(tr_lo, turn.n)
                nc.tensor.matmul(ps[0:8, 2, 0:T], ident[0:16, 0:8], gt, start=True, stop=True)
                nc.tensor.matmul(ps[0:8, 2, T:2 * T], ident[0:16, 8:16], gt, start=True,
                                 stop=True).then_inc(l1["g_pe"], 1)

            def gates_c():
                pe.wait_ge(l1["g_m"], 2)
                for b in range(TB):
                    nc.tensor.transpose(ps[:, 3, 8 * b:8 * b + 8], grow[:, 3, b * P:(b + 1) * P], ident[0:8, 0:8])
                    m = nc.tensor.transpose(ps[:, 3, 16 + 8 * b:24 + 8 * b], grow[:, 5, b * P:(b + 1) * P],
                                            ident[0:8, 0:8])
                m.then_inc(l1["g_pe2"], 1)

            def window(s, j):
                landed(pe, f"l1_{s}", j)
                pe.wait_ge(tr_lo, turn.n)
                if 2 * s + j > 0:
                    pe.wait_ge(l1["q_c"], 2 * s + j)
                if s > 0:
                    pe.wait_ge(l1["st"], 4 * s)
                for h in range(4):
                    for b in range(TB):
                        m = nc.tensor.transpose(ps2(0)[:, h * T + b * P:h * T + (b + 1) * P],
                                                qkw[j][:, b, h * P:(h + 1) * P], ident[:])
                m.then_inc(l1["q_pe"], 1)

            def weigh(s, c):
                h = c % 4
                pe.wait_ge(l1["q_r"], 2 * s + 2)
                pe.wait_ge(l1["q_c"], 2 * s + 2)
                if c > 0:
                    pe.wait_ge(l1["st"], c)
                pe.wait_ge(l1["g_m"], 2)
                nc.tensor.matmul(ps[:, 0, 0:T], ident[0:8, c:c + 1].to_broadcast([8, P]), negM, start=True, stop=True)
                nc.tensor.matmul(ps[:, 1, 0:T], kT1[:, h, 0:P], qT1[:, h, :], start=True, stop=True)
                nc.tensor.matmul(ps[:, 1, T:384], kT1[:, h, P:T], qT1[:, h, P:T], start=True,
                                 stop=True).then_inc(l1["sc"], 1)

            def number(s, c):
                h = c % 4
                landed(pe, f"l1_{s}", 2 + h // 2)
                pe.wait_ge(l1["pads"], 2)
                pe.wait_ge(l1["st"], c + 1)
                if c > 0:
                    pe.wait_ge(l1["h"], 2 * c)
                pe.wait_ge(l1["g_col"], 2)
                v = lambda b: vw[:, b, h, 0:MV + 1]
                nc.tensor.matmul(ps[:, 2, 0:MV + 1], wst[:, 0:P], v(0), start=True, stop=True)
                nc.tensor.matmul(ps[:, 3, 0:MV + 1], wst[:, P:T], v(0), start=True, stop=False)
                nc.tensor.matmul(ps[:, 3, 0:MV + 1], wst[:, T:384], v(1), start=False, stop=True).then_inc(l1["nm"], 1)

            def gated_turn(s, j):
                pe.wait_ge(l1["og"], 8 * s + 4 * j + 4)
                pe.wait_ge(l1["h"], 8 * s + 8)
                for b in range(TB):
                    turn_pe(pe, turn, [ow[:, b, j * COLS + i * P:j * COLS + (i + 1) * P] for i in range(4)])

            def l1_side(s, p):
                if s == 0 and p == 5:
                    gates_a()
                if s == 0 and p == 8:
                    gates_c()
                if s == 1:
                    l1_rest(0, p)
                for j in range(2):
                    if p == L1_AT["qk"[j]]:
                        window(s, j)
                for h in range(4):
                    if p == L1_AT["ws"][h]:
                        weigh(s, 4 * s + h)
                    if p == L1_AT["nm"][h]:
                        number(s, 4 * s + h)
                if p == L1_AT["t0"]:
                    gated_turn(s, 0)

            def l1_rest(s, p):
                if p == 6:
                    gated_turn(s, 1)

            for s in range(2):
                for p in range(length("l1_0")):
                    products(pe, f"l1_{s}", p, in_src)
                    l1_side(s, p)
            for p in range(length("l1_out") - SPLIT):
                if p == 0:
                    pe.wait_ge(tr_lo, L1_BASE + 6)
                if p == 12:
                    pe.wait_ge(tr_lo, L1_BASE + 8)
                products(pe, "l1_out", p, out1_src)
                l1_rest(1, p)

            last_products(pe, "l1_out", out1_src)
            for b in range(TB):
                pe.wait_ge(tr_src, 4 + b + 1)
                for q in range(4):
                    turn_block(hn, b, q)

            first_products(pe, "l2", in_src, turn.n)
            pe.wait_ge(tr_lo, turn.n)

            def l2_side(g, u):
                def turned():
                    landed(pe, "l2", 1, g)
                    for w, bank in ((qw2, 0), (fw2, 2)):
                        for h in range(4):
                            for b in range(TB):
                                m = nc.tensor.transpose(ps2(bank)[:, h * T + b * P:h * T + (b + 1) * P],
                                                        w[:, b, h * P:(h + 1) * P], ident[:])
                        m.then_inc(l2["tq" if bank == 0 else "tf"], 1)

                def diag():
                    pe.wait_ge(l2["qT"], 1 + g)
                    pe.wait_ge(l2["kt"], 1 + g)
                    for h in range(4):
                        for b in range(TB):
                            c = slice(b * P, (b + 1) * P)
                            m = nc.tensor.matmul(ps2(0)[:, (2 * h + b) * P:(2 * h + b + 1) * P], kT2[:, h, c],
                                                 qT2[:, h, c], start=True, stop=True)
                    m.then_inc(l2["dg"], 1)

                def level(j):
                    pe.wait_ge(l2["op"], 2 * j + 2 + 16 * g)
                    if j >= 2:
                        pe.wait_ge(l2["sel"], j - 1 + 8 * g)
                    k = dT[:, j % 2, :].rearrange("p (h t) -> p h t", t=T)
                    for h in range(4):
                        if j == 0:
                            m = nc.tensor.matmul(ps[:, 2, h * P:(h + 1) * P], k[:, h, 0:P],
                                                 qx[:, 0, h * P:(h + 1) * P], start=True, stop=True)
                            continue
                        for b in range(TB):
                            n = 2 * h + b
                            m = nc.tensor.matmul(ps[:, 2 + j % 2, n * 64:(n + 1) * 64], k[:, h, b * P:(b + 1) * P],
                                                 qx[:, j % 2, n * 64:(n + 1) * 64], start=True, stop=True)
                    m.then_inc(l2["lv"], 1)

                def values():
                    pe.wait_ge(l2["sel"], 8 + 8 * g)
                    landed(pe, "l2", 2, g)
                    for h in range(4):
                        v = lambda b: vw2[:, b, h * HD:(h + 1) * HD]
                        o = slice(h * HD, (h + 1) * HD)
                        nc.tensor.matmul(ps[:, 0, o], aT[:, 2 * h, :], v(0), start=True, stop=True)
                        nc.tensor.matmul(ps[:, 1, o], a01[:, h, :], v(0), start=True, stop=False)
                        m = nc.tensor.matmul(ps[:, 1, o], aT[:, 2 * h + 1, :], v(1), start=False, stop=True)
                    m.then_inc(l2["pv"], 1)

                def back():
                    pe.wait_ge(l2["og"], 1 + g)
                    for b in range(TB):
                        for i in range(4):
                            m = nc.tensor.transpose(ps[:, 2 + b, i * P:(i + 1) * P], gw2[:, b, i * P:(i + 1) * P],
                                                    ident[:])
                        m.then_inc(l2["ogp"], 1)

                if u == L2_AT["turn"]:
                    turned()
                if u == L2_AT["diag"]:
                    diag()
                for j in range(8):
                    if u == L2_AT["level"][j]:
                        level(j)
                if u == L2_AT["pv"]:
                    values()
                if u == L2_AT["back"]:
                    back()

            for p in range(SPLIT, length("l2")):
                products(pe, "l2", p, in_src)
                l2_side(0, p)
            with pe.Fori(1, 4) as it:
                for p in range(length("l2")):
                    products(pe, "l2", p, in_src, it)
                    l2_side(it - 1, p + length("l2"))
                    l2_side(it, p)
            for p in range(length("l2_out") - SPLIT):
                if p == 0:
                    pe.wait_ge(l2["lo"], 6)
                if p == 12:
                    pe.wait_ge(l2["lo"], 8)
                products(pe, "l2_out", p, out1_src)
                l2_side(3, p + length("l2"))

            last_products(pe, "l2_out", out1_src)
            pe.wait_ge(l2["lo"], 8)
            for b in range(TB):
                pe.wait_ge(tr_src, 6 + b + 1)
                for q in range(4):
                    turn_block(hn, b, q)

            first_products(pe, "l3_f", in_src, turn.n)
            pe.wait_ge(tr_lo, turn.n)
            for p in range(SPLIT, length("l3_f")):
                products(pe, "l3_f", p, in_src)

            def turn_window(done):
                for h in range(4):
                    for b in range(TB):
                        m = nc.tensor.transpose(ps2(0)[:, h * T + b * P:h * T + (b + 1) * P],
                                                qw3[:, b, h * HD:(h + 1) * HD], ident[:])
                m.then_inc(done, 1)

            def kv_side(g, p):
                if p == 5:
                    pe.wait_ge(l3["kn"], 2 * g + 2)
                    pe.wait_ge(tr_lo, turn.n)
                    turn_window(l3["kt"])

            for p in range(length("l3_kv")):
                products(pe, "l3_kv", p, in_src)
                for n in query_banks(p):
                    turn_block(hn, n // 4, n % 4)
            with pe.Fori(1, 4) as it:
                for p in range(length("l3_kv")):
                    products(pe, "l3_kv", p, in_src, it)
                    kv_side(it - 1, p)

            def q_src(k, q):
                return TBf[0], TBf[1], q

            def q_side(g, u):
                def queries():
                    pe.wait_ge(l3["qn"], 2 * g + 2)
                    pe.wait_ge(l3["kT"], 4)
                    if g > 0:
                        pe.wait_ge(l3["lo"], 2 * g)
                    turn_window(l3["qt"])

                def scores(hh):
                    pe.wait_ge(l3["qT"], g + 1)
                    pe.wait_ge(l3["f_ok"], 2)
                    fox.scores(pe, g, hh)
                    fox.scores(pe, g, hh + 1)

                def back():
                    pe.wait_ge(l3["og"], g + 1)
                    pe.wait_ge(l3["msk"], 4 * g + 4)
                    for b in range(TB):
                        for i in range(4):
                            m = nc.tensor.transpose(ps[:, b, i * P:(i + 1) * P], o3[:, b, i * P:(i + 1) * P], ident[:])
                        m.then_inc(l3["ogp"], 1)

                if u == L3_AT["turn"]:
                    queries()
                if u == L3_AT["sc0"]:
                    scores(0)
                if u == L3_AT["t0"]:
                    fox.turn(pe, g, 0)
                if u == L3_AT["v0"]:
                    fox.values(pe, g, 0)
                    fox.turn(pe, g, 1)
                if u == L3_AT["v1"]:
                    fox.values(pe, g, 1)
                    scores(2)
                if u == L3_AT["t2"]:
                    fox.turn(pe, g, 2)
                if u == L3_AT["v2"]:
                    fox.values(pe, g, 2)
                    fox.turn(pe, g, 3)
                if u == L3_AT["v3"]:
                    fox.values(pe, g, 3)
                if u == L3_AT["back"]:
                    back()

            pe.wait_ge(tr_lo, turn.n)
            for p in range(length("l3_q")):
                products(pe, "l3_q", p, q_src)
                kv_side(3, p)
                q_side(0, p)
            for it in range(1, 4):
                for p in range(length("l3_q")):
                    products(pe, "l3_q", p, q_src, it)
                    q_side(it - 1, p + length("l3_q"))
                    q_side(it, p)
            for p in range(length("l3_out") - SPLIT):
                if p == 0:
                    pe.wait_ge(l3["lo"], 6)
                if p == 12:
                    pe.wait_ge(l3["lo"], 8)
                products(pe, "l3_out", p, in_src)
                q_side(3, p + length("l3_q"))
            last_products(pe, "l3_out", in_src)


_INS = ["x", "positions", "mla_w_in", "mla_q_norm", "mla_w_qb", "mla_kv_norm", "mla_w_kvb", "mla_w_out", "ml_w_in",
        "ml_conv_w", "ml_conv_b", "ml_gate_b", "ml_head_norm", "ml_w_out", "ln_w", "ln_b", "a_norm_w_2", "a_w_in_2",
        "a_lb_logits_2", "a_out_norm_w_2", "a_w_out_2", "kv_norm_w_2", "kv_w_2", "kv_f_bias_2", "k_norm_w_2",
        "b_norm_w_2", "b_w_in_2", "b_q_norm_w_2", "b_out_norm_w_2", "b_w_out_2"]


def kernel(**inputs):
    import numpy as _np
    import concourse.bacc as _bacc
    from concourse.bass_utils import run_bass_kernel_spmd as _run

    nc = _bacc.Bacc("TRN2", target_bir_lowering=False, num_devices=1)
    arrays, args = {}, {}
    for name in _INS:
        v = _np.ascontiguousarray(inputs[name])
        arrays[f"in_{name}"] = v
        args[name] = nc.dram_tensor(f"in_{name}", v.shape, mybir.dt.from_np(v.dtype), kind="ExternalInput").ap()
    out = nc.dram_tensor("out_x", (1, T, D), F32, kind="ExternalOutput").ap()
    build(nc, args, out)
    r = _run(nc, [arrays], core_ids=[0])
    return r.results[0]["out_x"]
```
